# Optimizing a Trainium2 kernel written in Bass

```python
import jax, jax.numpy as jnp
from jax import lax
import numpy as np
import jax
import jax.numpy as jnp

D_MODEL = 1024
BATCH = 1
SEQ = 512
DEPTH = 2

RW_HEADS = 8
RW_HEAD_DIM = 64
RW_WIDTH = RW_HEADS * RW_HEAD_DIM
RW_DECAY_RANK = 64
RW_ICLR_RANK = 64
RW_GATE_RANK = 128
RW_COLS = 3 * RW_WIDTH + RW_DECAY_RANK + RW_ICLR_RANK + RW_GATE_RANK
RW_GN_EPS = 64e-5
RET_HEADS = 4
RET_QK_DIM = 64
RET_V_DIM = 128
RET_QK_WIDTH = RET_HEADS * RET_QK_DIM
RET_V_WIDTH = RET_HEADS * RET_V_DIM
RET_COLS = 2 * RET_QK_WIDTH + 2 * RET_V_WIDTH
RET_CHUNK = 128
ROPE_BASE = 10000.0
SG_GROUPS = 4
SG_CHUNK = 128
SG_WIDTH = 512
SG_GROUP_DIM = SG_WIDTH // SG_GROUPS
SG_COLS = 2 * SG_WIDTH
N_BRANCH = 3
BRANCH_WIDTH = 512
GATE_COLS = N_BRANCH * D_MODEL
IN_COLS = RW_COLS + RET_COLS + SG_COLS + GATE_COLS
D_FF = 2816
CONV_WIDTH = 3
EPS = 1e-6


def rmsnorm(x, g):
    xf = x.astype(jnp.float32)
    y = xf * lax.rsqrt(jnp.mean(xf * xf, axis=-1, keepdims=True) + EPS) * g.astype(jnp.float32)
    return y.astype(x.dtype)

def rwkv7_scan(r, w, k, v, kk, a):
    B, S, H, N = r.shape

    def step(state, inp):
        r_t, w_t, k_t, v_t, kk_t, a_t = inp
        sa = jnp.einsum('bhvk,bhk->bhv', state, -kk_t)
        state = (state * w_t[:, :, None, :]
                 + sa[..., None] * (kk_t * a_t)[:, :, None, :]
                 + v_t[..., None] * k_t[:, :, None, :])
        y = jnp.einsum('bhvk,bhk->bhv', state, r_t)
        return state, y

    xs = tuple(jnp.moveaxis(t.astype(jnp.float32), 1, 0) for t in (r, w, k, v, kk, a))
    s0 = jnp.zeros((B, H, N, N), jnp.float32)
    _, ys = lax.scan(step, s0, xs)
    return jnp.moveaxis(ys, 0, 1)

def rwkv7_branch(p, mu, w0, w_up, a0, a_up, g_up, k_k, k_a, r_k, lnx_g, lnx_b):
    B, S, _ = p.shape
    p_prev = jnp.pad(p, ((0, 0), (1, 0), (0, 0)))[:, :S]
    p = p + mu * (p_prev - p)
    cuts = [RW_WIDTH, 2 * RW_WIDTH, 3 * RW_WIDTH, 3 * RW_WIDTH + RW_DECAY_RANK,
            3 * RW_WIDTH + RW_DECAY_RANK + RW_ICLR_RANK]
    r, k, v, wd, ad, gd = jnp.split(p, cuts, axis=-1)
    w = -jax.nn.softplus(-(w0 + jnp.tanh(wd) @ w_up)) - 0.5
    decay = jnp.exp(-jnp.exp(w.astype(jnp.float32)))
    a = jax.nn.sigmoid(a0 + ad @ a_up)
    g = jax.nn.sigmoid(gd) @ g_up
    kk = (k * k_k).astype(jnp.float32)
    k = k * (1.0 + (a - 1.0) * k_a)

    def heads(t):
        return t.reshape(B, S, RW_HEADS, RW_HEAD_DIM)

    r, k, v, decay, a, kk = map(heads, (r, k, v, decay, a, kk))
    kk = kk / jnp.maximum(jnp.sqrt(jnp.sum(kk * kk, axis=-1, keepdims=True)), 1e-12)
    y = rwkv7_scan(r, decay, k, v, kk, a)
    mean = jnp.mean(y, axis=-1, keepdims=True)
    var = jnp.mean(jnp.square(y - mean), axis=-1, keepdims=True)
    y = (y - mean) * lax.rsqrt(var + RW_GN_EPS) * lnx_g + lnx_b
    y = y + jnp.sum(r * k * r_k, axis=-1, keepdims=True) * v
    return (y.reshape(B, S, RW_WIDTH) * g).astype(p.dtype)

def rotary(t, cos, sin):
    t1, t2 = jnp.split(t, 2, axis=-1)
    c = cos[None, :, None, :]
    s = sin[None, :, None, :]
    return jnp.concatenate([t1 * c - t2 * s, t2 * c + t1 * s], axis=-1)

def retention_branch(p, cos, sin):
    B, S, _ = p.shape
    nC = S // RET_CHUNK
    q, k, v, g = jnp.split(p, [RET_QK_WIDTH, 2 * RET_QK_WIDTH, 2 * RET_QK_WIDTH + RET_V_WIDTH], axis=-1)
    q = rotary(q.reshape(B, S, RET_HEADS, RET_QK_DIM), cos, sin)
    k = rotary(k.reshape(B, S, RET_HEADS, RET_QK_DIM), cos, sin) * (RET_QK_DIM ** -0.5)
    v = v.reshape(B, S, RET_HEADS, RET_V_DIM)

    def chunks(t):
        return t.reshape(B, nC, RET_CHUNK, RET_HEADS, t.shape[-1]).transpose(0, 3, 1, 2, 4)

    qc, kc, vc = chunks(q), chunks(k), chunks(v)
    log_gamma = jnp.log(1.0 - 2.0 ** (-5.0 - jnp.arange(RET_HEADS, dtype=jnp.float32)))
    pos = jnp.arange(RET_CHUNK, dtype=jnp.float32)
    diff = pos[:, None] - pos[None, :]
    decay_in = jnp.where(diff[None] >= 0,
                         jnp.exp(jnp.maximum(diff, 0.0)[None] * log_gamma[:, None, None]), 0.0)
    scores = jnp.einsum('bhnid,bhnjd->bhnij', qc, kc) * decay_in[:, None]
    inner = jnp.einsum('bhnij,bhnje->bhnie', scores, vc)
    k_dec = jnp.exp((RET_CHUNK - 1.0 - pos)[None] * log_gamma[:, None])
    kv = jnp.einsum('bhnjd,bhnje,hj->nbhde', kc, vc, k_dec).astype(jnp.float32)
    chunk_decay = jnp.exp(RET_CHUNK * log_gamma)[None, :, None, None]

    def step(R, kv_n):
        return R * chunk_decay + kv_n, R

    _, R_prev = lax.scan(step, jnp.zeros((B, RET_HEADS, RET_QK_DIM, RET_V_DIM), jnp.float32), kv)
    q_dec = jnp.exp((pos + 1.0)[None] * log_gamma[:, None])
    cross = jnp.einsum('bhnid,nbhde,hi->bhnie', qc, R_prev, q_dec)
    y = (inner + cross).transpose(0, 2, 3, 1, 4).reshape(B, S, RET_HEADS, RET_V_DIM)
    y = y * lax.rsqrt(jnp.mean(y * y, axis=-1, keepdims=True) + EPS)
    return (y.reshape(B, S, RET_V_WIDTH) * jax.nn.silu(g)).astype(p.dtype)

def sgu_branch(p, ln_g, ln_b, w_s, b_s):
    B, S, _ = p.shape
    nC = S // SG_CHUNK
    z = jax.nn.gelu(p, approximate=False)
    u, v = jnp.split(z, 2, axis=-1)
    vf = v.astype(jnp.float32)
    mean = jnp.mean(vf, axis=-1, keepdims=True)
    var = jnp.mean(jnp.square(vf - mean), axis=-1, keepdims=True)
    v = ((vf - mean) * lax.rsqrt(var + EPS) * ln_g + ln_b).astype(p.dtype)
    vc = v.reshape(B, nC, SG_CHUNK, SG_GROUPS, SG_GROUP_DIM)
    causal = jnp.tril(jnp.ones((SG_CHUNK, SG_CHUNK), dtype=bool))
    w = jnp.where(causal[None], w_s, 0.0)
    mixed = jnp.einsum('gij,bnjgd->bnigd', w, vc) + b_s.T[:, :, None]
    return u * mixed.reshape(B, S, SG_WIDTH)

def conv_ffn(h, w_up, conv_w, conv_b, w_down):
    S = h.shape[1]
    u = h @ w_up
    up = jnp.pad(u, ((0, 0), (CONV_WIDTH - 1, 0), (0, 0)))
    c = conv_b
    for j in range(CONV_WIDTH):
        c = c + conv_w[j] * up[:, j:j + S]
    gate, val = jnp.split(c, 2, axis=-1)
    return (jax.nn.silu(gate) * val) @ w_down

def _normal(k, shape, scale):
    return scale * jax.random.normal(k, shape, jnp.float32)

def first_inputs(seed: int = 0) -> dict:
    key = jax.random.key(seed)
    ks = jax.random.split(key, 32)
    L = DEPTH
    f32 = jnp.float32
    return {
        "x": jax.random.normal(ks[0], (BATCH, SEQ, D_MODEL), f32),
        "norm1_g": 1.0 + _normal(ks[1], (L, D_MODEL), 0.05),
        "w_in": _normal(ks[2], (L, D_MODEL, IN_COLS), D_MODEL ** -0.5),
        "rw_mu": jax.random.uniform(ks[3], (L, RW_COLS), f32),
        "rw_w0": jax.random.uniform(ks[4], (L, RW_WIDTH), f32, -6.0, 1.0),
        "rw_w_up": _normal(ks[5], (L, RW_DECAY_RANK, RW_WIDTH), 0.1 * RW_DECAY_RANK ** -0.5),
        "rw_a0": _normal(ks[6], (L, RW_WIDTH), 0.1),
        "rw_a_up": _normal(ks[7], (L, RW_ICLR_RANK, RW_WIDTH), 0.3 * RW_ICLR_RANK ** -0.5),
        "rw_g_up": _normal(ks[8], (L, RW_GATE_RANK, RW_WIDTH), RW_GATE_RANK ** -0.5),
        "rw_k_k": 0.85 + _normal(ks[9], (L, RW_WIDTH), 0.05),
        "rw_k_a": 1.0 + _normal(ks[10], (L, RW_WIDTH), 0.05),
        "rw_r_k": _normal(ks[11], (L, RW_HEADS, RW_HEAD_DIM), 0.1),
        "rw_lnx_g": 1.0 + _normal(ks[12], (L, RW_HEADS, RW_HEAD_DIM), 0.05),
        "rw_lnx_b": _normal(ks[13], (L, RW_HEADS, RW_HEAD_DIM), 0.02),
        "sg_ln_g": 1.0 + _normal(ks[14], (L, SG_WIDTH), 0.05),
        "sg_ln_b": _normal(ks[15], (L, SG_WIDTH), 0.02),
        "sg_w_s": _normal(ks[16], (L, SG_GROUPS, SG_CHUNK, SG_CHUNK), SG_CHUNK ** -0.5),
        "sg_b": 1.0 + _normal(ks[17], (L, SG_GROUPS, SG_CHUNK), 0.1),
        "w_branch": _normal(ks[18], (L, N_BRANCH, BRANCH_WIDTH, D_MODEL), BRANCH_WIDTH ** -0.5),
        "w_out": _normal(ks[19], (L, D_MODEL, D_MODEL), 0.5 * D_MODEL ** -0.5),
        "norm2_g": 1.0 + _normal(ks[20], (L, D_MODEL), 0.05),
        "ffn_w_up": _normal(ks[21], (L, D_MODEL, 2 * D_FF), D_MODEL ** -0.5),
        "ffn_conv_w": _normal(ks[22], (L, CONV_WIDTH, 2 * D_FF), CONV_WIDTH ** -0.5),
        "ffn_conv_b": _normal(ks[23], (L, 2 * D_FF), 0.02),
        "ffn_w_down": _normal(ks[24], (L, D_FF, D_MODEL), 0.5 * D_FF ** -0.5),
        "final_g": 1.0 + _normal(ks[25], (D_MODEL,), 0.05),
    }

def first_block(x, norm1_g, w_in, rw_mu, rw_w0, rw_w_up, rw_a0, rw_a_up, rw_g_up, rw_k_k, rw_k_a,
              rw_r_k, rw_lnx_g, rw_lnx_b, sg_ln_g, sg_ln_b, sg_w_s, sg_b, w_branch, w_out,
              norm2_g, ffn_w_up, ffn_conv_w, ffn_conv_b, ffn_w_down, final_g):
    B, S, _ = x.shape
    inv_freq = 1.0 / (ROPE_BASE ** jnp.linspace(0.0, 1.0, RET_QK_DIM // 2, dtype=jnp.float32))
    ang = jnp.arange(S, dtype=jnp.float32)[:, None] * inv_freq[None, :]
    cos, sin = jnp.cos(ang), jnp.sin(ang)
    in_cuts = [RW_COLS, RW_COLS + RET_COLS, RW_COLS + RET_COLS + SG_COLS]
    for l in range(DEPTH):
        h = rmsnorm(x, norm1_g[l])
        p = h @ w_in[l]
        p_rw, p_ret, p_sg, gate_logits = jnp.split(p, in_cuts, axis=-1)
        y_rw = rwkv7_branch(p_rw, rw_mu[l], rw_w0[l], rw_w_up[l], rw_a0[l], rw_a_up[l], rw_g_up[l],
                            rw_k_k[l], rw_k_a[l], rw_r_k[l], rw_lnx_g[l], rw_lnx_b[l])
        y_ret = retention_branch(p_ret, cos, sin)
        y_sg = sgu_branch(p_sg, sg_ln_g[l], sg_ln_b[l], sg_w_s[l], sg_b[l])
        branches = jnp.stack([y_rw, y_ret, y_sg], axis=2)
        proj = jnp.einsum('bsgc,gcd->bsgd', branches, w_branch[l])
        gates = jax.nn.sigmoid(gate_logits.reshape(B, S, N_BRANCH, D_MODEL))
        x = x + jnp.sum(gates * proj, axis=2) @ w_out[l]
        x = x + conv_ffn(rmsnorm(x, norm2_g[l]), ffn_w_up[l], ffn_conv_w[l], ffn_conv_b[l], ffn_w_down[l])
    return rmsnorm(x, final_g)


N_HEADS = 4
HEAD_DIM = 64
BR_WIDTH = N_HEADS * HEAD_DIM
N_BRANCH_2 = 5
N_MEM = 256
ROPE_THETA = 10000.0
Q_BLOCK = 128
DSA_TOPK_MAX = 256
IDX_HEADS = 4
IDX_DIM = 32
KV_LATENT = 128
NSA_KV_DIM = 64
CMP_LEN = 32
CMP_STRIDE = 16
CMP_HIDDEN = 128
SLC_BLOCK = 64
SLC_TOPN = 16
WINDOW = 512
FORCE_SCORE = 1e4

IN_LAYOUT = (
    ('dsa_q', BR_WIDTH), ('dsa_ckv', KV_LATENT), ('idx_q', IDX_HEADS * IDX_DIM), ('idx_k', IDX_DIM), ('idx_w', IDX_HEADS), ('dsa_z', BR_WIDTH),
    ('fox_q', BR_WIDTH), ('fox_k', BR_WIDTH), ('fox_v', BR_WIDTH), ('fox_f', N_HEADS), ('fox_z', BR_WIDTH),
    ('sb_q', BR_WIDTH), ('sb_k', BR_WIDTH), ('sb_v', BR_WIDTH), ('sb_z', BR_WIDTH),
    ('nsa_q', BR_WIDTH), ('nsa_kc', NSA_KV_DIM), ('nsa_vc', NSA_KV_DIM), ('nsa_ks', NSA_KV_DIM), ('nsa_vs', NSA_KV_DIM),
    ('nsa_kw', NSA_KV_DIM), ('nsa_vw', NSA_KV_DIM), ('nsa_g', 3 * N_HEADS), ('nsa_z', BR_WIDTH),
    ('mem_q', BR_WIDTH), ('mem_z', BR_WIDTH),
    ('merge', N_BRANCH_2 * D_MODEL),
)
N_IN = sum(n for _, n in IN_LAYOUT)


def _rmsnorm(x, g):
    xf = x.astype(jnp.float32)
    y = xf * lax.rsqrt(jnp.mean(xf * xf, axis=-1, keepdims=True) + EPS)
    return (y * g.astype(jnp.float32)).astype(x.dtype)

def _rope(x, pos):
    dh = x.shape[-1]
    inv = ROPE_THETA ** (-jnp.arange(0, dh, 2, dtype=jnp.float32) / dh)
    ang = pos.astype(jnp.float32)[..., None] * inv
    ang = ang.reshape(ang.shape[:2] + (1,) * (x.ndim - 3) + ang.shape[-1:])
    cos, sin = jnp.cos(ang), jnp.sin(ang)
    xf = x.astype(jnp.float32)
    x1, x2 = xf[..., : dh // 2], xf[..., dh // 2:]
    return jnp.concatenate([x1 * cos - x2 * sin, x2 * cos + x1 * sin], axis=-1).astype(x.dtype)

def _masked_softmax(logits, mask):
    l = jnp.where(mask, logits, -jnp.inf)
    m = jnp.max(l, axis=-1, keepdims=True)
    m = jnp.where(jnp.isfinite(m), m, 0.0)
    e = jnp.where(mask, jnp.exp(l - m), 0.0)
    return e / jnp.maximum(jnp.sum(e, axis=-1, keepdims=True), 1e-30)

def _to_blocks(a):
    b, s = a.shape[:2]
    return jnp.moveaxis(a.reshape((b, s // Q_BLOCK, Q_BLOCK) + a.shape[2:]), 1, 0)

def _from_blocks(a):
    nq, b, q = a.shape[:3]
    return jnp.moveaxis(a, 0, 1).reshape((b, nq * q) + a.shape[3:])

def _gather_rows(table, idx):
    return jax.vmap(lambda tb, ib: tb[ib])(table, idx)

def _split_columns(p):
    out, off = {}, 0
    for name, n in IN_LAYOUT:
        out[name] = p[..., off:off + n]
        off += n
    return out

def _dsa_attention(q, k, v, qi, ki, wi):
    B, S, H, Dh = q.shape
    k_sel = min(DSA_TOPK_MAX, S // 4)
    s_pos = jnp.arange(S)
    scale = Dh ** -0.5
    idx_scale = (IDX_DIM ** -0.5) * (IDX_HEADS ** -0.5)

    def block(args):
        qb, q_blk, qi_blk, wi_blk = args
        t = qb * Q_BLOCK + jnp.arange(Q_BLOCK)
        rel = jax.nn.relu(jnp.einsum('bqhd,bsd->bqhs', qi_blk, ki).astype(jnp.float32))
        score = jnp.einsum('bqhs,bqh->bqs', rel, wi_blk.astype(jnp.float32)) * idx_scale
        score = jnp.where(s_pos[None, None, :] <= t[None, :, None], score, -jnp.inf)
        _, sel = lax.top_k(score, k_sel)
        kg = _gather_rows(k, sel)
        vg = _gather_rows(v, sel)
        logits = jnp.einsum('bqhd,bqkhd->bhqk', q_blk, kg).astype(jnp.float32) * scale
        mask = (sel <= t[None, :, None])[:, None]
        p = _masked_softmax(logits, mask).astype(v.dtype)
        return jnp.einsum('bhqk,bqkhd->bqhd', p, vg)

    out = lax.map(block, (jnp.arange(S // Q_BLOCK), _to_blocks(q), _to_blocks(qi), _to_blocks(wi)))
    return _from_blocks(out)

def _fox_attention(q, k, v, log_f):
    B, S, H, Dh = q.shape
    s_pos = jnp.arange(S)
    scale = Dh ** -0.5
    cum = jnp.cumsum(log_f.astype(jnp.float32), axis=1)
    cum_s = jnp.moveaxis(cum, 1, 2)

    def block(args):
        qb, q_blk, c_blk = args
        t = qb * Q_BLOCK + jnp.arange(Q_BLOCK)
        logits = (jnp.einsum('bqhd,bshd->bhqs', q_blk, k).astype(jnp.float32) * scale
                  + jnp.moveaxis(c_blk, 1, 2)[..., None] - cum_s[:, :, None, :])
        mask = (s_pos[None, :] <= t[:, None])[None, None]
        p = _masked_softmax(logits, mask).astype(v.dtype)
        return jnp.einsum('bhqs,bshd->bqhd', p, v)

    out = lax.map(block, (jnp.arange(S // Q_BLOCK), _to_blocks(q), _to_blocks(cum)))
    return _from_blocks(out)

def _stick_breaking_attention(q, k, v):
    B, S, H, Dh = q.shape
    s_pos = jnp.arange(S)
    scale = Dh ** -0.5

    def block(args):
        qb, q_blk = args
        t = qb * Q_BLOCK + jnp.arange(Q_BLOCK)
        z = jnp.einsum('bqhd,bshd->bhqs', q_blk, k).astype(jnp.float32) * scale
        strict = (s_pos[None, :] < t[:, None])[None, None]
        log_keep = jnp.where(strict, jax.nn.log_sigmoid(-z), 0.0)
        later = lax.cumsum(log_keep, axis=3, reverse=True) - log_keep
        a = jnp.where(strict, jnp.exp(jax.nn.log_sigmoid(z) + later), 0.0).astype(v.dtype)
        return jnp.einsum('bhqs,bshd->bqhd', a, v)

    out = lax.map(block, (jnp.arange(S // Q_BLOCK), _to_blocks(q)))
    return _from_blocks(out)

def _nsa_attention(q, kc_tok, vc_tok, ks, vs, kw, vw, gates, pe_k, pe_v, wc1_k, wc2_k, wc1_v, wc2_v):
    B, S, H, Dh = q.shape
    scale = Dh ** -0.5
    n_cmp = (S - CMP_LEN) // CMP_STRIDE + 1
    n_blk = S // SLC_BLOCK
    n_sel = min(SLC_TOPN, n_blk)
    per_blk = SLC_BLOCK // CMP_STRIDE
    tok = (jnp.arange(n_cmp) * CMP_STRIDE)[:, None] + jnp.arange(CMP_LEN)[None, :]

    def compress(x_tok, pe, w1, w2):
        blocks = (x_tok[:, tok] + pe).reshape(B, n_cmp, CMP_LEN * x_tok.shape[-1])
        return jax.nn.silu(blocks @ w1) @ w2

    kc = compress(kc_tok, pe_k, wc1_k, wc2_k)
    vc = compress(vc_tok, pe_v, wc1_v, wc2_v)
    cmp_end = jnp.arange(n_cmp) * CMP_STRIDE + CMP_LEN - 1
    ks_blk = ks.reshape(B, n_blk, SLC_BLOCK, -1)
    vs_blk = vs.reshape(B, n_blk, SLC_BLOCK, -1)
    kw_pad = jnp.pad(kw, ((0, 0), (WINDOW, 0), (0, 0)))
    vw_pad = jnp.pad(vw, ((0, 0), (WINDOW, 0), (0, 0)))
    blk_ids = jnp.arange(n_blk)
    in_blk = jnp.arange(SLC_BLOCK)
    win_off = jnp.arange(WINDOW + Q_BLOCK) - WINDOW

    def block(args):
        qb, q_blk, g_blk = args
        t = qb * Q_BLOCK + jnp.arange(Q_BLOCK)
        lc = jnp.einsum('bqhd,bnd->bhqn', q_blk, kc).astype(jnp.float32) * scale
        pc = _masked_softmax(lc, (cmp_end[None, :] <= t[:, None])[None, None])
        o_cmp = jnp.einsum('bhqn,bnd->bqhd', pc.astype(vc.dtype), vc)
        imp = jnp.pad(jnp.sum(pc, axis=1), ((0, 0), (0, 0), (0, n_blk * per_blk - n_cmp)))
        imp = jnp.sum(imp.reshape(B, Q_BLOCK, n_blk, per_blk), axis=-1)
        cur = t // SLC_BLOCK
        forced = (blk_ids[None, :] == 0) | (blk_ids[None, :] == cur[:, None]) | (blk_ids[None, :] == cur[:, None] - 1)
        visible = blk_ids[None, :] <= cur[:, None]
        imp = jnp.where(forced[None], FORCE_SCORE, jnp.where(visible[None], imp, -1.0))
        _, sel = lax.top_k(imp, n_sel)
        ksg = _gather_rows(ks_blk, sel).reshape(B, Q_BLOCK, n_sel * SLC_BLOCK, -1)
        vsg = _gather_rows(vs_blk, sel).reshape(B, Q_BLOCK, n_sel * SLC_BLOCK, -1)
        pos = (sel[..., None] * SLC_BLOCK + in_blk).reshape(B, Q_BLOCK, n_sel * SLC_BLOCK)
        ls = jnp.einsum('bqhd,bqkd->bhqk', q_blk, ksg).astype(jnp.float32) * scale
        ps = _masked_softmax(ls, (pos <= t[None, :, None])[:, None])
        o_slc = jnp.einsum('bhqk,bqkd->bqhd', ps.astype(vs.dtype), vsg)
        kwb = lax.dynamic_slice_in_dim(kw_pad, qb * Q_BLOCK, WINDOW + Q_BLOCK, axis=1)
        vwb = lax.dynamic_slice_in_dim(vw_pad, qb * Q_BLOCK, WINDOW + Q_BLOCK, axis=1)
        s = qb * Q_BLOCK + win_off
        d = t[:, None] - s[None, :]
        mw = ((d >= 0) & (d < WINDOW) & (s[None, :] >= 0))[None, None]
        lw = jnp.einsum('bqhd,bkd->bhqk', q_blk, kwb).astype(jnp.float32) * scale
        pw = _masked_softmax(lw, mw)
        o_win = jnp.einsum('bhqk,bkd->bqhd', pw.astype(vw.dtype), vwb)
        return (g_blk[:, :, 0, :, None] * o_cmp + g_blk[:, :, 1, :, None] * o_slc
                + g_blk[:, :, 2, :, None] * o_win)

    out = lax.map(block, (jnp.arange(S // Q_BLOCK), _to_blocks(q), _to_blocks(gates)))
    return _from_blocks(out)

def _memory_attention(q, mem_k, mem_v):
    logits = jnp.einsum('bshd,bmhd->bhsm', q, mem_k).astype(jnp.float32) * HEAD_DIM ** -0.5
    p = jax.nn.softmax(logits, axis=-1).astype(mem_v.dtype)
    return jnp.einsum('bhsm,bmhd->bshd', p, mem_v)

def _layer(x, mem, positions, norm_g, w_in, kv_norm, w_uk, w_uv, fox_b, pe_k, pe_v,
           wc1_k, wc2_k, wc1_v, wc2_v, mem_norm, w_mem_kv, w_branch, w_out):
    B, S, _ = x.shape
    h = _rmsnorm(x, norm_g)
    p = _split_columns(h @ w_in)
    heads = lambda a: a.reshape(B, S, N_HEADS, HEAD_DIM)

    c_kv = _rmsnorm(p['dsa_ckv'], kv_norm)
    k_a = _rope(heads(c_kv @ w_uk), positions)
    v_a = heads(c_kv @ w_uv)
    q_a = _rope(heads(p['dsa_q']), positions)
    qi = _rope(p['idx_q'].reshape(B, S, IDX_HEADS, IDX_DIM), positions)
    ki = _rope(p['idx_k'], positions)
    y_a = _dsa_attention(q_a, k_a, v_a, qi, ki, p['idx_w'])

    log_f = jax.nn.log_sigmoid(p['fox_f'].astype(jnp.float32) + fox_b.astype(jnp.float32))
    y_b = _fox_attention(heads(p['fox_q']), heads(p['fox_k']), heads(p['fox_v']), log_f)

    y_c = _stick_breaking_attention(heads(p['sb_q']), heads(p['sb_k']), heads(p['sb_v']))

    q_d = _rope(heads(p['nsa_q']), positions)
    gates = jax.nn.sigmoid(p['nsa_g'].reshape(B, S, 3, N_HEADS))
    y_d = _nsa_attention(q_d, _rope(p['nsa_kc'], positions), p['nsa_vc'],
                         _rope(p['nsa_ks'], positions), p['nsa_vs'],
                         _rope(p['nsa_kw'], positions), p['nsa_vw'], gates,
                         pe_k, pe_v, wc1_k, wc2_k, wc1_v, wc2_v)

    mkv = _rmsnorm(mem, mem_norm) @ w_mem_kv
    mem_k = mkv[..., :BR_WIDTH].reshape(B, -1, N_HEADS, HEAD_DIM)
    mem_v = mkv[..., BR_WIDTH:].reshape(B, -1, N_HEADS, HEAD_DIM)
    y_e = _memory_attention(heads(p['mem_q']), mem_k, mem_v)

    ys = jnp.stack([
        y_a.reshape(B, S, BR_WIDTH) * jax.nn.silu(p['dsa_z']),
        y_b.reshape(B, S, BR_WIDTH) * jax.nn.silu(p['fox_z']),
        y_c.reshape(B, S, BR_WIDTH) * jax.nn.silu(p['sb_z']),
        y_d.reshape(B, S, BR_WIDTH) * jax.nn.silu(p['nsa_z']),
        y_e.reshape(B, S, BR_WIDTH) * jax.nn.silu(p['mem_z']),
    ], axis=2)
    merge = jax.nn.sigmoid(p['merge'].reshape(B, S, N_BRANCH_2, D_MODEL))
    merged = jnp.sum(merge * jnp.einsum('bsnc,ncd->bsnd', ys, w_branch), axis=2)
    return x + merged @ w_out

def second_inputs(seed: int = 0) -> dict:
    key = jax.random.key(seed)
    ks = jax.random.split(key, 24)
    f32 = jnp.float32

    def nrm(k, shape, fan_in):
        return jax.random.normal(k, shape, f32) * fan_in ** -0.5

    def gain(k, shape):
        return 1.0 + 0.02 * jax.random.normal(k, shape, f32)

    return {
        'x': jax.random.normal(ks[0], (BATCH, SEQ, D_MODEL), f32),
        'mem': jax.random.normal(ks[1], (BATCH, N_MEM, D_MODEL), f32),
        'positions': jnp.broadcast_to(jnp.arange(SEQ, dtype=jnp.int32), (BATCH, SEQ)),
        'norm_g': gain(ks[2], (DEPTH, D_MODEL)),
        'w_in': nrm(ks[3], (DEPTH, D_MODEL, N_IN), D_MODEL),
        'kv_norm': gain(ks[4], (DEPTH, KV_LATENT)),
        'w_uk': nrm(ks[5], (DEPTH, KV_LATENT, BR_WIDTH), KV_LATENT),
        'w_uv': nrm(ks[6], (DEPTH, KV_LATENT, BR_WIDTH), KV_LATENT),
        'fox_bias': jnp.linspace(1.0, 4.0, N_HEADS, dtype=f32)[None, :] + 0.1 * jax.random.normal(ks[7], (DEPTH, N_HEADS), f32),
        'nsa_pe_k': 0.1 * jax.random.normal(ks[8], (DEPTH, CMP_LEN, NSA_KV_DIM), f32),
        'nsa_pe_v': 0.1 * jax.random.normal(ks[9], (DEPTH, CMP_LEN, NSA_KV_DIM), f32),
        'nsa_wc1_k': nrm(ks[10], (DEPTH, CMP_LEN * NSA_KV_DIM, CMP_HIDDEN), CMP_LEN * NSA_KV_DIM),
        'nsa_wc2_k': nrm(ks[11], (DEPTH, CMP_HIDDEN, NSA_KV_DIM), CMP_HIDDEN),
        'nsa_wc1_v': nrm(ks[12], (DEPTH, CMP_LEN * NSA_KV_DIM, CMP_HIDDEN), CMP_LEN * NSA_KV_DIM),
        'nsa_wc2_v': nrm(ks[13], (DEPTH, CMP_HIDDEN, NSA_KV_DIM), CMP_HIDDEN),
        'mem_norm': gain(ks[14], (DEPTH, D_MODEL)),
        'w_mem_kv': nrm(ks[15], (DEPTH, D_MODEL, 2 * BR_WIDTH), D_MODEL),
        'w_branch': nrm(ks[16], (DEPTH, N_BRANCH_2, BR_WIDTH, D_MODEL), BR_WIDTH),
        'w_out': nrm(ks[17], (DEPTH, D_MODEL, D_MODEL), D_MODEL),
        'final_norm': gain(ks[18], (D_MODEL,)),
    }

def second_block(x, mem, positions, norm_g, w_in, kv_norm, w_uk, w_uv, fox_bias, nsa_pe_k, nsa_pe_v,
              nsa_wc1_k, nsa_wc2_k, nsa_wc1_v, nsa_wc2_v, mem_norm, w_mem_kv, w_branch, w_out, final_norm):
    for l in range(DEPTH):
        x = _layer(x, mem, positions, norm_g[l], w_in[l], kv_norm[l], w_uk[l], w_uv[l], fox_bias[l],
                   nsa_pe_k[l], nsa_pe_v[l], nsa_wc1_k[l], nsa_wc2_k[l], nsa_wc1_v[l], nsa_wc2_v[l],
                   mem_norm[l], w_mem_kv[l], w_branch[l], w_out[l])
    return _rmsnorm(x, final_norm)


def setup_inputs(seed=0):
    out = dict(first_inputs(seed))
    for name, value in second_inputs(seed + 1).items():
        if name != "x":
            out[name + "_2"] = value
    return out


def reference(
    x, norm1_g, w_in, rw_mu, rw_w0, rw_w_up, rw_a0, rw_a_up, rw_g_up, rw_k_k, rw_k_a, rw_r_k,
    rw_lnx_g, rw_lnx_b, sg_ln_g, sg_ln_b, sg_w_s, sg_b, w_branch, w_out, norm2_g, ffn_w_up,
    ffn_conv_w, ffn_conv_b, ffn_w_down, final_g, mem_2, positions_2, norm_g_2, w_in_2,
    kv_norm_2, w_uk_2, w_uv_2, fox_bias_2, nsa_pe_k_2, nsa_pe_v_2, nsa_wc1_k_2, nsa_wc2_k_2,
    nsa_wc1_v_2, nsa_wc2_v_2, mem_norm_2, w_mem_kv_2, w_branch_2, w_out_2, final_norm_2,
):
    x = first_block(
        x, norm1_g, w_in, rw_mu, rw_w0, rw_w_up, rw_a0, rw_a_up, rw_g_up, rw_k_k, rw_k_a,
        rw_r_k, rw_lnx_g, rw_lnx_b, sg_ln_g, sg_ln_b, sg_w_s, sg_b, w_branch, w_out, norm2_g,
        ffn_w_up, ffn_conv_w, ffn_conv_b, ffn_w_down, final_g,
    )
    return second_block(
        x, mem_2, positions_2, norm_g_2, w_in_2, kv_norm_2, w_uk_2, w_uv_2, fox_bias_2,
        nsa_pe_k_2, nsa_pe_v_2, nsa_wc1_k_2, nsa_wc2_k_2, nsa_wc1_v_2, nsa_wc2_v_2, mem_norm_2,
        w_mem_kv_2, w_branch_2, w_out_2, final_norm_2,
    )


_drawn_inputs = setup_inputs


def setup_inputs(seed=0):
    import zlib

    import numpy as np

    out = dict(_drawn_inputs(seed))
    spreads = {}
    factors = {'rw_w_up': 8.0,
     'rw_a0': 4.8,
     'rw_k_k': 4.971,
     'rw_k_a': 4.233,
     'rw_lnx_g': 4.426,
     'rw_lnx_b': 8.0,
     'sg_ln_g': 5.07,
     'sg_ln_b': 8.0,
     'ffn_conv_b': 3.88,
     'norm_g_2': 3.821,
     'kv_norm_2': 8.0,
     'nsa_pe_k_2': 8.0,
     'nsa_pe_v_2': 3.962,
     'nsa_wc1_k_2': 2.726,
     'nsa_wc2_k_2': 2.73,
     'mem_norm_2': 8.0,
     'final_norm_2': 2.788}
    for name, (base, spread) in spreads.items():
        noise = np.random.default_rng([zlib.crc32(name.encode()), seed]).standard_normal(out[name].shape)
        drawn = base * np.exp(spread * noise) if base else spread * noise
        out[name] = jnp.asarray(drawn.astype(out[name].dtype))
    for name, factor in factors.items():
        out[name] = (out[name] * factor).astype(out[name].dtype)
    return out
```

```python
from contextlib import ExitStack, contextmanager

import numpy as np
import concourse.bass as bass
import concourse.mybir as mybir

F32 = mybir.dt.float32
I32 = mybir.dt.int32
ALU = mybir.AluOpType
ACT = mybir.ActivationFunctionType
AX = mybir.AxisListType

P = 128
T = 512
D = 1024
KD = D // P
DEPTH = 2
CH = 128
NCH = T // CH
RING = 4
RING_COLUMNS = 5 * 10 * P
EPS = 1e-6
NEG = -1e30
RW_TILES, RET_TILES, SG_TILES = 14, 12, 8
IN1_TILES = RW_TILES + RET_TILES + SG_TILES
FFN_TILES = 22
GN_EPS = 64e-5
DECAY_RATE = float(np.exp(-0.5))


def offsets(sizes):
    at, out = 0, {}
    for name, n in sizes:
        out[name] = at
        at += n
    return out, at


PAR1, NPAR1 = offsets([("norm1", 8), ("mu", 14), ("w0", 4), ("a0", 4), ("k_k", 4), ("k_a", 4), ("r_k", 4),
                       ("lnx_g", 4), ("lnx_b", 4), ("ln_g", 4), ("ln_b", 4), ("norm2", 8),
                       ("conv", 3 * 44), ("conv_b", 44)])
SMALL1, NSMALL1 = offsets([("lora_up", 512), ("g_up", 512), ("w_sT", 512), ("sg_b", 512)])

CONST1, NCONST1 = offsets([("ident", 128), ("headsum", 128), ("rot", 128), ("strict_su", 128), ("neg_strict_su", 128), ("incl_su", 128),
                           ("level", 7 * 128), ("level0", 128), ("scan", 512), ("ret_cos", 512), ("ret_sin", 512),
                           ("ret_decay", 512), ("ret_qdec", 1024), ("ret_kdec", 4), ("ret_chunk", 2)])


def constants1():
    c = np.zeros((P, NCONST1), np.float32)

    def put(name, a):
        a = np.asarray(a, np.float32).reshape(P, -1)
        c[:, CONST1[name]:CONST1[name] + a.shape[1]] = a

    i, j = np.arange(P)[:, None], np.arange(P)[None, :]
    put("ident", i == j)
    put("headsum", i // 64 == j // 64)
    put("rot", rotation(64))
    put("strict_su", i < j)
    put("neg_strict_su", -(i < j).astype(np.float32))
    put("incl_su", i <= j)
    level = [(i >> (l + 1) == j >> (l + 1)) & ((i >> l) % 2 == 0) & ((j >> l) % 2 == 1) for l in range(7)]
    put("level", np.stack([m.astype(np.float32) for m in level], 1))
    put("level0", -level[0].T.astype(np.float32))
    put("scan", np.broadcast_to((np.arange(T) % CH != 0).astype(np.float32), (P, T)))
    inv = np.float32(1.0) / np.power(np.float32(10000.0), np.linspace(0, 1, 32, dtype=np.float32))
    ang = np.arange(T, dtype=np.float32)[None, :] * inv[np.arange(P) % 32][:, None]
    put("ret_cos", np.cos(ang.astype(np.float64)))
    put("ret_sin", np.sin(ang.astype(np.float64)))
    lg = np.log(1.0 - 2.0 ** (-5.0 - np.arange(4, dtype=np.float64)))
    put("ret_decay", np.stack([np.where(j >= i, np.exp(np.maximum(j - i, 0) * g), 0.0) for g in lg], 1))
    pos = np.arange(T) % CH
    head = np.stack([2 * t + np.arange(P) // 64 for t in range(2)], 1)
    put("ret_qdec", np.exp((pos + 1.0)[None, None, :] * lg[head][:, :, None]))
    put("ret_kdec", np.exp((CH - 1.0 - np.arange(P))[:, None] * lg[None, :]))
    put("ret_chunk", np.exp(CH * lg[head]))
    return c


def rotation(width):
    r = np.zeros((P, P), np.float32)
    half = width // 2
    for c in range(P):
        o = c % width
        if o < half:
            r[c + half, c] = -1.0
        else:
            r[c - half, c] = 1.0
    return r


class Core:
    pass


class Own:

    def __init__(self, engine, sem):
        self.engine, self.sem, self.n = engine, sem, 0

    def __call__(self, instruction):
        instruction.then_inc(self.sem, 1)
        self.n += 1

    def settle(self):
        self.engine.wait_ge(self.sem, self.n)

    def tell(self, sem):
        self.settle()
        self.engine.sem_inc(sem, 1)


@contextmanager
def phase(nc, *names):
    with ExitStack() as stack:
        sems = {name: stack.enter_context(nc.semaphore(name)) for name in names}
        with nc.Block() as block:
            yield block, sems
        for sem in sems.values():
            nc.sync.sem_clear(sem)
        nc.all_engine_barrier()


LANDED = [f"landed{s}" for s in range(RING)]


def slot(core, s, width):
    return core.ring[:, s * width:(s + 1) * width]


def stream(sp, sems, core, unit, count, blocks=KD, ring=RING):
    def load(n, s):
        sp.dma_start(slot(core, s, blocks * P), unit(n)).then_inc(sems[LANDED[s]], 16)

    for s in range(min(ring, count)):
        load(s, s)
    rounds = count // ring
    if rounds > 1:
        with sp.Fori(1, rounds) as r:
            for s in range(ring):
                sp.wait_ge(sems["projected"], r * ring + (s + 1 - ring))
                load(r * ring + s, s)
    for n in range(max(rounds, 1) * ring, count):
        sp.wait_ge(sems["projected"], n + 1 - ring)
        load(n, n % ring)


def project(pe, sems, core, rhs, count, blocks=KD):
    def tile(s, landed, evacuated):
        pe.wait_ge(sems[LANDED[s]], landed)
        if evacuated is not None:
            pe.wait_ge(sems["evacuated"], evacuated)
        w = slot(core, s, blocks * P)
        for k in range(blocks):
            mm = pe.matmul(core.banks[s][:, :], w[:, k * P:(k + 1) * P], rhs(k), start=(k == 0), stop=(k == blocks - 1))
        mm.then_inc(sems["projected"], 1)

    for s in range(min(RING, count)):
        tile(s, 16, None)
    rounds = count // RING
    if rounds > 1:
        with pe.Fori(1, rounds) as r:
            for s in range(RING):
                tile(s, r * 16 + 16, r * RING + (s + 1 - RING))
    for n in range(max(rounds, 1) * RING, count):
        tile(n % RING, 16 * (n // RING + 1), n + 1 - RING)


def evacuate(act, sems, banks, out, count):
    def tile(n, s, projected):
        act.wait_ge(sems["projected"], projected)
        act.copy(out(n), banks[s][:, :]).then_inc(sems["evacuated"], 1)

    rounds = count // RING
    if rounds:
        with act.Fori(0, rounds) as r:
            for s in range(RING):
                tile(r * RING + s, s, r * RING + (s + 1))
    for n in range(rounds * RING, count):
        tile(n, n % RING, n + 1)


def norm_squares(act, sems, x, squares, tiles=KD):
    for k in range(tiles):
        act.activation(squares[:, k, :], x[:, k, :], ACT.Square).then_inc(sems["squared"], 1)


def norm_sum(pe, sems, ones, squares, bank, tiles=KD):
    for k in range(tiles):
        pe.wait_ge(sems["squared"], k + 1)
        mm = pe.matmul(bank, ones, squares[:, k, :], start=(k == 0), stop=(k == tiles - 1))
    mm.then_inc(sems["summed"], 1)


def norm_root(act, sems, bank, root, eps, width=D):
    act.wait_ge(sems["summed"], 1)
    act.activation(root, bank, ACT.Sqrt, bias=eps, scale=1.0 / width).then_inc(sems["rooted"], 1)


def norm_scale(dve, sems, own, x, root, gain, out, tiles=KD):
    dve.wait_ge(sems["rooted"], 1)
    own(dve.reciprocal(root, root))
    own.settle()
    for k in range(tiles):
        dve.scalar_tensor_tensor(out=out[:, k, :], in0=x[:, k, :], scalar=gain[:, k:k + 1], in1=root,
                                 op0=ALU.mult, op1=ALU.mult).then_inc(sems["normed"], 1)


def wide(ap, tiles):
    return ap.rearrange("p (a b) -> p a b", a=tiles)


def project_in1(nc, core, layer, w, first, tiles, out, normalise):
    par = core.par
    with phase(nc, *LANDED, "projected", "evacuated", "squared", "summed", "rooted", "normed", "params", "own") as (block, sems):
        @block.sync
        def _(sp):
            stream(sp, sems, core, lambda n: w["in1"][layer * IN1_TILES + first + n], tiles)

        @block.scalar
        def _(act):
            if normalise:
                act.dma_start(par[:, 0:NPAR1], w["par1"][layer]).then_inc(sems["params"], 16)
                act.dma_start(core.small[:, 0:NSMALL1], w["small1"][layer]).then_inc(sems["params"], 16)
                norm_squares(act, sems, core.x, core.h)
                norm_root(act, sems, core.banks[7][:, :], core.root[:, :], core.eps[:, 0:1])
            evacuate(act, sems, core.banks, out, tiles)
            if normalise:
                act.wait_ge(sems["params"], 32)

        @block.tensor
        def _(pe):
            if normalise:
                norm_sum(pe, sems, core.ones[:, :], core.h, core.banks[7][:, :])
                pe.wait_ge(sems["normed"], KD)
            project(pe, sems, core, lambda k: core.h[:, k, :], tiles)

        if normalise:
            @block.vector
            def _(dve):
                dve.wait_ge(sems["params"], 32)
                norm_scale(dve, sems, Own(dve, sems["own"]), core.x, core.root[:, :],
                           par[:, PAR1["norm1"]:PAR1["norm1"] + 8], core.h)


def rwkv_prepare(nc, core, b):
    par, small, con, banks = core.par, core.small, core.con, core.banks

    def col(name, n):
        return par[:, PAR1[name] + n:PAR1[name] + n + 1]

    p = b["p_rw"]
    r, k, v = (p[:, 4 * n:4 * n + 4, 1:] for n in range(3))
    lw, decay, rate, gate, kk, bonus = (b[n] for n in ("A", "B", "C", "D", "E", "F"))
    tmp, grow = b["H"], b["G"]
    mid, end = core.tiny[:, 8:24], core.tiny[:, 24:40]
    with phase(nc, "low_shifted", "hidden", "decay_mm", "rate_mm", "gate_mm", "norm_mm", "bonus_mm", "decay_rate_out",
               "gate_out", "norm_out", "keys_squared", "exponents", "before_exp", "grown", "rkk", "own", "own_act") as (block, sems):
        @block.vector
        def _(dve):
            own = Own(dve, sems["own"])
            own(dve.memset(p[:, :, 0:1], 0.0))
            own.settle()
            for lo in (12, 8, 4, 0):
                n = 2 if lo == 12 else 4
                diff = grow[:, 0:n, :]
                own(dve.tensor_tensor(diff, p[:, lo:lo + n, 0:T], p[:, lo:lo + n, 1:], ALU.subtract))
                own.settle()
                for m in range(n):
                    own(dve.scalar_tensor_tensor(out=p[:, lo + m, 1:], in0=diff[:, m, :], scalar=col("mu", lo + m),
                                                 in1=p[:, lo + m, 1:], op0=ALU.mult, op1=ALU.add))
                own.settle()
                if lo == 12:
                    own.tell(sems["low_shifted"])
            own(dve.tensor_scalar(core.tiny[:, 0:4], par[:, PAR1["k_a"]:PAR1["k_a"] + 4], -1.0, 1.0, ALU.mult, ALU.add))
            for m in range(4):
                own(dve.tensor_scalar(kk[:, m, :], k[:, m, :], col("k_k", m), None, ALU.mult))
            own.settle()
            own(dve.tensor_tensor(grow[:, :, :], kk[:, :, :], kk[:, :, :], ALU.mult))
            own.tell(sems["keys_squared"])
            dve.wait_ge(sems["decay_rate_out"], 1)
            own(dve.tensor_scalar(lw[:, :, :], lw[:, :, :], -DECAY_RATE, None, ALU.mult))
            own.settle()
            for m in range(4):
                own(dve.tensor_tensor_scan(decay[:, m, :], con[:, CONST1["scan"]:CONST1["scan"] + T], lw[:, m, :], 0.0,
                                           ALU.mult, ALU.add))
            own.settle()
            chunks = [decay[:, m, :].rearrange("p (c t) -> p c t", c=NCH) for m in range(4)]
            for m in range(4):
                own(dve.tensor_copy(mid[:, 4 * m:4 * m + 4], chunks[m][:, :, CH // 2 - 1]))
                own(dve.tensor_tensor(end[:, 4 * m:4 * m + 4], chunks[m][:, :, CH - 1], chunks[m][:, :, CH // 2 - 1],
                                      ALU.subtract))
            own.settle()
            for m in range(4):
                own(dve.tensor_tensor(chunks[m], chunks[m],
                                      mid[:, 4 * m:4 * m + 4].rearrange("p (c o) -> p c o", o=1).to_broadcast([P, NCH, CH]),
                                      ALU.subtract))
            own.settle()
            own(dve.tensor_tensor(lw[:, :, :], decay[:, :, :], lw[:, :, :], ALU.subtract))
            own.tell(sems["exponents"])
            for m in range(4):
                own(dve.tensor_scalar(tmp[:, m, :], rate[:, m, :], col("k_a", m), core.tiny[:, m:m + 1], ALU.mult, ALU.add))
            own.settle()
            own(dve.tensor_tensor(k, k, tmp[:, :, :], ALU.mult))
            own.settle()
            for m in range(4):
                own(dve.scalar_tensor_tensor(out=tmp[:, m, :], in0=r[:, m, :], scalar=col("r_k", m), in1=k[:, m, :],
                                             op0=ALU.mult, op1=ALU.mult))
            own.tell(sems["rkk"])
            dve.wait_ge(sems["norm_out"], 1)
            own(dve.tensor_scalar(bonus[:, :, :], bonus[:, :, :], 1e-12, None, ALU.max))
            own.settle()
            own(dve.reciprocal(bonus[:, :, :], bonus[:, :, :]))
            own.settle()
            own(dve.tensor_tensor(kk[:, :, :], kk[:, :, :], bonus[:, :, :], ALU.mult))
            own.settle()
            own(dve.tensor_tensor(rate[:, :, :], rate[:, :, :], kk[:, :, :], ALU.mult))
            dve.wait_ge(sems["before_exp"], 1)
            own(dve.tensor_tensor(lw[:, :, :], lw[:, :, :], kk[:, :, :], ALU.mult))
            own.settle()
            dve.wait_ge(sems["grown"], 1)
            own(dve.tensor_tensor(rate[:, :, :], rate[:, :, :], grow[:, :, :], ALU.mult))
            own(dve.tensor_tensor(k, k, grow[:, :, :], ALU.mult))
            own(dve.tensor_tensor(r, r, decay[:, :, :], ALU.mult))
            for m in range(4):
                dve.wait_ge(sems["bonus_mm"], m + 1)
                own(dve.tensor_tensor(bonus[:, m, :], banks[m][:, :], v[:, m, :], ALU.mult))
            own.settle()

        @block.scalar
        def _(act):
            own = Own(act, sems["own_act"])
            act.wait_ge(sems["low_shifted"], 1)
            own(act.activation(p[0:64, 12, 1:], p[0:64, 12, 1:], ACT.Tanh))
            own(act.activation(p[:, 13, 1:], p[:, 13, 1:], ACT.Sigmoid))
            own.tell(sems["hidden"])
            for m in range(4):
                act.wait_ge(sems["decay_mm"], m + 1)
                own(act.activation(lw[:, m, :], banks[m][:, :], ACT.Sigmoid, bias=col("w0", m)))
            for m in range(4):
                act.wait_ge(sems["rate_mm"], m + 1)
                own(act.activation(rate[:, m, :], banks[4 + m][:, :], ACT.Sigmoid, bias=col("a0", m)))
            own.tell(sems["decay_rate_out"])
            for m in range(4):
                act.wait_ge(sems["gate_mm"], m + 1)
                own(act.copy(gate[:, m, :], banks[m][:, :]))
            own.tell(sems["gate_out"])
            for m in range(4):
                act.wait_ge(sems["norm_mm"], m + 1)
                own(act.activation(bonus[:, m, :], banks[4 + m][:, :], ACT.Sqrt))
            own.tell(sems["norm_out"])
            act.wait_ge(sems["exponents"], 1)
            own(act.activation(lw[:, :, :], lw[:, :, :], ACT.Exp))
            own.tell(sems["before_exp"])
            own(act.activation(grow[:, :, :], decay[:, :, :], ACT.Exp, scale=-1.0))
            own.settle()
            own(act.activation(decay[:, :, :], decay[:, :, :], ACT.Exp))
            own(act.activation(core.tiny[:, 8:40], core.tiny[:, 8:40], ACT.Exp))
            own.tell(sems["grown"])

        @block.tensor
        def _(pe):
            lora = small[:, SMALL1["lora_up"]:SMALL1["lora_up"] + 512]
            g_up = small[:, SMALL1["g_up"]:SMALL1["g_up"] + 512]
            head = con[:, CONST1["headsum"]:CONST1["headsum"] + P]

            def product(bank, lhsT, rhs, name):
                pe.matmul(bank[:, :], lhsT, rhs, start=True, stop=True).then_inc(sems[name], 1)

            pe.wait_ge(sems["hidden"], 1)
            for m in range(4):
                product(banks[m], lora[0:64, m * P:(m + 1) * P], p[0:64, 12, 1:], "decay_mm")
            for m in range(4):
                product(banks[4 + m], lora[64:128, m * P:(m + 1) * P], p[64:128, 12, 1:], "rate_mm")
            pe.wait_ge(sems["decay_rate_out"], 1)
            for m in range(4):
                product(banks[m], g_up[:, m * P:(m + 1) * P], p[:, 13, 1:], "gate_mm")
            pe.wait_ge(sems["keys_squared"], 1)
            for m in range(4):
                product(banks[4 + m], head, grow[:, m, :], "norm_mm")
            pe.wait_ge(sems["gate_out"], 1)
            pe.wait_ge(sems["rkk"], 1)
            for m in range(4):
                product(banks[m], head, tmp[:, m, :], "bonus_mm")


def rwkv_scan(nc, core, b, y):
    con, banks, ident = core.con, core.banks, core.ident
    A, B, V, Kt, R = b["A"], b["C"], b["p_rw"][:, 8:12, 1:], b["p_rw"][:, 4:8, 1:], b["p_rw"][:, 0:4, 1:]
    S = b["state"]

    def heads(name, n=P):
        return con[:, CONST1[name]:CONST1[name] + n].rearrange("p (o t) -> p o t", o=1).to_broadcast([P, 4, P])

    def level(l):
        at = CONST1["level"] + l * P
        return con[:, at:at + P].rearrange("p (o t) -> p o t", o=1).to_broadcast([P, 4, P])

    def token_major(h, m):
        return slice(m * P + h * 64, m * P + h * 64 + 64)

    with phase(nc, "tok_mm", "tok_out", "pair_mm", "pair_out", "level_ready", "x_mm", "x_out", "inv_mm", "inv_out",
               "mix_mm", "mix_out", "u_mm", "u_out", "y_mm", "y_out", "state_mm", "scaled", "own",
               "own_act") as (block, sems):
        @block.vector
        def _(dve):
            own = Own(dve, sems["own"])
            own(dve.memset(S[:, :, :], 0.0))
            own.settle()
            for c in range(NCH):
                for m in range(4):
                    own(dve.tensor_scalar(S[:, m, :], S[:, m, :], core.tiny[:, 8 + 4 * m + c:9 + 4 * m + c], None, ALU.mult))
                own.tell(sems["scaled"])
                for h in range(2):
                    n = 2 * c + h
                    w = b["work"][h]
                    dve.wait_ge(sems["pair_mm"], 5 * n + 1)
                    own(dve.tensor_tensor(w["negNT"][:, :, :], wide(banks[0][:, :], 4), heads("neg_strict_su"), ALU.mult))
                    own.settle()
                    own(dve.tensor_tensor(w["invT"][:, :, :], w["negNT"][:, :, :], level(0), ALU.mult))
                    own.tell(sems["pair_out"])
                    dve.wait_ge(sems["pair_mm"], 5 * n + 2)
                    own(dve.tensor_tensor(w["inv"][:, :, :], wide(banks[1][:, :], 4), heads("level0"), ALU.mult))
                    own.tell(sems["pair_out"])
                    own(dve.tensor_tensor(w["invT"][:, :, :], w["invT"][:, :, :], heads("ident"), ALU.add))
                    own(dve.tensor_tensor(w["inv"][:, :, :], w["inv"][:, :, :], heads("ident"), ALU.add))
                    for q, name in enumerate(("PmT", "QbT", "QkT")):
                        dve.wait_ge(sems["pair_mm"], 5 * n + 3 + q)
                        own(dve.tensor_tensor(w[name][:, :, :], wide(banks[(2 + q) % 2][:, :], 4),
                                              heads("strict_su") if q == 0 else heads("incl_su"), ALU.mult))
                        own.tell(sems["pair_out"])
                for l in range(1, 7):
                    for h in range(2):
                        n = (c * 6 + l - 1) * 2 + h
                        w = b["work"][h]
                        dve.wait_ge(sems["inv_mm"], n + 1)
                        if l < 6:
                            own(dve.tensor_tensor(w["inv"][:, :, :], w["inv"][:, :, :], wide(banks[4 + h][:, :], 4), ALU.add))
                        own(dve.tensor_tensor(w["invT"][:, :, :], w["invT"][:, :, :], wide(banks[6 + h][:, :], 4), ALU.add))
                        own.tell(sems["inv_out"])
                dve.wait_ge(sems["state_mm"], c + 1)
                own(dve.tensor_tensor(S[:, :, :], S[:, :, :], wide(banks[2][:, 0:256], 4), ALU.add))
                own.settle()
                for m in range(4):
                    own(dve.tensor_scalar(S[:, m, :], S[:, m, :], core.tiny[:, 24 + 4 * m + c:25 + 4 * m + c], None, ALU.mult))
                own.settle()

        @block.gpsimd
        def _(pool):
            for c in range(NCH):
                for l in range(1, 7):
                    for h in range(2):
                        n = (c * 6 + l - 1) * 2 + h
                        w = b["work"][h]
                        if l == 1:
                            pool.wait_ge(sems["pair_out"], (2 * c + h) * 5 + 1)
                        if n >= 2:
                            pool.wait_ge(sems["x_mm"], n - 1)
                        pool.tensor_tensor(w["levelT"][:, :, :], w["negNT"][:, :, :], level(l), ALU.mult)\
                            .then_inc(sems["level_ready"], 1)

        @block.scalar
        def _(act):
            own = Own(act, sems["own_act"])
            for c in range(NCH):
                for i, name in enumerate(("Vt", "Kt", "Bt")):
                    act.wait_ge(sems["tok_mm"], 3 * c + i + 1)
                    act.copy(b[name][:, :], banks[5 + i][:, :]).then_inc(sems["tok_out"], 1)
                for l in range(1, 7):
                    for h in range(2):
                        n = (c * 6 + l - 1) * 2 + h
                        act.wait_ge(sems["x_mm"], n + 1)
                        act.copy(b["work"][h]["X"][:, :, :], wide(banks[2 + h][:, :], 4)).then_inc(sems["x_out"], 1)
                for name, ready, out, at, by in (("mix", "mix_mm", "mix_out", 0, -1.0), ("U", "u_mm", "u_out", 256, 1.0)):
                    for h in range(2):
                        act.wait_ge(sems[ready], 2 * c + h + 1)
                        act.mul(wide(b[name][:, :], 4)[:, :, 64 * h:64 * h + 64], wide(banks[h][:, at:at + 256], 4), by)\
                            .then_inc(sems[out], 1)
                act.wait_ge(sems["y_mm"], c + 1)
                act.copy(y[:, :, c * CH:(c + 1) * CH], wide(banks[3][:, :], 4)).then_inc(sems["y_out"], 1)

        @block.tensor
        def _(pe):
            for c in range(NCH):
                t = slice(c * CH, (c + 1) * CH)
                for i, src in enumerate((V, Kt, B)):
                    if c:
                        pe.wait_ge(sems["inv_out"], 12 * c)
                    for m in range(4):
                        mm = pe.transpose(banks[5 + i][:, m * P:(m + 1) * P], src[:, m, t], ident)
                    mm.then_inc(sems["tok_mm"], 1)
                for h in range(2):
                    n = 2 * c + h

                    def pairs(index, left, right):
                        if index >= 2:
                            pe.wait_ge(sems["pair_out"], 5 * n + index - 1)
                        elif n and index == 0:
                            pe.wait_ge(sems["pair_out"], 5 * n)
                            if h == 0:
                                pe.wait_ge(sems["mix_out"], 2 * c)
                                pe.wait_ge(sems["u_out"], 2 * c)
                        for m in range(4):
                            lo = 64 * h
                            mm = pe.matmul(banks[index % 2][:, m * P:(m + 1) * P], left[lo:lo + 64, m, t],
                                           right[lo:lo + 64, m, t], start=True, stop=True)
                        mm.then_inc(sems["pair_mm"], 1)

                    pairs(0, B, A)
                    pairs(1, A, B)
                    pairs(2, Kt, A)
                    pairs(3, B, R)
                    pairs(4, Kt, R)
                pe.wait_ge(sems["tok_out"], 3 * c + 3)
                for l in range(1, 7):
                    for h in range(2):
                        n = (c * 6 + l - 1) * 2 + h
                        w = b["work"][h]
                        pe.wait_ge(sems["level_ready"], n + 1)
                        if l == 1:
                            pe.wait_ge(sems["pair_out"], 10 * c + 10)
                        else:
                            pe.wait_ge(sems["inv_out"], n - 1)
                        for q in range(4):
                            mm = pe.matmul(banks[2 + h][:, q * P:(q + 1) * P], w["levelT"][:, q, :], w["inv"][:, q, :],
                                           start=True, stop=True)
                        mm.then_inc(sems["x_mm"], 1)
                    for h in range(2):
                        n = (c * 6 + l - 1) * 2 + h
                        w = b["work"][h]
                        pe.wait_ge(sems["x_out"], n + 1)
                        for q in range(4):
                            if l < 6:
                                pe.matmul(banks[4 + h][:, q * P:(q + 1) * P], w["invT"][:, q, :], w["X"][:, q, :],
                                          start=True, stop=True)
                            mm = pe.matmul(banks[6 + h][:, q * P:(q + 1) * P], w["X"][:, q, :], w["invT"][:, q, :],
                                           start=True, stop=True)
                        mm.then_inc(sems["inv_mm"], 1)
                pe.wait_ge(sems["scaled"], c + 1)
                for h in range(2):
                    w, lo = b["work"][h], 64 * h
                    for m in range(4):
                        out = banks[h][:, m * 64:(m + 1) * 64]
                        pe.matmul(out, A[lo:lo + 64, m, t], S[lo:lo + 64, m, :], start=True, stop=False)
                        mm = pe.matmul(out, w["PmT"][:, m, :], b["Vt"][:, token_major(h, m)], start=False, stop=True)
                    mm.then_inc(sems["mix_mm"], 1)
                pe.wait_ge(sems["inv_out"], 12 * c + 12)
                for h in range(2):
                    pe.wait_ge(sems["mix_out"], 2 * c + h + 1)
                    for m in range(4):
                        mm = pe.matmul(banks[h][:, 256 + m * 64:256 + (m + 1) * 64], b["work"][h]["invT"][:, m, :],
                                       b["mix"][:, token_major(h, m)], start=True, stop=True)
                    mm.then_inc(sems["u_mm"], 1)
                for h in range(2):
                    pe.wait_ge(sems["u_out"], 2 * c + h + 1)
                    w, lo = b["work"][h], 64 * h
                    for m in range(4):
                        out, at = banks[3][lo:lo + 64, m * P:(m + 1) * P], token_major(h, m)
                        pe.matmul(out, S[lo:lo + 64, m, :], R[lo:lo + 64, m, t], start=True, stop=False)
                        pe.matmul(out, b["U"][:, at], w["QbT"][:, m, :], start=False, stop=False)
                        mm = pe.matmul(out, b["Vt"][:, at], w["QkT"][:, m, :], start=False, stop=True)
                mm.then_inc(sems["y_mm"], 1)
                for h in range(2):
                    for m in range(4):
                        out, at = banks[2][64 * h:64 * h + 64, m * 64:(m + 1) * 64], token_major(h, m)
                        pe.matmul(out, b["Kt"][:, at], b["Vt"][:, at], start=True, stop=False)
                        mm = pe.matmul(out, b["Bt"][:, at], b["U"][:, at], start=False, stop=True)
                mm.then_inc(sems["state_mm"], 1)


def rwkv_finish(nc, core, b, y):
    par, con, banks = core.par, core.con, core.banks
    centred, squares, root = b["E"], b["B"], b["G"]
    with phase(nc, "mean_mm", "centred", "var_mm", "rooted", "own", "own_act") as (block, sems):
        head = con[:, CONST1["headsum"]:CONST1["headsum"] + P]

        @block.tensor
        def _(pe):
            for m in range(4):
                pe.matmul(banks[m][:, :], head, y[:, m, :], start=True, stop=True).then_inc(sems["mean_mm"], 1)
            for m in range(4):
                pe.wait_ge(sems["centred"], m + 1)
                pe.matmul(banks[4 + m][:, :], head, squares[:, m, :], start=True, stop=True).then_inc(sems["var_mm"], 1)

        @block.scalar
        def _(act):
            for m in range(4):
                act.wait_ge(sems["var_mm"], m + 1)
                act.activation(root[:, m, :], banks[4 + m][:, :], ACT.Sqrt, bias=core.eps[:, 1:2], scale=1.0 / 64)\
                    .then_inc(sems["rooted"], 1)

        @block.vector
        def _(dve):
            own = Own(dve, sems["own"])
            for m in range(4):
                dve.wait_ge(sems["mean_mm"], m + 1)
                own(dve.scalar_tensor_tensor(out=centred[:, m, :], in0=banks[m][:, :], scalar=-1.0 / 64, in1=y[:, m, :],
                                             op0=ALU.mult, op1=ALU.add))
                own.settle()
                dve.tensor_tensor(squares[:, m, :], centred[:, m, :], centred[:, m, :], ALU.mult).then_inc(sems["centred"], 1)
            dve.wait_ge(sems["rooted"], 4)
            own(dve.reciprocal(root[:, :, :], root[:, :, :]))
            own.settle()
            own(dve.tensor_tensor(centred[:, :, :], centred[:, :, :], root[:, :, :], ALU.mult))
            own.settle()
            for m in range(4):
                g, beta = PAR1["lnx_g"] + m, PAR1["lnx_b"] + m
                own(dve.tensor_scalar(centred[:, m, :], centred[:, m, :], par[:, g:g + 1], par[:, beta:beta + 1], ALU.mult, ALU.add))
            own.settle()
            own(dve.tensor_tensor(centred[:, :, :], centred[:, :, :], b["F"][:, :, :], ALU.add))
            own.settle()
            own(dve.tensor_tensor(y[:, :, :], centred[:, :, :], b["D"][:, :, :], ALU.mult))
            own.settle()


def retention(nc, core, b, y):
    con, banks, ident = core.con, core.banks, core.ident
    q, k, v, g = (b["p_rs"][:, lo:hi, :] for lo, hi in ((0, 2), (2, 4), (4, 8), (8, 12)))

    def table(name, n):
        return con[:, CONST1[name]:CONST1[name] + n]

    def block_of(name, c):
        return b[name][:, c, :]

    with phase(nc, "rot_mm", "rotated", "k_mm", "k_out", "v_mm", "v_out", "score_mm", "score_out", "kv_mm", "state_ready",
               "y_mm", "y_out", "squared", "summed", "rooted", "gated", "own", "own_act") as (block, sems):
        @block.tensor
        def _(pe):
            rot = table("rot", P)
            for i in range(4):
                src = q if i < 2 else k
                pe.matmul(banks[i][:, :], rot, src[:, i % 2, :], start=True, stop=True).then_inc(sems["rot_mm"], 1)
            for c in range(NCH):
                if c >= 2:
                    pe.wait_ge(sems["v_out"], c - 1)
                for m in range(4):
                    mm = pe.transpose(banks[4 + c % 2][:, m * P:(m + 1) * P], v[:, m, c * CH:(c + 1) * CH], ident)
                mm.then_inc(sems["v_mm"], 1)
            pe.wait_ge(sems["rotated"], 4)
            for c in range(NCH):
                t = slice(c * CH, (c + 1) * CH)
                if c >= 2:
                    pe.wait_ge(sems["k_out"], c - 1)
                for m in range(2):
                    mm = pe.transpose(banks[6 + c % 2][:, m * P:(m + 1) * P], k[:, m, t], ident)
                mm.then_inc(sems["k_mm"], 1)
                if c >= 2:
                    pe.wait_ge(sems["score_out"], 2 * (c - 1))
                if c == 1:
                    pe.wait_ge(sems["v_out"], NCH)
                for h in range(2):
                    for m in range(2):
                        mm = pe.matmul(banks[4 * (c % 2) + h][:, m * P:(m + 1) * P], k[64 * h:64 * h + 64, m, t],
                                       q[64 * h:64 * h + 64, m, t], start=True, stop=True)
                    mm.then_inc(sems["score_mm"], 1)
            for c in range(NCH):
                t = slice(c * CH, (c + 1) * CH)
                pe.wait_ge(sems["k_out"], c + 1)
                pe.wait_ge(sems["v_out"], c + 1)
                if c:
                    pe.wait_ge(sems["state_ready"], c + 1)
                if c < NCH - 1:
                    for h in range(4):
                        m, lo = h // 2, 64 * (h % 2)
                        mm = pe.matmul(banks[2][lo:lo + 64, m * P:(m + 1) * P], b["kt"][:, c, h * 64:(h + 1) * 64],
                                       b["vt"][:, c, h * P:(h + 1) * P], start=True, stop=True)
                    mm.then_inc(sems["kv_mm"], 1)
                pe.wait_ge(sems["score_out"], 2 * (c + 1))
                if c:
                    pe.wait_ge(sems["y_out"], 2 * c)
                else:
                    pe.wait_ge(sems["k_out"], NCH)
                for half in range(2):
                    for m in range(2):
                        h, lo = 2 * m + half, 64 * half
                        out = banks[3 + 4 * half][:, m * P:(m + 1) * P]
                        mm = pe.matmul(out, b["vt"][:, c, h * P:(h + 1) * P], b["scores"][:, c, h * P:(h + 1) * P],
                                       start=True, stop=(c == 0))
                        if c:
                            mm = pe.matmul(out, b["states"][lo:lo + 64, c, m * P:(m + 1) * P],
                                           b["qdec"][lo:lo + 64, m, t], start=False, stop=True)
                    mm.then_inc(sems["y_mm"], 1)
            pe.wait_ge(sems["y_out"], 2 * NCH)
            for h in range(4):
                pe.wait_ge(sems["squared"], h + 1)
                pe.matmul(banks[4 + h][:, :], core.ones[:, :], b["tmp"][:, h, :], start=True, stop=True)\
                    .then_inc(sems["summed"], 1)

        @block.scalar
        def _(act):
            for c in range(NCH):
                act.wait_ge(sems["v_mm"], c + 1)
                act.copy(b["vt"][:, c, :], banks[4 + c % 2][:, :]).then_inc(sems["v_out"], 1)
            for c in range(NCH):
                for half in range(2):
                    act.wait_ge(sems["y_mm"], 2 * c + half + 1)
                    act.copy(y[:, half::2, c * CH:(c + 1) * CH], wide(banks[3 + 4 * half][:, 0:256], 2))\
                        .then_inc(sems["y_out"], 1)
            act.activation(g, g, ACT.Silu).then_inc(sems["gated"], 1)
            for h in range(4):
                act.wait_ge(sems["summed"], h + 1)
                act.activation(b["root"][:, h, :], banks[4 + h][:, :], ACT.Sqrt, bias=core.eps[:, 0:1], scale=1.0 / P)\
                    .then_inc(sems["rooted"], 1)

        @block.vector
        def _(dve):
            own = Own(dve, sems["own"])
            scale = 64 ** -0.5
            for i in range(4):
                src = (q if i < 2 else k)[:, i % 2, :]
                by = 1.0 if i < 2 else scale
                dve.wait_ge(sems["rot_mm"], i + 1)
                own(dve.scalar_tensor_tensor(out=b["tmp"][:, i, :], in0=banks[i][:, :], scalar=by, in1=table("ret_sin", T),
                                             op0=ALU.mult, op1=ALU.mult))
                own(dve.scalar_tensor_tensor(out=src, in0=src, scalar=by, in1=table("ret_cos", T), op0=ALU.mult, op1=ALU.mult))
                own.settle()
                own(dve.tensor_tensor(src, src, b["tmp"][:, i, :], ALU.add))
                own.tell(sems["rotated"])
            own(dve.tensor_tensor(b["qdec"][:, :, :], q, wide(table("ret_qdec", 1024), 2), ALU.mult))
            kdec = table("ret_kdec", 4).rearrange("p (h o) -> p h o", o=1).to_broadcast([P, 4, 64])
            for c in range(NCH):
                dve.wait_ge(sems["k_mm"], c + 1)
                dve.tensor_tensor(wide(block_of("kt", c), 4), wide(banks[6 + c % 2][:, 0:256], 4), kdec, ALU.mult)\
                    .then_inc(sems["k_out"], 1)
                for h in range(2):
                    dve.wait_ge(sems["score_mm"], 2 * c + h + 1)
                    dve.tensor_tensor(wide(block_of("scores", c), 4)[:, h::2, :], wide(banks[4 * (c % 2) + h][:, 0:256], 2),
                                      wide(table("ret_decay", 512), 4)[:, h::2, :], ALU.mult).then_inc(sems["score_out"], 1)
            own(dve.memset(b["states"][:, 0, :], 0.0))
            own.tell(sems["state_ready"])
            for c in range(NCH - 1):
                dve.wait_ge(sems["kv_mm"], c + 1)
                for m in range(2):
                    cd = CONST1["ret_chunk"] + m
                    own(dve.scalar_tensor_tensor(out=b["states"][:, c + 1, m * P:(m + 1) * P],
                                                 in0=b["states"][:, c, m * P:(m + 1) * P], scalar=con[:, cd:cd + 1],
                                                 in1=banks[2][:, m * P:(m + 1) * P], op0=ALU.mult, op1=ALU.add))
                own.tell(sems["state_ready"])
            dve.wait_ge(sems["y_out"], 2 * NCH)
            for h in range(4):
                dve.tensor_tensor(b["tmp"][:, h, :], y[:, h, :], y[:, h, :], ALU.mult).then_inc(sems["squared"], 1)
            dve.wait_ge(sems["rooted"], 4)
            own(dve.reciprocal(b["root"][:, :, :], b["root"][:, :, :]))
            own.settle()
            own(dve.tensor_tensor(y[:, :, :], y[:, :, :], b["root"][:, :, :], ALU.mult))
            own.settle()
            dve.wait_ge(sems["gated"], 1)
            own(dve.tensor_tensor(y[:, :, :], y[:, :, :], g, ALU.mult))
            own.settle()


def spatial_gate(nc, core, b, y):
    con, par, small, banks, ident = core.con, core.par, core.small, core.banks, core.ident
    u, v = b["p_rs"][:, 12:16, :], b["p_rs"][:, 16:20, :]
    squares, root, ws, vt = b["tmp"], b["root"], b["ws"], b["vt"]
    with phase(nc, "activated", "mean_mm", "squared", "var_mm", "rooted", "normed", "t_mm", "t_out", "masked", "mix_mm",
               "own", "own_act") as (block, sems):
        @block.scalar
        def _(act):
            act.activation(v, v, ACT.Gelu).then_inc(sems["activated"], 1)
            act.activation(u, u, ACT.Gelu).then_inc(sems["activated"], 1)
            act.wait_ge(sems["var_mm"], 1)
            act.activation(root[:, 0, :], banks[1][:, :], ACT.Sqrt, bias=core.eps[:, 0:1], scale=1.0 / 512)\
                .then_inc(sems["rooted"], 1)
            for c in range(NCH):
                act.wait_ge(sems["t_mm"], c + 1)
                act.copy(vt[:, c, :], banks[2 + c % 2][:, :]).then_inc(sems["t_out"], 1)

        @block.vector
        def _(dve):
            own = Own(dve, sems["own"])
            w = small[:, SMALL1["w_sT"]:SMALL1["w_sT"] + 512]
            causal = con[:, CONST1["incl_su"]:CONST1["incl_su"] + P].rearrange("p (o t) -> p o t", o=1).to_broadcast([P, 4, P])
            own(dve.tensor_tensor(wide(ws[:, :], 4), wide(w, 4), causal, ALU.mult))
            own.tell(sems["masked"])
            dve.wait_ge(sems["mean_mm"], 1)
            for m in range(4):
                own(dve.scalar_tensor_tensor(out=v[:, m, :], in0=banks[0][:, :], scalar=-1.0 / 512, in1=v[:, m, :],
                                             op0=ALU.mult, op1=ALU.add))
            own.settle()
            for m in range(4):
                dve.tensor_tensor(squares[:, m, :], v[:, m, :], v[:, m, :], ALU.mult).then_inc(sems["squared"], 1)
            dve.wait_ge(sems["rooted"], 1)
            own(dve.reciprocal(root[:, 0, :], root[:, 0, :]))
            own.settle()
            for m in range(4):
                g = PAR1["ln_g"] + m
                own(dve.scalar_tensor_tensor(out=v[:, m, :], in0=v[:, m, :], scalar=par[:, g:g + 1], in1=root[:, 0, :],
                                             op0=ALU.mult, op1=ALU.mult))
            own.settle()
            for m in range(4):
                beta = PAR1["ln_b"] + m
                own(dve.tensor_scalar(v[:, m, :], v[:, m, :], par[:, beta:beta + 1], None, ALU.add))
            own.tell(sems["normed"])
            dve.wait_ge(sems["activated"], 2)
            for g in range(4):
                dve.wait_ge(sems["mix_mm"], g + 1)
                own(dve.tensor_tensor(y[:, g, :], u[:, g, :], banks[4 + g][:, :], ALU.mult))
            own.settle()

        @block.tensor
        def _(pe):
            pe.wait_ge(sems["activated"], 1)
            for m in range(4):
                mm = pe.matmul(banks[0][:, :], core.ones[:, :], v[:, m, :], start=(m == 0), stop=(m == 3))
            mm.then_inc(sems["mean_mm"], 1)
            for m in range(4):
                pe.wait_ge(sems["squared"], m + 1)
                mm = pe.matmul(banks[1][:, :], core.ones[:, :], squares[:, m, :], start=(m == 0), stop=(m == 3))
            mm.then_inc(sems["var_mm"], 1)
            pe.wait_ge(sems["normed"], 1)
            for c in range(NCH):
                if c >= 2:
                    pe.wait_ge(sems["t_out"], c - 1)
                for m in range(4):
                    mm = pe.transpose(banks[2 + c % 2][:, m * P:(m + 1) * P], v[:, m, c * CH:(c + 1) * CH], ident)
                mm.then_inc(sems["t_mm"], 1)
            pe.wait_ge(sems["t_out"], NCH)
            pe.wait_ge(sems["masked"], 1)
            for g in range(4):
                at = SMALL1["sg_b"] + g * P
                bias = small[0:1, at:at + P].rearrange("p (o i) -> p o i", o=1).to_broadcast([1, NCH, P])
                pe.matmul(wide(banks[4 + g][:, :], 4), core.ones[0:1, :], bias, start=True, stop=False)
                for c in range(NCH):
                    mm = pe.matmul(banks[4 + g][:, c * CH:(c + 1) * CH], vt[:, c, g * P:(g + 1) * P],
                                   ws[:, g * P:(g + 1) * P], start=False, stop=(c == NCH - 1))
                mm.then_inc(sems["mix_mm"], 1)


def merge(nc, core, layer, units, ys, blocks, merged, gate, part):
    n_br = len(ys)
    banks = core.banks
    with phase(nc, *LANDED, "landed4", "projected", "gated", "taken", "merged", "own") as (block, sems):
        names = LANDED + ["landed4"]

        @block.sync
        def _(sp):
            def load(n, s):
                sp.dma_start(slot(core, s, (KD + blocks) * P), units[layer * (KD * n_br) + n]).then_inc(sems[names[s]], 16)

            for s in range(n_br):
                load(s, s)
            with sp.Fori(1, KD) as d:
                for s in range(n_br):
                    sp.wait_ge(sems["projected"], (d - 1) * n_br + (s + 1))
                    load(d * n_br + s, s)

        @block.tensor
        def _(pe):
            def unit(s, landed, taken):
                pe.wait_ge(sems[names[s]], landed)
                if taken is not None:
                    pe.wait_ge(sems["taken"], taken)
                w = slot(core, s, (KD + blocks) * P)
                for k in range(KD):
                    pe.matmul(banks[s % 4][:, :], w[:, k * P:(k + 1) * P], core.h[:, k, :], start=(k == 0), stop=(k == KD - 1))
                for k in range(blocks):
                    mm = pe.matmul(banks[4 + s % 4][:, :], w[:, (KD + k) * P:(KD + k + 1) * P], ys[s][:, k, :],
                                   start=(k == 0), stop=(k == blocks - 1))
                mm.then_inc(sems["projected"], 1)

            for s in range(n_br):
                unit(s, 16, s - 3 if s >= 4 else None)
            with pe.Fori(1, KD) as d:
                for s in range(n_br):
                    before = s - 3 if s >= 4 else min(s + 4, s + 4 * ((n_br - 1 - s) // 4)) + 1 - n_br
                    unit(s, d * 16 + 16, d * n_br + before)

        @block.scalar
        def _(act):
            with act.Fori(0, KD) as d:
                for s in range(n_br):
                    act.wait_ge(sems["projected"], d * n_br + (s + 1))
                    act.activation(gate[:, s, :], banks[s % 4][:, :], ACT.Sigmoid).then_inc(sems["gated"], 1)

        @block.vector
        def _(dve):
            with dve.Fori(0, KD) as d:
                for s in range(n_br):
                    dve.wait_ge(sems["gated"], d * n_br + (s + 1))
                    to = merged[:, d, :] if s == 0 else part[:, s, :]
                    dve.tensor_tensor(to, gate[:, s, :], banks[4 + s % 4][:, :], ALU.mult).then_inc(sems["taken"], 1)
                    if s:
                        dve.wait_ge(sems["taken"], d * n_br + (s + 1))
                        if s > 1:
                            dve.wait_ge(sems["own"], d * (n_br - 1) + (s - 1))
                        dve.tensor_tensor(merged[:, d, :], merged[:, d, :], part[:, s, :], ALU.add).then_inc(sems["own"], 1)
                dve.wait_ge(sems["own"], d * (n_br - 1) + (n_br - 1))


def add_projection(nc, core, layer, units, src, blocks, parts):
    x, banks = core.x, core.banks
    count = KD * parts
    with phase(nc, *LANDED, "projected", "added") as (block, sems):
        @block.sync
        def _(sp):
            stream(sp, sems, core, lambda n: units[layer * count + n], count, blocks)

        @block.tensor
        def _(pe):
            def unit(s, d, landed, added):
                pe.wait_ge(sems[LANDED[s]], landed)
                if added is not None:
                    pe.wait_ge(sems["added"], added)
                w, half = slot(core, s, blocks * P), s % parts
                for k in range(blocks):
                    mm = pe.matmul(banks[d % 4][:, :], w[:, k * P:(k + 1) * P], src[:, half * blocks + k, :],
                                   start=(half == 0 and k == 0), stop=(half == parts - 1 and k == blocks - 1))
                mm.then_inc(sems["projected"], 1)

            for n in range(count):
                unit(n % RING, n // parts, 16 * (n // RING + 1), n // parts - 3 if n // parts >= 4 else None)

        @block.vector
        def _(dve):
            for d in range(KD):
                dve.wait_ge(sems["projected"], parts * (d + 1))
                dve.tensor_tensor(x[:, d, :], x[:, d, :], banks[d % 4][:, :], ALU.add).then_inc(sems["added"], 1)
            dve.wait_ge(sems["added"], KD)


def ffn_up(nc, core, layer, units, conv, f):
    par, banks = core.par, core.banks
    count = 2 * FFN_TILES
    with phase(nc, *LANDED, "projected", "evacuated", "squared", "summed", "rooted", "normed", "tapped", "silu", "own",
               "product") as (block, sems):
        @block.sync
        def _(sp):
            stream(sp, sems, core, lambda n: units[layer * count + n], count)

        @block.tensor
        def _(pe):
            norm_sum(pe, sems, core.ones[:, :], core.h, banks[7][:, :])
            pe.wait_ge(sems["normed"], KD)
            project(pe, sems, core, lambda k: core.h[:, k, :], count)

        def tap(j, n):
            at = PAR1["conv"] + j * count + n
            return par[:, at:at + 1]

        @block.scalar
        def _(act):
            norm_squares(act, sems, core.x, core.h)
            norm_root(act, sems, banks[7][:, :], core.root[:, :], core.eps[:, 0:1])

            def silu(j):
                act.wait_ge(sems["evacuated"], 2 * j + 1)
                act.activation(conv[:, 2 * j % 4, :], conv[:, 2 * j % 4, :], ACT.Silu).then_inc(sems["silu"], 1)

            for n in range(count):
                j = n // 2
                act.wait_ge(sems["projected"], n + 1)
                if n >= 4:
                    act.wait_ge(sems["product"], j - 1)
                at = PAR1["conv_b"] + n
                act.activation(conv[:, n % 4, :], banks[n % 4][:, :], ACT.Identity, bias=par[:, at:at + 1], scale=tap(2, n))\
                    .then_inc(sems["tapped"], 1)
                if n % 2 and j:
                    silu(j - 1)
            silu(FFN_TILES - 1)

        @block.vector
        def _(dve):
            own = Own(dve, sems["own"])
            norm_scale(dve, sems, own, core.x, core.root[:, :], par[:, PAR1["norm2"]:PAR1["norm2"] + 8], core.h)

            def product(j):
                dve.wait_ge(sems["silu"], j + 1)
                dve.tensor_tensor(f[:, j, :], conv[:, 2 * j % 4, :], conv[:, (2 * j + 1) % 4, :], ALU.mult)\
                    .then_inc(sems["product"], 1)

            for n in range(count):
                bank, c = banks[n % 4], conv[:, n % 4, :]
                dve.wait_ge(sems["tapped"], n + 1)
                own(dve.scalar_tensor_tensor(out=c[:, 1:], in0=bank[:, 0:T - 1], scalar=tap(1, n), in1=c[:, 1:],
                                             op0=ALU.mult, op1=ALU.add))
                own.settle()
                dve.scalar_tensor_tensor(out=c[:, 2:], in0=bank[:, 0:T - 2], scalar=tap(0, n), in1=c[:, 2:],
                                         op0=ALU.mult, op1=ALU.add).then_inc(sems["evacuated"], 1)
                if n % 2 and n > 1:
                    product(n // 2 - 1)
            dve.wait_ge(sems["evacuated"], count)
            product(FFN_TILES - 1)
            dve.wait_ge(sems["product"], FFN_TILES)


def final_norm(nc, core, gain, out):
    with phase(nc, "squared", "summed", "rooted", "normed", "own") as (block, sems):
        @block.tensor
        def _(pe):
            norm_sum(pe, sems, core.ones[:, :], core.h, core.banks[7][:, :])

        @block.scalar
        def _(act):
            norm_squares(act, sems, core.x, core.h)
            norm_root(act, sems, core.banks[7][:, :], core.root[:, :], core.eps[:, 0:1])

        @block.vector
        def _(dve):
            norm_scale(dve, sems, Own(dve, sems["own"]), core.x, core.root[:, :], gain, out)
            dve.wait_ge(sems["normed"], KD)


def block1_layer(nc, core, layer, w):
    with ExitStack() as outer:
        def buf(stack, name, shape):
            return stack.enter_context(nc.sbuf_tensor(name, [P] + shape, F32))

        y = buf(outer, "y1", [12, T])
        with ExitStack() as stack:
            b = {"p_rw": buf(stack, "p_rw", [RW_TILES, T + 1])}
            for name in "ACDF":
                b[name] = buf(stack, f"rw_{name}", [4, T])
            with ExitStack() as scratch:
                for name in "BEGH":
                    b[name] = buf(scratch, f"rw_{name}", [4, T])
                project_in1(nc, core, layer, w, 0, RW_TILES, lambda n: b["p_rw"][:, n, 1:], True)
                rwkv_prepare(nc, core, b)
            with ExitStack() as scratch:
                b["state"] = buf(scratch, "rw_state", [4, 64])
                for name in ("Vt", "Kt", "Bt", "mix", "U"):
                    b[name] = buf(scratch, f"rw_{name}_", [T])
                b["work"] = [{name: buf(scratch, f"{name}{h}", [4, P])
                              for name in ("negNT", "inv", "invT", "levelT", "X")} for h in range(2)]
                for h in range(2):
                    for i, name in enumerate(("PmT", "QbT", "QkT")):
                        at = (3 * h + i) * T
                        b["work"][h][name] = wide(core.ring[:, at:at + T], 4)
                rwkv_scan(nc, core, b, y[:, 0:4, :])
            with ExitStack() as scratch:
                for name in "BEG":
                    b[name] = buf(scratch, f"rwf_{name}", [4, T])
                rwkv_finish(nc, core, b, y[:, 0:4, :])
        with ExitStack() as stack:
            b = {"p_rs": buf(stack, "p_rs", [RET_TILES + SG_TILES, T])}
            project_in1(nc, core, layer, w, RW_TILES, RET_TILES + SG_TILES, lambda n: b["p_rs"][:, n, :], False)
            b["tmp"] = buf(stack, "rs_tmp", [4, T])
            b["root"] = buf(stack, "rs_root", [4, T])
            b["vt"] = buf(stack, "rs_vt", [NCH, T])
            b["ws"] = buf(stack, "rs_ws", [T])
            with ExitStack() as scratch:
                b["kt"] = buf(scratch, "ret_kt", [NCH, 256])
                b["scores"] = buf(scratch, "ret_scores", [NCH, T])
                b["states"] = buf(scratch, "ret_states", [NCH, 256])
                b["qdec"] = buf(scratch, "ret_q", [2, T])
                retention(nc, core, b, y[:, 4:8, :])
            spatial_gate(nc, core, b, y[:, 8:12, :])
        with ExitStack() as stack:
            merged = buf(stack, "merged1", [KD, T])
            gate, part = buf(stack, "gate1", [3, T]), buf(stack, "part1", [3, T])
            merge(nc, core, layer, w["merge1"], [y[:, 4 * i:4 * i + 4, :] for i in range(3)], 4, merged, gate, part)
            add_projection(nc, core, layer, w["out1"], merged, KD, 1)
    with ExitStack() as stack:
        f = stack.enter_context(nc.sbuf_tensor("ffn", [P, FFN_TILES, T], F32))
        conv = stack.enter_context(nc.sbuf_tensor("conv", [P, 4, T], F32))
        ffn_up(nc, core, layer, w["up1"], conv, f)
        add_projection(nc, core, layer, w["down1"], f, 11, 2)


def by_tiles(w, rows):
    L, _, n = w.shape
    return w.reshape(L, rows, P, n // P, P).transpose(0, 3, 2, 1, 4)


def vectors(v):
    return v.reshape(v.shape[0], -1, P).transpose(0, 2, 1)


def layout1(i):
    w_in = i["w_in"]
    n_in = IN1_TILES * P
    a = {}
    a["in1"] = by_tiles(w_in[:, :, :n_in], KD).reshape(-1, P, KD * P)
    gates = by_tiles(w_in[:, :, n_in:], KD).reshape(DEPTH, 3, KD, P, KD, P)
    wb = i["w_branch"]
    branch = np.stack([by_tiles(wb[:, n], 4) for n in range(3)], 1)
    a["merge1"] = np.concatenate([gates, branch], 4).transpose(0, 2, 1, 3, 4, 5).reshape(-1, P, 12 * P)
    a["out1"] = by_tiles(i["w_out"], KD).reshape(-1, P, KD * P)
    up = by_tiles(i["ffn_w_up"], KD).reshape(DEPTH, 2, FFN_TILES, P, KD * P).transpose(0, 2, 1, 3, 4)
    a["up1"] = up.reshape(-1, P, KD * P)
    down = by_tiles(i["ffn_w_down"], FFN_TILES).reshape(DEPTH, KD, P, 2, 11 * P).transpose(0, 1, 3, 2, 4)
    a["down1"] = down.reshape(-1, P, 11 * P)

    def interleave(v):
        return v.reshape(DEPTH, P, 2, FFN_TILES).transpose(0, 1, 3, 2).reshape(DEPTH, P, 2 * FFN_TILES)

    cols = [vectors(i["norm1_g"]), vectors(i["rw_mu"])]
    cols += [vectors(i[n]) for n in ("rw_w0", "rw_a0", "rw_k_k", "rw_k_a")]
    cols += [vectors(i[n].reshape(DEPTH, -1)) for n in ("rw_r_k", "rw_lnx_g", "rw_lnx_b")]
    cols += [vectors(i["sg_ln_g"]), vectors(i["sg_ln_b"]), vectors(i["norm2_g"])]
    cols += [interleave(vectors(i["ffn_conv_w"][:, j])) for j in range(3)] + [interleave(vectors(i["ffn_conv_b"]))]
    a["par1"] = np.concatenate(cols, 2)
    lora = np.concatenate([i["rw_w_up"], i["rw_a_up"]], 1)
    w_sT = i["sg_w_s"].transpose(0, 3, 1, 2).reshape(DEPTH, P, 512)
    sg_b = np.broadcast_to(i["sg_b"].reshape(DEPTH, 1, 512), (DEPTH, P, 512))
    a["small1"] = np.concatenate([lora, i["rw_g_up"], w_sT, sg_b], 2)
    return a


TILES2 = {name: i for i, name in enumerate((
    "dsa_q", "dsa_q1", "ckv", "idx_q", "idx_k", "dsa_z", "dsa_z1", "fox_q", "fox_q1", "fox_k", "fox_k1", "fox_z", "fox_z1",
    "sb_q", "sb_q1", "sb_k", "sb_k1", "sb_z", "sb_z1", "nsa_q", "nsa_q1", "kc_vc", "ks", "kw", "nsa_z", "nsa_z1",
    "mem_q", "mem_q1", "mem_z", "mem_z1"))}
IN2_TILES = len(TILES2)
N_BR2 = 5
NH = 4
TM_V, TM_S = 512, 148
VS, VW, IDX_W, NSA_G, FOX_F = 0, 64, 128, 132, 144
N_MEM = 256
CMP_LEN, CMP_STRIDE = 32, 16
N_CMP = (T - CMP_LEN) // CMP_STRIDE + 1
SELECTED = min(256, T // 4)
IDX_SCALE = (32 ** -0.5) * (4 ** -0.5)
TAKEN = -3e38
SCALE = 64 ** -0.5

PAR2, NPAR2 = offsets([("norm", 8), ("kv_norm", 1), ("fox_b", 4), ("mem_norm", 8)])
SMALL2, NSMALL2 = offsets([("w_uk", 256), ("w_uv", 256), ("pe", 32), ("w2_k", 128), ("w2_v", 64)])
CONST2, NCONST2 = offsets([("ident", 128), ("rot64", 128), ("rot32", 128), ("causal", 896), ("after", 896), ("cmp", 128),
                           ("suffix", 128), ("strict01", 128), ("strict_neg", 128), ("sel", 512), ("inv", 2)])


def constants2():
    c = np.zeros((P, NCONST2), np.float32)

    def put(name, a):
        a = np.asarray(a, np.float32).reshape(P, -1)
        c[:, CONST2[name]:CONST2[name] + a.shape[1]] = a

    i, j = np.arange(P)[:, None], np.arange(P)[None, :]
    at = np.arange(896)[None, :] - 384
    put("ident", i == j)
    put("rot64", rotation(64))
    put("rot32", rotation(32))
    put("causal", np.where(at <= i, 0.0, NEG))
    put("after", at >= i)
    ends = np.arange(32) * CMP_STRIDE + CMP_LEN - 1
    tok = np.arange(4)[None, :, None] * P + i[:, :, None]
    put("cmp", np.where(ends[None, None, :] <= tok, 0.0, NEG))
    put("suffix", i >= j)
    put("strict01", i < j)
    put("strict_neg", np.where(i < j, 0.0, NEG))
    sel = np.zeros((P, 4, P), np.float32)
    for h in range(4):
        sel[h, h] = 1.0
    put("sel", sel)
    inv = np.stack([10000.0 ** (-np.float32(2.0) * (np.arange(P) % (w // 2)).astype(np.float32) / np.float32(w))
                    for w in (64, 32)], 1)
    put("inv", inv)
    return c


def rope_tables(nc, core, con, tables, positions):
    turn = 2 * np.pi
    high = 6.28125
    middle = float(np.float32(int((turn - high) * 2 ** 22) / 2 ** 22))
    low = turn - high - middle
    with phase(nc, "loaded", "reduced", "own") as (block, sems), \
            nc.sbuf_tensor("pos_i", [P, T], I32) as whole, nc.sbuf_tensor("angles", [P, 4, T], F32) as angle, \
            nc.sbuf_tensor("turns", [P, T], F32) as turns:
        @block.sync
        def _(sp):
            sp.dma_start(whole[:, :], positions.to_broadcast([P, T])).then_inc(sems["loaded"], 16)

        @block.vector
        def _(dve):
            own = Own(dve, sems["own"])
            dve.wait_ge(sems["loaded"], 16)
            own(dve.tensor_copy(turns[:, :], whole[:, :]))
            own.settle()
            for n in range(4):
                inv = con[:, CONST2["inv"] + n // 2:CONST2["inv"] + n // 2 + 1]
                own(dve.tensor_scalar(angle[:, n, :], turns[:, :], inv, None, ALU.mult))
            own.settle()
            for n in range(4):
                a = angle[:, n, :]
                quarter = 0.25 if n % 2 == 0 else 0.0
                own(dve.tensor_scalar(turns[:, :], a, float(1 / turn), quarter, ALU.mult, ALU.add))
                own.settle()
                own(dve.tensor_copy(whole[:, :], turns[:, :]))
                own.settle()
                own(dve.tensor_copy(turns[:, :], whole[:, :]))
                own.settle()
                for part in (high, middle, low):
                    own(dve.scalar_tensor_tensor(out=a, in0=turns[:, :], scalar=-part, in1=a, op0=ALU.mult, op1=ALU.add))
                    own.settle()
                if quarter:
                    own(dve.tensor_scalar(a, a, float(np.pi / 2), None, ALU.add))
                    own.settle()
                for test, by in ((ALU.is_gt, -1.0), (ALU.is_lt, 1.0)):
                    own(dve.tensor_scalar(turns[:, :], a, -by * float(np.pi), by * turn, test, ALU.mult))
                    own.settle()
                    own(dve.tensor_tensor(a, a, turns[:, :], ALU.add))
                    own.settle()
                own(dve.tensor_scalar(a, a, 3.1415925, -3.1415925, ALU.min, ALU.max))
                own.settle()
            own.tell(sems["reduced"])

        @block.scalar
        def _(act):
            act.wait_ge(sems["reduced"], 1)
            act.activation(tables[:, :, :], angle[:, :, :], ACT.Sin)


def project_in2(nc, core, layer, w, p):
    with phase(nc, *LANDED, "projected", "evacuated", "squared", "summed", "rooted", "normed", "params", "own") as (block, sems):
        @block.sync
        def _(sp):
            stream(sp, sems, core, lambda n: w["in2"][layer * IN2_TILES + n], IN2_TILES)

        @block.scalar
        def _(act):
            act.dma_start(core.par[:, 0:NPAR2], w["par2"][layer]).then_inc(sems["params"], 16)
            act.dma_start(core.small[:, 0:NSMALL2], w["small2"][layer]).then_inc(sems["params"], 16)
            norm_squares(act, sems, core.x, core.h)
            norm_root(act, sems, core.banks[7][:, :], core.root[:, :], core.eps[:, 0:1])
            evacuate(act, sems, core.banks, lambda n: p[:, n, :], IN2_TILES)
            act.wait_ge(sems["params"], 32)

        @block.tensor
        def _(pe):
            norm_sum(pe, sems, core.ones[:, :], core.h, core.banks[7][:, :])
            pe.wait_ge(sems["normed"], KD)
            project(pe, sems, core, lambda k: core.h[:, k, :], IN2_TILES)

        @block.vector
        def _(dve):
            dve.wait_ge(sems["params"], 32)
            norm_scale(dve, sems, Own(dve, sems["own"]), core.x, core.root[:, :],
                       core.par[:, PAR2["norm"]:PAR2["norm"] + 8], core.h)


def token_major(nc, core, layer, w, b):
    banks, par = core.banks, core.par
    ring, mem, memh = core.ring, b["mem"], b["memh"]
    wv = ring[:, 0:KD * TM_V].rearrange("p (k n) -> p k n", k=KD)
    ws = ring[:, KD * TM_V:KD * (TM_V + TM_S)].rearrange("p (k n) -> p k n", k=KD)
    wm = b["wm"]
    with phase(nc, "w_landed", "mem_landed", "v_mm", "v_out", "s_mm", "s_out", "squared", "summed", "rooted", "normed",
               "mk_mm", "mv_mm", "own", "own_act") as (block, sems):
        @block.sync
        def _(sp):
            sp.dma_start(ring[:, 0:KD * (TM_V + TM_S)], w["tm2"][layer]).then_inc(sems["w_landed"], 16)
            sp.dma_start(mem[:, :, :], w["mem"]).then_inc(sems["mem_landed"], 16)
            sp.dma_start(wm[:, :], w["wm2"][layer]).then_inc(sems["mem_landed"], 16)

        @block.tensor
        def _(pe):
            pe.wait_ge(sems["w_landed"], 16)
            for i in range(4):
                if i >= 2:
                    pe.wait_ge(sems["v_out"], i - 1)
                    pe.wait_ge(sems["s_out"], i - 1)
                for k in range(KD):
                    mm = pe.matmul(banks[i % 2][:, :], core.h[:, k, i * P:(i + 1) * P], wv[:, k, :], start=(k == 0),
                                   stop=(k == KD - 1))
                mm.then_inc(sems["v_mm"], 1)
                for k in range(KD):
                    mm = pe.matmul(banks[2 + i % 2][:, 0:TM_S], core.h[:, k, i * P:(i + 1) * P], ws[:, k, :], start=(k == 0),
                                   stop=(k == KD - 1))
                mm.then_inc(sems["s_mm"], 1)
            for k in range(KD):
                pe.wait_ge(sems["squared"], k + 1)
                mm = pe.matmul(banks[4][:, 0:N_MEM], core.ones[:, :], memh[:, k, :], start=(k == 0), stop=(k == KD - 1))
            mm.then_inc(sems["summed"], 1)
            pe.wait_ge(sems["normed"], KD)
            for m in range(2):
                for k in range(KD):
                    mm = pe.matmul(banks[5][:, m * 256:(m + 1) * 256], wm[:, (m * KD + k) * P:(m * KD + k + 1) * P],
                                   memh[:, k, :], start=(k == 0), stop=(k == KD - 1))
            mm.then_inc(sems["mk_mm"], 1)
            for m in range(2):
                for k in range(KD):
                    at = 2 * KD * P + k * 256
                    mm = pe.matmul(banks[6][:, m * 256:(m + 1) * 256], memh[:, k, m * P:(m + 1) * P], wm[:, at:at + 256],
                                   start=(k == 0), stop=(k == KD - 1))
            mm.then_inc(sems["mv_mm"], 1)

        @block.scalar
        def _(act):
            own = Own(act, sems["own_act"])
            act.wait_ge(sems["mem_landed"], 32)
            for k in range(KD):
                act.activation(memh[:, k, :], mem[:, k, :], ACT.Square).then_inc(sems["squared"], 1)
            for i in range(4):
                act.wait_ge(sems["v_mm"], i + 1)
                act.copy(b["tm_v"][:, i, :], banks[i % 2][:, :]).then_inc(sems["v_out"], 1)
                act.wait_ge(sems["s_mm"], i + 1)
                act.copy(b["tm_s"][:, i, :], banks[2 + i % 2][:, 0:TM_S]).then_inc(sems["s_out"], 1)
            act.wait_ge(sems["summed"], 1)
            act.activation(core.root[:, 0:N_MEM], banks[4][:, 0:N_MEM], ACT.Sqrt, bias=core.eps[:, 0:1], scale=1.0 / D)\
                .then_inc(sems["rooted"], 1)
            act.wait_ge(sems["mk_mm"], 1)
            own(act.copy(b["mem_k"][:, :, :], wide(banks[5][:, :], 2)))
            act.wait_ge(sems["mv_mm"], 1)
            own(act.copy(b["mem_v"][:, :, :], wide(banks[6][:, :], 2)))
            own.settle()

        @block.vector
        def _(dve):
            norm_scale(dve, sems, Own(dve, sems["own"]), mem, core.root[:, 0:N_MEM],
                       par[:, PAR2["mem_norm"]:PAR2["mem_norm"] + 8], memh)


def prepare2(nc, core, b, p):
    con, small, par, banks, tables = b["con"], core.small, core.par, core.banks, b["tables"]
    tl = TILES2

    def table(name, n):
        return con[:, CONST2[name]:CONST2[name] + n]

    rot64, rot32 = table("rot64", P), table("rot32", P)
    ckv, ka = p[:, tl["ckv"], :], b["dsa_k"]
    turning = [(p[:, tl[n], :], rot64, 0, P) for n in ("dsa_q", "dsa_q1", "nsa_q", "nsa_q1", "ks", "kw")]
    turning += [(p[:, tl[n], :], rot32, 2, P) for n in ("idx_q", "idx_k")]
    turning += [(p[:, tl["kc_vc"], :], rot64, 0, 64)]
    turning += [(ka[:, m, :], rot64, 0, P) for m in range(2)]
    n_turn = len(turning)
    f, fa, lf = b["tm_s"][:, :, FOX_F:FOX_F + 4], b["f_abs"], b["f_log"]
    w1 = core.ring
    with phase(nc, "w1_landed", "ckv_squared", "ckv_sum", "ckv_rooted", "ckv_normed", "ka_mm", "ka_out", "va_mm", "va_out",
               "rot_mm", "turned", "hid_mm", "bias_out", "hid_out", "cmp_mm", "f_biased", "f_exped", "f_logged", "cum_mm",
               "own", "own_act") as (block, sems):
        @block.sync
        def _(sp):
            sp.dma_start(w1[:, 0:CMP_LEN * P], b["w1_dram"]).then_inc(sems["w1_landed"], 16)

        @block.tensor
        def _(pe):
            pe.wait_ge(sems["ckv_squared"], 1)
            pe.matmul(banks[2][:, :], core.ones[:, :], b["squares"][:, :], start=True, stop=True).then_inc(sems["ckv_sum"], 1)
            for n, (x, rot, _, _) in enumerate(turning):
                if n == n_turn - 2:
                    pe.wait_ge(sems["ckv_normed"], 1)
                    for m in range(2):
                        at = SMALL2["w_uk"] + m * P
                        pe.matmul(banks[3 + m][:, :], small[:, at:at + P], ckv, start=True, stop=True)\
                            .then_inc(sems["ka_mm"], 1)
                    for i in range(4):
                        at = SMALL2["w_uv"]
                        mm = pe.matmul(banks[5 + i // 2][:, (i % 2) * 256:(i % 2) * 256 + 256], ckv[:, i * P:(i + 1) * P],
                                       small[:, at:at + 256], start=True, stop=True)
                    mm.then_inc(sems["va_mm"], 1)
                    pe.wait_ge(sems["ka_out"], 2)
                if n >= 2:
                    pe.wait_ge(sems["turned"], n - 1)
                pe.matmul(banks[n % 2][:, :], rot, x, start=True, stop=True).then_inc(sems["rot_mm"], 1)
            pe.wait_ge(sems["w1_landed"], 16)
            pe.wait_ge(sems["turned"], n_turn)
            pe.wait_ge(sems["ckv_rooted"], 1)
            pe.wait_ge(sems["va_out"], 1)
            kc_vc = p[:, tl["kc_vc"], :]
            for half in range(2):
                lo = 64 * half
                for j in range(CMP_LEN):
                    wj = w1[lo:lo + 64, j * P:(j + 1) * P]
                    pe.matmul(banks[2 * half][:, 0:N_CMP], wj, kc_vc[lo:lo + 64, j:j + CMP_STRIDE * (N_CMP - 1) + 1:CMP_STRIDE],
                              start=(j == 0), stop=(j == CMP_LEN - 1))
                    at = SMALL2["pe"] + j
                    mm = pe.matmul(banks[2 * half + 1][:, 0:1], wj, small[lo:lo + 64, at:at + 1], start=(j == 0),
                                   stop=(j == CMP_LEN - 1))
                mm.then_inc(sems["hid_mm"], 1)
            pe.wait_ge(sems["hid_out"], 2)
            pe.matmul(banks[4][:, 0:N_CMP], small[:, SMALL2["w2_k"]:SMALL2["w2_k"] + P], b["hidden"][:, 0, 0:N_CMP],
                      start=True, stop=True)
            pe.matmul(banks[4][0:N_CMP, 64:128], b["hidden"][:, 1, 0:N_CMP], small[:, SMALL2["w2_v"]:SMALL2["w2_v"] + 64],
                      start=True, stop=True).then_inc(sems["cmp_mm"], 1)
            pe.wait_ge(sems["f_logged"], 1)
            for j in range(4):
                at = CONST2["after"] + 384 - j * P
                mm = pe.matmul(banks[7][0:4, :], lf[:, j, :], con[:, at:at + T], start=(j == 0), stop=(j == 3))
            mm.then_inc(sems["cum_mm"], 1)

        @block.scalar
        def _(act):
            own = Own(act, sems["own_act"])
            act.activation(b["squares"][:, :], ckv, ACT.Square).then_inc(sems["ckv_squared"], 1)
            act.wait_ge(sems["ckv_sum"], 1)
            act.activation(core.root[:, :], banks[2][:, :], ACT.Sqrt, bias=core.eps[:, 0:1], scale=1.0 / P)\
                .then_inc(sems["ckv_rooted"], 1)
            for m in range(2):
                act.wait_ge(sems["ka_mm"], m + 1)
                act.copy(ka[:, m, :], banks[3 + m][:, :]).then_inc(sems["ka_out"], 1)
            act.wait_ge(sems["va_mm"], 1)
            for i in range(2):
                own(act.copy(b["dsa_v"][:, 2 * i:2 * i + 2, :], wide(banks[5 + i][:, :], 2)))
            own.tell(sems["va_out"])
            act.wait_ge(sems["f_biased"], 1)
            own(act.activation(fa[:, :, :], lf[:, :, :], ACT.Abs))
            own.settle()
            own(act.activation(fa[:, :, :], fa[:, :, :], ACT.Exp, scale=-1.0))
            own.settle()
            own(act.activation(fa[:, :, :], fa[:, :, :], ACT.Ln, bias=core.ones[:, 0:1]))
            own.tell(sems["f_exped"])
            own(act.activation(b["tm_s"][:, :, NSA_G:NSA_G + 12], b["tm_s"][:, :, NSA_G:NSA_G + 12], ACT.Sigmoid))
            for half in range(2):
                act.wait_ge(sems["bias_out"], half + 1)
                act.activation(b["hidden"][:, half, 0:N_CMP], banks[2 * half][:, 0:N_CMP], ACT.Silu,
                               bias=core.tiny[:, half:half + 1]).then_inc(sems["hid_out"], 1)
            for name in ("dsa_z", "fox_z", "sb_z", "nsa_z", "mem_z"):
                z = p[:, tl[name]:tl[name] + 2, :]
                own(act.activation(z, z, ACT.Silu))
            act.wait_ge(sems["cmp_mm"], 1)
            own(act.copy(b["cmp_k"][:, :], banks[4][:, 0:N_CMP]))
            own(act.copy(b["cmp_v"][:, :], banks[4][0:N_CMP, 64:128]))
            own.settle()

        @block.vector
        def _(dve):
            own = Own(dve, sems["own"])
            fb = par[:, PAR2["fox_b"]:PAR2["fox_b"] + 4].rearrange("p (o h) -> p o h", o=1).to_broadcast([P, 4, 4])
            own(dve.tensor_tensor(lf[:, :, :], f, fb, ALU.add))
            own.tell(sems["f_biased"])
            dve.wait_ge(sems["ckv_rooted"], 1)
            own(dve.reciprocal(core.root[:, :], core.root[:, :]))
            own.settle()
            own(dve.scalar_tensor_tensor(out=ckv, in0=ckv, scalar=par[:, PAR2["kv_norm"]:PAR2["kv_norm"] + 1],
                                         in1=core.root[:, :], op0=ALU.mult, op1=ALU.mult))
            own.tell(sems["ckv_normed"])
            for n, (x, _, at, rows) in enumerate(turning):
                if n == n_turn - 2:
                    dve.wait_ge(sems["ka_out"], 2)
                dve.wait_ge(sems["rot_mm"], n + 1)
                s = b["turn"][:, n % 2, :]
                own(dve.tensor_tensor(s[0:rows, :], banks[n % 2][0:rows, :], tables[0:rows, at + 1, :], ALU.mult))
                own(dve.tensor_tensor(x[0:rows, :], x[0:rows, :], tables[0:rows, at, :], ALU.mult))
                own.settle()
                own(dve.tensor_tensor(x[0:rows, :], x[0:rows, :], s[0:rows, :], ALU.add))
                own.tell(sems["turned"])
            dve.wait_ge(sems["f_exped"], 1)
            own(dve.scalar_tensor_tensor(out=lf[:, :, :], in0=lf[:, :, :], scalar=0.0, in1=fa[:, :, :], op0=ALU.min,
                                         op1=ALU.subtract))
            own.tell(sems["f_logged"])
            for half in range(2):
                dve.wait_ge(sems["hid_mm"], half + 1)
                dve.tensor_copy(core.tiny[:, half:half + 1], banks[2 * half + 1][:, 0:1]).then_inc(sems["bias_out"], 1)
            dve.wait_ge(sems["cum_mm"], 1)
            own(dve.tensor_scalar(b["cum"][0:4, 0, :], banks[7][0:4, :], 1.0 / SCALE, None, ALU.mult))
            own(dve.tensor_scalar(b["cum"][0:4, 1, :], banks[7][0:4, :], -1.0 / SCALE, None, ALU.mult))
            own.settle()


def select_keys(nc, core, b, p):
    con, banks, rel, score, bias = b["con"], core.banks, b["rel"], b["score"], b["bias"]
    qi, ki = p[:, TILES2["idx_q"], :], p[:, TILES2["idx_k"], :]

    def causal(i):
        at = CONST2["causal"] + 384 - i * P
        return con[:, at:at + (i + 1) * P]

    with phase(nc, "rel_mm", "rel_out", "weighted", "own", "ranked") as (block, sems):
        @block.tensor
        def _(pe):
            for i in range(1, 4):
                for h in range(4):
                    n = 4 * (i - 1) + h
                    if i > 1:
                        pe.wait_ge(sems["rel_out"], n - 3)
                    pe.matmul(banks[h][:, 0:(i + 1) * P], qi[32 * h:32 * h + 32, i * P:(i + 1) * P],
                              ki[32 * h:32 * h + 32, 0:(i + 1) * P], start=True, stop=True).then_inc(sems["rel_mm"], 1)

        @block.scalar
        def _(act):
            for i in range(1, 4):
                for h in range(4):
                    n = 4 * (i - 1) + h
                    act.wait_ge(sems["rel_mm"], n + 1)
                    if i > 1:
                        act.wait_ge(sems["weighted"], n - 3)
                    act.activation(rel[:, h, 0:(i + 1) * P], banks[h][:, 0:(i + 1) * P], ACT.Relu).then_inc(sems["rel_out"], 1)

        @block.vector
        def _(dve):
            own = Own(dve, sems["own"])
            own(dve.tensor_copy(bias[:, 0, 0:P], causal(0)))
            for i in range(1, 4):
                s = score[:, i, 0:(i + 1) * P]
                for h in range(4):
                    n = 4 * (i - 1) + h
                    dve.wait_ge(sems["rel_out"], n + 1)
                    wi = b["tm_s"][:, i, IDX_W + h:IDX_W + h + 1]
                    r = rel[:, h, 0:(i + 1) * P]
                    if h == 0:
                        dve.tensor_scalar(s, r, wi, None, ALU.mult).then_inc(sems["weighted"], 1)
                    else:
                        dve.wait_ge(sems["weighted"], n)
                        dve.scalar_tensor_tensor(out=s, in0=r, scalar=wi, in1=s, op0=ALU.mult, op1=ALU.add)\
                            .then_inc(sems["weighted"], 1)
                dve.wait_ge(sems["weighted"], 4 * i)
                own(dve.scalar_tensor_tensor(out=s, in0=s, scalar=IDX_SCALE, in1=causal(i), op0=ALU.mult, op1=ALU.add))
            own.settle()
            for r in range(SELECTED // 8):
                for i in range(1, 4):
                    dve.max(b["top"][:, i, :], score[:, i, 0:(i + 1) * P]).then_inc(sems["ranked"], 1)
                for i in range(1, 4):
                    dve.wait_ge(sems["ranked"], r * 6 + i)
                    s = score[:, i, 0:(i + 1) * P]
                    dve.match_replace(s, b["top"][:, i, :], s, TAKEN).then_inc(sems["ranked"], 1)
                dve.wait_ge(sems["ranked"], r * 6 + 6)
            for i in range(1, 4):
                own(dve.tensor_scalar(bias[:, i, 0:(i + 1) * P], score[:, i, 0:(i + 1) * P], TAKEN / 2, NEG, ALU.is_gt, ALU.mult))
            own.settle()


def attention(nc, core, b, parts):
    banks, ident = core.banks, core.ident2
    stats, probs, turned = b["stats"], b["probs"], b["probsT"]
    n_parts = len(parts)
    ev = {0: [], 1: []}
    for n, part in enumerate(parts):
        for j in range(len(part["blocks"])):
            ev[j % 2].append((n, j))
    count = {nj: (side, c + 1) for side, l in ev.items() for c, nj in enumerate(l)}
    outs = [n for n in range(n_parts) if parts[n]["last"]]

    with phase(nc, "logit_mm", "masked", "exped", "ready", "t_mm0", "t_mm1", "t_out0", "t_out1", "pv_mm", "y_out", "own") as (block, sems):
        @block.tensor
        def _(pe):
            def logits(n):
                part = parts[n]
                for i in range(4):
                    if n:
                        pe.wait_ge(sems["masked"], 4 * (n - 1) + i + 1)
                    width = part["keys"](i)
                    extra = part["extra"]
                    mm = pe.matmul(banks[i][:, 0:width], part["q"][:, i * P:(i + 1) * P], part["k"][:, 0:width],
                                   start=True, stop=extra is None)
                    if extra is not None:
                        mm = extra(pe, banks[i], i)
                    mm.then_inc(sems["logit_mm"], 1)

            def values(n):
                part = parts[n]
                pe.wait_ge(sems["ready"], n + 1)
                for j, (rows, first) in enumerate(part["blocks"]):
                    side, c = count[n, j]
                    if c > 1:
                        pe.wait_ge(sems[f"t_out{side}"], c - 1)
                    for i in range(first, 4):
                        mm = pe.transpose(banks[4 + side][0:rows, i * P:(i + 1) * P],
                                          probs[:, n % 2, i, j * P:j * P + rows], ident)
                    mm.then_inc(sems[f"t_mm{side}"], 1)
                done = sum(m < n for m in outs)
                if part["first"] and done >= 2:
                    pe.wait_ge(sems["y_out"], done - 1)
                lo = part["lo"]
                out = banks[6 + done % 2][lo:lo + 64, :]
                last = len(part["blocks"]) - 1
                for j, (rows, first) in enumerate(part["blocks"]):
                    side, c = count[n, j]
                    pe.wait_ge(sems[f"t_out{side}"], c)
                    mm = pe.matmul(out[:, first * P:], part["values"](j), turned[0:rows, n % 2, j, first * P:],
                                   start=(part["first"] and j == 0), stop=(part["last"] and j == last))
                mm.then_inc(sems["pv_mm"], 1)

            logits(0)
            for n in range(n_parts):
                if n + 1 < n_parts:
                    logits(n + 1)
                values(n)

        @block.scalar
        def _(act):
            def exps(n):
                for i in range(4):
                    act.wait_ge(sems["masked"], 4 * n + i + 1)
                    l = probs[:, n % 2, i, 0:parts[n]["keys"](i)]
                    act.activation(l, l, ACT.Exp, scale=SCALE, bias=stats[:, n % 2, 4 + i:5 + i],
                                   accum_out=stats[:, n % 2, 8 + i:9 + i]).then_inc(sems["exped"], 1)

            def evacuate_even(n):
                for j in range(0, len(parts[n]["blocks"]), 2):
                    rows, first = parts[n]["blocks"][j]
                    act.wait_ge(sems["t_mm0"], count[n, j][1])
                    act.copy(turned[0:rows, n % 2, j, first * P:], banks[4][0:rows, first * P:]).then_inc(sems["t_out0"], 1)

            exps(0)
            for n in range(n_parts):
                if n + 1 < n_parts:
                    exps(n + 1)
                evacuate_even(n)

        @block.vector
        def _(dve):
            own = Own(dve, sems["own"])

            def mask(n):
                part = parts[n]
                if n >= 2:
                    dve.wait_ge(sems["pv_mm"], n - 1)
                for i in range(4):
                    dve.wait_ge(sems["logit_mm"], 4 * n + i + 1)
                    width = part["keys"](i)
                    own(dve.tensor_tensor_reduce(out=probs[:, n % 2, i, 0:width], in0=banks[i][:, 0:width],
                                                 in1=part["mask"](i), scale=1.0, scalar=NEG * 1e-5, op0=ALU.add, op1=ALU.max,
                                                 accum_out=stats[:, n % 2, i:i + 1]))
                    own.settle()
                    dve.tensor_scalar(stats[:, n % 2, 4 + i:5 + i], stats[:, n % 2, i:i + 1], -SCALE, None, ALU.mult)\
                        .then_inc(sems["masked"], 1)

            def normalise(n):
                part = parts[n]
                dve.wait_ge(sems["exped"], 4 * n + 4)
                s = stats[:, n % 2, 8:12]
                own(dve.tensor_scalar(s, s, 1e-30, None, ALU.max))
                own.settle()
                own(dve.reciprocal(s, s))
                own.settle()
                if part["row"] is not None:
                    own(dve.tensor_tensor(s, s, part["row"], ALU.mult))
                    own.settle()
                for i in range(4):
                    l = probs[:, n % 2, i, 0:part["keys"](i)]
                    own(dve.tensor_scalar(l, l, stats[:, n % 2, 8 + i:9 + i], None, ALU.mult))
                own.tell(sems["ready"])

            def finish(n):
                for j in range(1, len(parts[n]["blocks"]), 2):
                    rows, first = parts[n]["blocks"][j]
                    dve.wait_ge(sems["t_mm1"], count[n, j][1])
                    dve.tensor_copy(turned[0:rows, n % 2, j, first * P:], banks[5][0:rows, first * P:]).then_inc(sems["t_out1"], 1)

            def output(n):
                part = parts[n]
                if part["last"]:
                    dve.wait_ge(sems["pv_mm"], n + 1)
                    lo, done = part["lo"], sum(m < n for m in outs)
                    dve.tensor_tensor(part["out"], banks[6 + done % 2][lo:lo + 64, :], part["z"], ALU.mult).then_inc(sems["y_out"], 1)

            mask(0)
            for n in range(n_parts):
                if n + 1 < n_parts:
                    mask(n + 1)
                normalise(n)
                if n:
                    output(n - 1)
                finish(n)
            output(n_parts - 1)
            dve.wait_ge(sems["y_out"], len(outs))


def stick_breaking(nc, core, b, p):
    con, banks = b["con"], core.banks
    tl = TILES2
    width = [T - j * P for j in range(4)]
    at = [sum(width[:j]) for j in range(5)]
    zs, soft = b["z"], b["soft"]
    suffix, strict01, strict_neg = (con[:, CONST2[n]:CONST2[n] + P] for n in ("suffix", "strict01", "strict_neg"))

    def span(buf, h, j):
        return buf[:, h % 2, at[j]:at[j + 1]]

    cum = [(4, 0), (5, 0), (6, 0), (6, 256)]

    with phase(nc, "z_mm", "z_out", "logged", "soft", "cum_mm", "less", "weights", "pv_mm", "y_out", "own", "own_act") as (block, sems):
        @block.tensor
        def _(pe):
            def logits(h):
                m, lo = h // 2, 64 * (h % 2)
                q, k = p[lo:lo + 64, tl["sb_q"] + m, :], p[lo:lo + 64, tl["sb_k"] + m, :]
                for j in range(4):
                    if h:
                        pe.wait_ge(sems["z_out"], 4 * (h - 1) + j + 1)
                    pe.matmul(banks[j][:, 0:width[j]], k[:, j * P:(j + 1) * P], q[:, j * P:], start=True, stop=True)\
                        .then_inc(sems["z_mm"], 1)

            logits(0)
            for h in range(4):
                m, lo = h // 2, 64 * (h % 2)
                if h < 3:
                    logits(h + 1)
                pe.wait_ge(sems["soft"], h + 1)
                if h:
                    pe.wait_ge(sems["less"], h)
                for j in range(4):
                    bank, c = cum[j]
                    mm = pe.matmul(banks[bank][:, c:c + width[j]], suffix, span(soft, h, j), start=True, stop=(j == 3))
                    for later in range(j + 1, 4):
                        off = c + (later - j) * P
                        mm = pe.matmul(banks[bank][:, off:off + width[later]], core.ones[:, :], span(soft, h, later),
                                       start=False, stop=(later == 3))
                mm.then_inc(sems["cum_mm"], 1)
                if h:
                    pe.wait_ge(sems["y_out"], h)
                pe.wait_ge(sems["weights"], h + 1)
                for j in range(4):
                    mm = pe.matmul(banks[7][lo:lo + 64, j * P:], b["tm_v"][:, j, 256 + h * 64:256 + (h + 1) * 64],
                                   span(zs, h, j), start=(j == 0), stop=(j == 3))
                mm.then_inc(sems["pv_mm"], 1)

        @block.scalar
        def _(act):
            own = Own(act, sems["own_act"])

            def whole(buf, h):
                return buf[:, h % 2, 0:at[4]]

            def logarithm(h):
                if h >= 2:
                    act.wait_ge(sems["pv_mm"], h - 1)
                for j in range(4):
                    act.wait_ge(sems["z_mm"], 4 * h + j + 1)
                    own(act.mul(span(zs, h, j), banks[j][:, 0:width[j]], SCALE))
                    own(act.activation(span(soft, h, j), banks[j][:, 0:width[j]], ACT.Abs, scale=SCALE))
                    own.tell(sems["z_out"])
                own(act.activation(whole(soft, h), whole(soft, h), ACT.Exp, scale=-1.0))
                own.settle()
                act.activation(whole(soft, h), whole(soft, h), ACT.Ln, bias=core.ones[:, 0:1]).then_inc(sems["logged"], 1)

            logarithm(0)
            for h in range(4):
                if h < 3:
                    logarithm(h + 1)
                act.wait_ge(sems["less"], h + 1)
                act.activation(whole(zs, h), whole(zs, h), ACT.Exp).then_inc(sems["weights"], 1)

        @block.vector
        def _(dve):
            own = Own(dve, sems["own"])

            def softplus(h):
                dve.wait_ge(sems["logged"], h + 1)
                a = slice(0, at[4])
                own(dve.scalar_tensor_tensor(out=soft[:, h % 2, a], in0=zs[:, h % 2, a], scalar=0.0, in1=soft[:, h % 2, a],
                                             op0=ALU.max, op1=ALU.add))
                own.settle()
                for j in range(4):
                    d = span(soft, h, j)[:, 0:P]
                    own(dve.tensor_tensor(d, d, strict01, ALU.mult))
                own.tell(sems["soft"])
                for j in range(4):
                    d = span(zs, h, j)[:, 0:P]
                    own(dve.tensor_tensor(d, d, strict_neg, ALU.add))
                own.settle()

            softplus(0)
            for h in range(4):
                dve.wait_ge(sems["cum_mm"], h + 1)
                for j in range(4):
                    bank, c = cum[j]
                    own(dve.scalar_tensor_tensor(out=span(zs, h, j), in0=banks[bank][:, c:c + width[j]], scalar=-1.0,
                                                 in1=span(zs, h, j), op0=ALU.mult, op1=ALU.add))
                own.tell(sems["less"])
                if h < 3:
                    softplus(h + 1)
                dve.wait_ge(sems["pv_mm"], h + 1)
                m, lo = h // 2, 64 * (h % 2)
                dve.tensor_tensor(p[lo:lo + 64, tl["sb_q"] + m, :], banks[7][lo:lo + 64, :], p[lo:lo + 64, tl["sb_z"] + m, :],
                                  ALU.mult).then_inc(sems["y_out"], 1)
            dve.wait_ge(sems["y_out"], 4)


def block2_layer(nc, core, layer, w, con, tables):
    with ExitStack() as outer:
        def buf(stack, name, shape, rows=P):
            return stack.enter_context(nc.sbuf_tensor(name, [rows] + shape, F32))

        p = buf(outer, "p2", [IN2_TILES, T])
        tl = TILES2
        project_in2(nc, core, layer, w, p)
        with ExitStack() as stack:
            b = {"con": con, "tables": tables, "w1_dram": w["w1_2"][layer]}
            b["tm_v"], b["tm_s"] = buf(stack, "tm_v", [4, TM_V]), buf(stack, "tm_s", [4, TM_S])
            b["mem_k"], b["mem_v"] = buf(stack, "mem_k", [2, N_MEM]), buf(stack, "mem_v", [2, 256])
            with ExitStack() as scratch:
                b["mem"], b["memh"] = buf(scratch, "mem_x", [KD, N_MEM]), buf(scratch, "mem_h", [KD, N_MEM])
                b["wm"] = buf(scratch, "mem_w", [4 * KD * P])
                token_major(nc, core, layer, w, b)
            b["dsa_k"], b["dsa_v"] = buf(stack, "dsa_k", [2, T]), buf(stack, "dsa_v", [4, 256])
            b["cmp_k"], b["cmp_v"] = buf(stack, "cmp_k", [N_CMP]), buf(stack, "cmp_v", [64], N_CMP)
            b["f_abs"], b["f_log"], b["cum"] = buf(stack, "f_abs", [4, 4]), buf(stack, "f_log", [4, 4]), buf(stack, "cum", [2, T], 4)
            b["stats"] = buf(stack, "stats", [2, 12])
            with ExitStack() as scratch:
                b["turn"], b["squares"], b["hidden"] = buf(scratch, "turn", [2, T]), buf(scratch, "ckv2", [T]), buf(scratch, "hidden", [2, 32])
                prepare2(nc, core, b, p)
            with ExitStack() as scratch:
                b["z"] = core.ring[:, 0:2560].rearrange("p (h n) -> p h n", h=2)
                b["soft"] = core.ring[:, 2560:5120].rearrange("p (h n) -> p h n", h=2)
                stick_breaking(nc, core, b, p)
                b["bias"] = buf(scratch, "bias", [4, T])
                with ExitStack() as temporary:
                    b["rel"], b["score"], b["top"] = (buf(temporary, "rel", [4, T]), buf(temporary, "score", [4, T]),
                                                      buf(temporary, "top", [4, 8]))
                    select_keys(nc, core, b, p)
                b["probs"] = buf(scratch, "probs", [2, 4, T])
                b["probsT"] = core.ring[:, 0:8 * T].rearrange("p (a j t) -> p a j t", a=2, j=4)

                def causal(i):
                    at = CONST2["causal"] + 384 - i * P
                    return con[:, at:at + (i + 1) * P]

                triangle = [(P, j) for j in range(4)]

                def grow(i):
                    return (i + 1) * P

                def part(name, h, k, values, mask, keys=grow, blocks=triangle, extra=None, row=None, first=True, last=True):
                    m, lo = h // 2, 64 * (h % 2)
                    return {"q": p[lo:lo + 64, tl[name + "_q"] + m, :], "k": k[lo:lo + 64], "values": values, "mask": mask,
                            "keys": keys, "blocks": blocks, "extra": extra, "row": row, "first": first, "last": last,
                            "lo": lo, "out": p[lo:lo + 64, tl[name + "_q"] + m, :], "z": p[lo:lo + 64, tl[name + "_z"] + m, :]}

                def forget(h):
                    sel = con[0:4, CONST2["sel"] + h * P:CONST2["sel"] + (h + 1) * P]

                    def extra(pe, bank, i):
                        width = (i + 1) * P
                        pe.matmul(wide(bank[:, 0:width], i + 1), b["cum"][0:4, 0, i * P:(i + 1) * P],
                                  sel.rearrange("p (o t) -> p o t", o=1).to_broadcast([4, i + 1, P]), start=False, stop=False)
                        return pe.matmul(bank[:, 0:width], sel, b["cum"][0:4, 1, 0:width], start=False, stop=True)
                    return extra

                parts = []
                for h in range(NH):
                    m = h // 2
                    parts.append(part("dsa", h, b["dsa_k"][:, m, :], lambda j, h=h: b["dsa_v"][:, j, h * 64:(h + 1) * 64],
                                      lambda i: b["bias"][:, i, 0:(i + 1) * P]))
                for h in range(NH):
                    m = h // 2
                    parts.append(part("fox", h, p[:, tl["fox_k"] + m, :], lambda j, h=h: b["tm_v"][:, j, h * 64:(h + 1) * 64],
                                      causal, extra=forget(h)))
                for h in range(NH):
                    def gate(n, h=h):
                        return b["tm_s"][:, :, NSA_G + 4 * n + h]

                    parts.append(part("nsa", h, b["cmp_k"], lambda j: b["cmp_v"][:, :],
                                      lambda i: con[:, CONST2["cmp"] + i * 32:CONST2["cmp"] + i * 32 + N_CMP],
                                      keys=lambda i: N_CMP, blocks=[(N_CMP, 0)], row=gate(0), last=False))
                    parts.append(part("nsa", h, p[:, tl["ks"], :], lambda j: b["tm_s"][:, j, VS:VS + 64], causal, row=gate(1),
                                      first=False, last=False))
                    parts.append(part("nsa", h, p[:, tl["kw"], :], lambda j: b["tm_s"][:, j, VW:VW + 64], causal, row=gate(2),
                                      first=False))
                for h in range(NH):
                    m = h // 2
                    parts.append(part("mem", h, b["mem_k"][:, m, :], lambda j, h=h: b["mem_v"][:, j, h * 64:(h + 1) * 64],
                                      lambda i: core.zeros[:, 0:N_MEM], keys=lambda i: N_MEM, blocks=[(P, 0), (P, 0)]))
                attention(nc, core, b, parts)
        with ExitStack() as stack:
            merged = buf(stack, "merged2", [KD, T])
            gate_buf, part_buf = buf(stack, "gate2", [N_BR2, T]), buf(stack, "part2", [N_BR2, T])
            ys = [p[:, tl[n + "_q"]:tl[n + "_q"] + 2, :] for n in ("dsa", "fox", "sb", "nsa", "mem")]
            merge(nc, core, layer, w["merge2"], ys, 2, merged, gate_buf, part_buf)
            add_projection(nc, core, layer, w["out2"], merged, KD, 1)


def layout2(i):
    w = i["w_in_2"]
    at, c = 0, {}
    for name, n in (("dsa_q", 256), ("ckv", 128), ("idx_q", 128), ("idx_k", 32), ("idx_w", 4), ("dsa_z", 256), ("fox_q", 256),
                    ("fox_k", 256), ("fox_v", 256), ("fox_f", 4), ("fox_z", 256), ("sb_q", 256), ("sb_k", 256), ("sb_v", 256),
                    ("sb_z", 256), ("nsa_q", 256), ("kc", 64), ("vc", 64), ("ks", 64), ("vs", 64), ("kw", 64), ("vw", 64),
                    ("nsa_g", 12), ("nsa_z", 256), ("mem_q", 256), ("mem_z", 256), ("merge", N_BR2 * D)):
        c[name] = w[:, :, at:at + n]
        at += n
    assert at == w.shape[2]
    tiles = [c["dsa_q"], c["ckv"], c["idx_q"]] + [c["idx_k"]] * 4 + [c["dsa_z"], c["fox_q"], c["fox_k"], c["fox_z"],
                                                                     c["sb_q"], c["sb_k"], c["sb_z"], c["nsa_q"],
                                                                     c["kc"], c["vc"], c["ks"], c["ks"], c["kw"], c["kw"],
                                                                     c["nsa_z"], c["mem_q"], c["mem_z"]]
    a = {"in2": by_tiles(np.concatenate(tiles, 2), KD).reshape(-1, P, KD * P)}

    def rows(v, k):
        return v.reshape(DEPTH, k, P, -1).transpose(0, 2, 1, 3).reshape(DEPTH, P, -1)

    a["tm2"] = np.concatenate([rows(np.concatenate([c["fox_v"], c["sb_v"]], 2), KD),
                               rows(np.concatenate([c["vs"], c["vw"], c["idx_w"], c["nsa_g"], c["fox_f"]], 2), KD)], 2)
    wm = i["w_mem_kv_2"]
    a["wm2"] = np.concatenate([by_tiles(wm[:, :, 0:256], KD).reshape(DEPTH, 2, P, KD * P).transpose(0, 2, 1, 3)
                               .reshape(DEPTH, P, -1), rows(wm[:, :, 256:], KD)], 2)
    gates = by_tiles(c["merge"], KD).reshape(DEPTH, N_BR2, KD, P, KD, P)
    branch = np.stack([by_tiles(i["w_branch_2"][:, n], 2) for n in range(N_BR2)], 1)
    a["merge2"] = np.concatenate([gates, branch], 4).transpose(0, 2, 1, 3, 4, 5).reshape(-1, P, 10 * P)
    a["out2"] = by_tiles(i["w_out_2"], KD).reshape(-1, P, KD * P)
    a["par2"] = np.concatenate([vectors(i["norm_g_2"]), vectors(i["kv_norm_2"]),
                                np.broadcast_to(i["fox_bias_2"][:, None, :], (DEPTH, P, 4)), vectors(i["mem_norm_2"])], 2)
    pe = np.concatenate([i["nsa_pe_k_2"], i["nsa_pe_v_2"]], 2).transpose(0, 2, 1)
    a["small2"] = np.concatenate([i["w_uk_2"], i["w_uv_2"], pe, i["nsa_wc2_k_2"], i["nsa_wc2_k_2"], i["nsa_wc2_v_2"]], 2)
    w1 = [i[n].reshape(DEPTH, CMP_LEN, 64, P).transpose(0, 2, 1, 3) for n in ("nsa_wc1_k_2", "nsa_wc1_v_2")]
    a["w1_2"] = np.concatenate(w1, 1).reshape(DEPTH, P, CMP_LEN * P)
    a["mem"] = i["mem_2"][0].T.reshape(KD, P, N_MEM).transpose(1, 0, 2)
    return a


def program(nc, w, positions, out, blocks=(1, 2)):
    core = Core()
    with ExitStack() as stack:
        def buf(ctx, name, shape):
            return ctx.enter_context(nc.sbuf_tensor(name, [P] + shape, F32))

        core.x, core.h, core.ring = buf(stack, "x", [KD, T]), buf(stack, "h", [KD, T]), buf(stack, "ring", [RING_COLUMNS])
        core.root, core.ones, core.eps, core.tiny = (buf(stack, "root", [T]), buf(stack, "ones", [P]), buf(stack, "eps", [2]),
                                                     buf(stack, "tiny", [64]))
        core.banks = [stack.enter_context(nc.psum_tensor(f"bank{n}", [P, T], F32)) for n in range(8)]
        gains = buf(stack, "gains", [2 * KD])
        with ExitStack() as ctx:
            core.par, core.small, core.con = (buf(ctx, "par1_sb", [NPAR1]), buf(ctx, "small1_sb", [NSMALL1]),
                                              buf(ctx, "con1_sb", [NCONST1]))
            core.ident = core.con[:, CONST1["ident"]:CONST1["ident"] + P]
            with phase(nc, "loaded") as (block, sems):
                @block.sync
                def _(sp):
                    for dst, src in ((core.x[:, :, :], w["x"]), (core.con[:, :], w["con1"]), (gains[:, :], w["gains"])):
                        sp.dma_start(dst, src).then_inc(sems["loaded"], 16)
                    sp.wait_ge(sems["loaded"], 48)

                @block.vector
                def _(dve):
                    dve.memset(core.ones[:, :], 1.0)
                    dve.memset(core.eps[:, 0:1], EPS)
                    dve.memset(core.eps[:, 1:2], GN_EPS)

            if 1 in blocks:
                with nc.Fori(0, DEPTH) as layer:
                    block1_layer(nc, core, layer, w)
                final_norm(nc, core, gains[:, 0:KD], core.x)
        if 2 in blocks:
            with ExitStack() as ctx:
                con, tables, core.zeros = buf(ctx, "con2_sb", [NCONST2]), buf(ctx, "rope", [4, T]), buf(ctx, "zeros", [N_MEM])
                core.par, core.small = buf(ctx, "par2_sb", [NPAR2]), buf(ctx, "small2_sb", [NSMALL2])
                core.ident2 = con[:, CONST2["ident"]:CONST2["ident"] + P]
                with phase(nc, "loaded") as (block, sems):
                    @block.sync
                    def _(sp):
                        sp.dma_start(con[:, :], w["con2"]).then_inc(sems["loaded"], 16)
                        sp.wait_ge(sems["loaded"], 16)

                    @block.vector
                    def _(dve):
                        dve.memset(core.zeros[:, :], 0.0)

                rope_tables(nc, core, con, tables, positions)
                with nc.Fori(0, DEPTH) as layer:
                    block2_layer(nc, core, layer, w, con, tables)
                final_norm(nc, core, gains[:, KD:2 * KD], core.x)
        with phase(nc, "stored") as (block, sems):
            @block.sync
            def _(sp):
                sp.dma_start(out, core.x[:, :, :]).then_inc(sems["stored"], 16)
                sp.wait_ge(sems["stored"], 16)


def kernel(**inputs):
    import concourse.bacc as _bacc
    from concourse import mybir as _mybir
    from concourse.bass_utils import run_bass_kernel_spmd as _run

    i = {name: np.asarray(a) for name, a in inputs.items()}
    arrays = {**layout1(i), **layout2(i), "con1": constants1(), "con2": constants2()}
    arrays["x"] = i["x"][0].T.reshape(KD, P, T).transpose(1, 0, 2)
    arrays["gains"] = np.concatenate([i["final_g"].reshape(KD, P).T, i["final_norm_2"].reshape(KD, P).T], 1)
    arrays["positions"] = i["positions_2"].reshape(1, T)
    arrays = {name: np.ascontiguousarray(a) for name, a in arrays.items()}
    nc = _bacc.Bacc("TRN2", target_bir_lowering=False, num_devices=1)
    w = {name: nc.dram_tensor(f"in_{name}", a.shape, _mybir.dt.from_np(a.dtype), kind="ExternalInput").ap()
         for name, a in arrays.items()}
    out = nc.dram_tensor("out", (P, KD, T), F32, kind="ExternalOutput").ap()
    program(nc, w, w["positions"], out)
    r = _run(nc, [{f"in_{name}": a for name, a in arrays.items()}], core_ids=[0])
    return r.results[0]["out"].transpose(1, 0, 2).reshape(1, D, T).transpose(0, 2, 1)
```

```python
from contextlib import ExitStack, contextmanager

import numpy as np
import concourse.bass as bass
import concourse.mybir as mybir

F32 = mybir.dt.float32
F32R = mybir.dt.float32r
I32 = mybir.dt.int32
ALU = mybir.AluOpType
ACT = mybir.ActivationFunctionType
AX = mybir.AxisListType

P = 128
T = 512
D = 1024
KD = D // P
DEPTH = 2
CH = 128
NCH = T // CH
RING = 4
RING_COLUMNS = 5 * 10 * P
EPS = 1e-6
NEG = -1e30
RW_TILES, RET_TILES, SG_TILES = 14, 12, 8
IN1_TILES = RW_TILES + RET_TILES + SG_TILES
FFN_TILES = 22
GN_EPS = 64e-5
DECAY_RATE = float(np.exp(-0.5))


def offsets(sizes):
    at, out = 0, {}
    for name, n in sizes:
        out[name] = at
        at += n
    return out, at


PAR1, NPAR1 = offsets([("norm1", 8), ("mu", 14), ("w0", 4), ("a0", 4), ("k_k", 4), ("k_a", 4), ("r_k", 4),
                       ("lnx_g", 4), ("lnx_b", 4), ("ln_g", 4), ("ln_b", 4), ("norm2", 8),
                       ("conv", 3 * 44), ("conv_b", 44)])
SMALL1, NSMALL1 = offsets([("lora_up", 512), ("g_up", 512), ("w_sT", 512), ("sg_b", 512)])

CONST1, NCONST1 = offsets([("ident", 128), ("headsum", 128), ("rot", 128), ("strict_su", 128), ("neg_strict_su", 128), ("incl_su", 128),
                           ("level", 7 * 128), ("level0", 128), ("scan", 512), ("ret_cos", 512), ("ret_sin", 512),
                           ("ret_decay", 512), ("ret_qdec", 1024), ("ret_kdec", 4), ("ret_chunk", 2)])


def constants1():
    c = np.zeros((P, NCONST1), np.float32)

    def put(name, a):
        a = np.asarray(a, np.float32).reshape(P, -1)
        c[:, CONST1[name]:CONST1[name] + a.shape[1]] = a

    i, j = np.arange(P)[:, None], np.arange(P)[None, :]
    put("ident", i == j)
    put("headsum", i // 64 == j // 64)
    put("rot", rotation(64))
    put("strict_su", i < j)
    put("neg_strict_su", -(i < j).astype(np.float32))
    put("incl_su", i <= j)
    level = [(i >> (l + 1) == j >> (l + 1)) & ((i >> l) % 2 == 0) & ((j >> l) % 2 == 1) for l in range(7)]
    put("level", np.stack([m.astype(np.float32) for m in level], 1))
    put("level0", -level[0].T.astype(np.float32))
    put("scan", np.broadcast_to((np.arange(T) % CH != 0).astype(np.float32), (P, T)))
    inv = np.float32(1.0) / np.power(np.float32(10000.0), np.linspace(0, 1, 32, dtype=np.float32))
    ang = np.arange(T, dtype=np.float32)[None, :] * inv[np.arange(P) % 32][:, None]
    put("ret_cos", np.cos(ang.astype(np.float64)))
    put("ret_sin", np.sin(ang.astype(np.float64)))
    lg = np.log(1.0 - 2.0 ** (-5.0 - np.arange(4, dtype=np.float64)))
    put("ret_decay", np.stack([np.where(j >= i, np.exp(np.maximum(j - i, 0) * g), 0.0) for g in lg], 1))
    pos = np.arange(T) % CH
    head = np.stack([2 * t + np.arange(P) // 64 for t in range(2)], 1)
    put("ret_qdec", np.exp((pos + 1.0)[None, None, :] * lg[head][:, :, None]))
    put("ret_kdec", np.exp((CH - 1.0 - np.arange(P))[:, None] * lg[None, :]))
    put("ret_chunk", np.exp(CH * lg[head]))
    return c


def rotation(width):
    r = np.zeros((P, P), np.float32)
    half = width // 2
    for c in range(P):
        o = c % width
        if o < half:
            r[c + half, c] = -1.0
        else:
            r[c - half, c] = 1.0
    return r


class Core:
    pass


class Own:

    def __init__(self, engine, sem):
        self.engine, self.sem, self.n = engine, sem, 0

    def __call__(self, instruction):
        instruction.then_inc(self.sem, 1)
        self.n += 1

    def settle(self):
        self.engine.wait_ge(self.sem, self.n)

    def tell(self, sem):
        self.settle()
        self.engine.sem_inc(sem, 1)


@contextmanager
def phase(nc, *names):
    with ExitStack() as stack:
        sems = {name: stack.enter_context(nc.semaphore(name)) for name in names}
        with nc.Block() as block:
            yield block, sems
        for sem in sems.values():
            nc.sync.sem_clear(sem)
        nc.all_engine_barrier()


LANDED = [f"landed{s}" for s in range(RING)]


def slot(core, s, width):
    return core.ring[:, s * width:(s + 1) * width]


def stream(sp, sems, core, unit, count, blocks=KD, ring=RING, freed="split"):
    def load(n, s):
        sp.dma_start(slot(core, s, blocks * P), unit(n)).then_inc(sems[LANDED[s]], 16)

    for s in range(min(ring, count)):
        load(s, s)
    rounds = count // ring
    if rounds > 1:
        with sp.Fori(1, rounds) as r:
            for s in range(ring):
                sp.wait_ge(sems[freed], r * ring + (s + 1 - ring))
                load(r * ring + s, s)
    for n in range(max(rounds, 1) * ring, count):
        sp.wait_ge(sems[freed], n + 1 - ring)
        load(n, n % ring)



def high_part(act, sems, core, s, half):
    width = s[1]
    act.copy(core.wh[:, half, 0:width], slot(core, s[0], s[1])[:, 0:width]).then_inc(sems["rounded"], 1)


def low_part(dve, sems, core, s, half):
    width = s[1]
    dve.tensor_tensor(core.wl[:, half, 0:width], slot(core, s[0], s[1])[:, 0:width],
                      core.wh[:, half, 0:width].bitcast(F32), ALU.subtract).then_inc(sems["split"], 1)


def block_passes(pe, bank, core, half, block, high, low, start, stop):
    w = slice(block * P, (block + 1) * P)
    pe.matmul(bank, core.wh[:, half, w], high, start=start, stop=False)
    pe.matmul(bank, core.wh[:, half, w], low, start=False, stop=False)
    return pe.matmul(bank, core.wl[:, half, w], high, start=False, stop=stop)


def three_passes(pe, bank, core, half, h_ready=None):
    for k in range(KD):
        if h_ready is not None:
            pe.wait_ge(h_ready, k + 1)
        mm = block_passes(pe, bank, core, half, k, core.hh[:, k, :], core.hl[:, k, :], k == 0, k == KD - 1)
    return mm


def source_high(act, src, high, sem):
    act.copy(high, src).then_inc(sem, 1)


def source_low(dve, src, high, low, sem):
    dve.tensor_tensor(low, src, high.bitcast(F32), ALU.subtract).then_inc(sem, 1)


def project(pe, sems, core, count, h_ready=None):
    def tile(s, split, evacuated, h_ready=None):
        pe.wait_ge(sems["split"], split)
        if evacuated is not None:
            pe.wait_ge(sems["evacuated"], evacuated)
        three_passes(pe, core.banks[s][:, :], core, s % 2, h_ready).then_inc(sems["projected"], 1)

    for s in range(min(RING, count)):
        tile(s, s + 1, None, h_ready if s == 0 else None)
    rounds = count // RING
    if rounds > 1:
        with pe.Fori(1, rounds) as r:
            for s in range(RING):
                tile(s, r * RING + (s + 1), r * RING + (s + 1 - RING))
    for n in range(max(rounds, 1) * RING, count):
        tile(n % RING, n + 1, n + 1 - RING)


def first_high_parts(act, sems, core):
    for n in range(2):
        act.wait_ge(sems[LANDED[n]], 16)
        high_part(act, sems, core, (n, KD * P), n)


def round_and_evacuate(act, sems, core, outs, count):
    def tile(out, n, s, projected, landed):
        act.wait_ge(sems["projected"], projected)
        if landed is not None:
            act.wait_ge(sems[LANDED[(s + 2) % RING]], landed)
            high_part(act, sems, core, ((s + 2) % RING, KD * P), s % 2)
        act.copy(out(n), core.banks[s][:, :]).then_inc(sems["evacuated"], 1)

    rounds = (count - 2) // RING
    first = 0
    for end, out in outs:
        last = min(end // RING, rounds)
        with act.Fori(first, last) as r:
            for s in range(RING):
                tile(out, r * RING + s, s, r * RING + (s + 1), r * 16 + 16 * (1 + (s + 2) // RING))
        first = last
    for n in range(rounds * RING, count):
        tile(out, n, n % RING, n + 1, 16 * (1 + (n + 2) // RING) if n + 2 < count else None)


def low_parts(dve, sems, core, count, first=0):
    rounds = count // RING
    done = first
    if not first and rounds:
        with dve.Fori(0, rounds) as r:
            for s in range(RING):
                dve.wait_ge(sems["rounded"], r * RING + (s + 1))
                low_part(dve, sems, core, (s, KD * P), s % 2)
        done = rounds * RING
    for n in range(done, count):
        dve.wait_ge(sems["rounded"], n + 1)
        low_part(dve, sems, core, (n % RING, KD * P), n % 2)


def low_parts_from(dve, sems, core, count):
    rounds = count // RING
    if rounds > 1:
        with dve.Fori(1, rounds) as r:
            for s in range(RING):
                dve.wait_ge(sems["rounded"], r * RING + (s + 1))
                low_part(dve, sems, core, (s, KD * P), s % 2)
    low_parts(dve, sems, core, count, first=max(rounds, 1) * RING)


ROOT = ["squared", "summed", "sum_steps", "rooted", "inverted"]


def square_tile(act, sems, core, d):
    if d >= 3:
        act.wait_ge(sems["summed"], d - 2)
    act.activation(core.squares[:, d % 2 if d else 2, :], core.x[:, d, :], ACT.Square).then_inc(sems["squared"], 1)


def sum_tile(dve, sems, core, d):
    dve.wait_ge(sems["squared"], d + 1)
    if d >= 2:
        dve.wait_ge(sems["summed"], d - 1)
    total = core.squares[:, 2, :]
    dve.tensor_tensor(total, total, core.squares[:, d % 2, :], ALU.add).then_inc(sems["summed"], 1)


def sum_channels(pe, sems, core):
    for ready, count, t in (("summed", KD - 2, 2), ("squared", KD, (KD - 1) % 2)):
        pe.wait_ge(sems[ready], count)
        mm = pe.matmul(core.banks[7][:, :], core.ones[:, :], core.squares[:, t, :], start=(t == 2), stop=(t != 2))
    mm.then_inc(sems["sum_steps"], 1)


def take_root(act, sems, core):
    act.wait_ge(sems["sum_steps"], 1)
    act.activation(core.root[:, :], core.banks[7][:, :], ACT.Sqrt, bias=core.eps[:, 0:1], scale=1.0 / D)\
        .then_inc(sems["rooted"], 1)


def invert_root(dve, sems, core):
    dve.wait_ge(sems["rooted"], 1)
    dve.reciprocal(core.root[:, :], core.root[:, :]).then_inc(sems["inverted"], 1)
    dve.wait_ge(sems["inverted"], 1)


def norm_scale(dve, sems, own, x, root, gain, out, tiles=KD):
    dve.wait_ge(sems["rooted"], 1)
    own(dve.reciprocal(root, root))
    own.settle()
    for k in range(tiles):
        dve.scalar_tensor_tensor(out=out[:, k, :], in0=x[:, k, :], scalar=gain[:, k:k + 1], in1=root,
                                 op0=ALU.mult, op1=ALU.mult).then_inc(sems["normed"], 1)


NORM = ["raw", "h_rounded", "normed"]


def norm_round(act, sems, core, tmp):
    for k in range(KD):
        if k == 3:
            act.wait_ge(sems[LANDED[0]], 16)
            high_part(act, sems, core, (0, KD * P), 0)
        act.wait_ge(sems["raw"], k + 1)
        act.copy(core.hh[:, k, :], tmp[:, k % 4, :]).then_inc(sems["h_rounded"], 1)
    act.wait_ge(sems[LANDED[1]], 16)
    high_part(act, sems, core, (1, KD * P), 1)


def norm_split(dve, sems, core, gain, tmp):
    def low(k):
        dve.wait_ge(sems["h_rounded"], k + 1)
        dve.tensor_tensor(core.hl[:, k, :], tmp[:, k % 4, :], core.hh[:, k, :].bitcast(F32), ALU.subtract)\
            .then_inc(sems["normed"], 1)

    for k in range(KD):
        if k >= 4:
            dve.wait_ge(sems["normed"], k - 3)
        dve.scalar_tensor_tensor(out=tmp[:, k % 4, :], in0=core.x[:, k, :], scalar=gain[:, k:k + 1], in1=core.root[:, :],
                                 op0=ALU.mult, op1=ALU.mult).then_inc(sems["raw"], 1)
        if k >= 2:
            low(k - 2)
        if k == 4:
            dve.wait_ge(sems["rounded"], 1)
            low_part(dve, sems, core, (0, KD * P), 0)
    low(KD - 2)
    low(KD - 1)
    dve.wait_ge(sems["rounded"], 2)
    low_part(dve, sems, core, (1, KD * P), 1)


def wide(ap, tiles):
    return ap.rearrange("p (a b) -> p a b", a=tiles)


def project_h(nc, core, units, count, out, gain=None, tmp=None, params=()):
    with phase(nc, *LANDED, "projected", "evacuated", "rounded", "split", *NORM, "gain_landed", "params") as (block, sems):
        @block.sync
        def _(sp):
            stream(sp, sems, core, units, count)

        @block.scalar
        def _(act):
            if gain is None:
                first_high_parts(act, sems, core)
            else:
                for n, (dst, src) in enumerate(params):
                    act.dma_start(dst, src).then_inc(sems["params" if n else "gain_landed"], 16)
                norm_round(act, sems, core, tmp)
            round_and_evacuate(act, sems, core, out, count)
            if params:
                act.wait_ge(sems["params"], 16 * (len(params) - 1))

        @block.tensor
        def _(pe):
            project(pe, sems, core, count, None if gain is None else sems["normed"])

        @block.vector
        def _(dve):
            if gain is not None:
                dve.wait_ge(sems["gain_landed"], 16)
                norm_split(dve, sems, core, gain, tmp)
                for n in range(2, RING):
                    dve.wait_ge(sems["rounded"], n + 1)
                    low_part(dve, sems, core, (n, KD * P), n % 2)
                low_parts_from(dve, sems, core, count)
            else:
                low_parts(dve, sems, core, count)


def rwkv_prepare(nc, core, b):
    par, small, con, banks = core.par, core.small, core.con, core.banks

    def col(name, n):
        return par[:, PAR1[name] + n:PAR1[name] + n + 1]

    p = b["p_rw"]
    r, k, v = (p[:, 4 * n:4 * n + 4, 1:] for n in range(3))
    lw, decay, rate, gate, kk, bonus = (b[n] for n in ("A", "B", "C", "D", "E", "F"))
    tmp, grow = b["H"], b["G"]
    mid, end = core.tiny[:, 8:24], core.tiny[:, 24:40]
    with phase(nc, "low_shifted", "hidden", "decay_mm", "rate_mm", "gate_mm", "norm_mm", "bonus_mm", "decay_rate_out",
               "gate_out", "norm_out", "keys_squared", "exponents", "before_exp", "grown", "rkk", "own", "own_act") as (block, sems):
        @block.vector
        def _(dve):
            own = Own(dve, sems["own"])
            own(dve.memset(p[:, :, 0:1], 0.0))
            own.settle()
            for lo in (12, 8, 4, 0):
                n = 2 if lo == 12 else 4
                diff = grow[:, 0:n, :]
                own(dve.tensor_tensor(diff, p[:, lo:lo + n, 0:T], p[:, lo:lo + n, 1:], ALU.subtract))
                own.settle()
                for m in range(n):
                    own(dve.scalar_tensor_tensor(out=p[:, lo + m, 1:], in0=diff[:, m, :], scalar=col("mu", lo + m),
                                                 in1=p[:, lo + m, 1:], op0=ALU.mult, op1=ALU.add))
                own.settle()
                if lo == 12:
                    own.tell(sems["low_shifted"])
            own(dve.tensor_scalar(core.tiny[:, 0:4], par[:, PAR1["k_a"]:PAR1["k_a"] + 4], -1.0, 1.0, ALU.mult, ALU.add))
            for m in range(4):
                own(dve.tensor_scalar(kk[:, m, :], k[:, m, :], col("k_k", m), None, ALU.mult))
            own.settle()
            own(dve.tensor_tensor(grow[:, :, :], kk[:, :, :], kk[:, :, :], ALU.mult))
            own.tell(sems["keys_squared"])
            dve.wait_ge(sems["decay_rate_out"], 1)
            own(dve.tensor_scalar(lw[:, :, :], lw[:, :, :], -DECAY_RATE, None, ALU.mult))
            own.settle()
            for m in range(4):
                own(dve.tensor_tensor_scan(decay[:, m, :], con[:, CONST1["scan"]:CONST1["scan"] + T], lw[:, m, :], 0.0,
                                           ALU.mult, ALU.add))
            own.settle()
            chunks = [decay[:, m, :].rearrange("p (c t) -> p c t", c=NCH) for m in range(4)]
            for m in range(4):
                own(dve.tensor_copy(mid[:, 4 * m:4 * m + 4], chunks[m][:, :, CH // 2 - 1]))
                own(dve.tensor_tensor(end[:, 4 * m:4 * m + 4], chunks[m][:, :, CH - 1], chunks[m][:, :, CH // 2 - 1],
                                      ALU.subtract))
            own.settle()
            for m in range(4):
                own(dve.tensor_tensor(chunks[m], chunks[m],
                                      mid[:, 4 * m:4 * m + 4].rearrange("p (c o) -> p c o", o=1).to_broadcast([P, NCH, CH]),
                                      ALU.subtract))
            own.settle()
            own(dve.tensor_tensor(lw[:, :, :], decay[:, :, :], lw[:, :, :], ALU.subtract))
            own.tell(sems["exponents"])
            for m in range(4):
                own(dve.tensor_scalar(tmp[:, m, :], rate[:, m, :], col("k_a", m), core.tiny[:, m:m + 1], ALU.mult, ALU.add))
            own.settle()
            own(dve.tensor_tensor(k, k, tmp[:, :, :], ALU.mult))
            own.settle()
            for m in range(4):
                own(dve.scalar_tensor_tensor(out=tmp[:, m, :], in0=r[:, m, :], scalar=col("r_k", m), in1=k[:, m, :],
                                             op0=ALU.mult, op1=ALU.mult))
            own.tell(sems["rkk"])
            dve.wait_ge(sems["norm_out"], 1)
            own(dve.tensor_scalar(bonus[:, :, :], bonus[:, :, :], 1e-12, None, ALU.max))
            own.settle()
            own(dve.reciprocal(bonus[:, :, :], bonus[:, :, :]))
            own.settle()
            own(dve.tensor_tensor(kk[:, :, :], kk[:, :, :], bonus[:, :, :], ALU.mult))
            own.settle()
            own(dve.tensor_tensor(rate[:, :, :], rate[:, :, :], kk[:, :, :], ALU.mult))
            dve.wait_ge(sems["before_exp"], 1)
            own(dve.tensor_tensor(lw[:, :, :], lw[:, :, :], kk[:, :, :], ALU.mult))
            own.settle()
            dve.wait_ge(sems["grown"], 1)
            own(dve.tensor_tensor(rate[:, :, :], rate[:, :, :], grow[:, :, :], ALU.mult))
            own(dve.tensor_tensor(k, k, grow[:, :, :], ALU.mult))
            own(dve.tensor_tensor(r, r, decay[:, :, :], ALU.mult))
            for m in range(4):
                dve.wait_ge(sems["bonus_mm"], m + 1)
                own(dve.tensor_tensor(bonus[:, m, :], banks[m][:, :], v[:, m, :], ALU.mult))
            own.settle()

        @block.scalar
        def _(act):
            own = Own(act, sems["own_act"])
            act.wait_ge(sems["low_shifted"], 1)
            own(act.activation(p[0:64, 12, 1:], p[0:64, 12, 1:], ACT.Tanh))
            own(act.activation(p[:, 13, 1:], p[:, 13, 1:], ACT.Sigmoid))
            own.tell(sems["hidden"])
            for m in range(4):
                act.wait_ge(sems["decay_mm"], m + 1)
                own(act.activation(lw[:, m, :], banks[m][:, :], ACT.Sigmoid, bias=col("w0", m)))
            for m in range(4):
                act.wait_ge(sems["rate_mm"], m + 1)
                own(act.activation(rate[:, m, :], banks[4 + m][:, :], ACT.Sigmoid, bias=col("a0", m)))
            own.tell(sems["decay_rate_out"])
            for m in range(4):
                act.wait_ge(sems["gate_mm"], m + 1)
                own(act.copy(gate[:, m, :], banks[m][:, :]))
            own.tell(sems["gate_out"])
            for m in range(4):
                act.wait_ge(sems["norm_mm"], m + 1)
                own(act.activation(bonus[:, m, :], banks[4 + m][:, :], ACT.Sqrt))
            own.tell(sems["norm_out"])
            act.wait_ge(sems["exponents"], 1)
            own(act.activation(lw[:, :, :], lw[:, :, :], ACT.Exp))
            own.tell(sems["before_exp"])
            own(act.activation(grow[:, :, :], decay[:, :, :], ACT.Exp, scale=-1.0))
            own.settle()
            own(act.activation(decay[:, :, :], decay[:, :, :], ACT.Exp))
            own(act.activation(core.tiny[:, 8:40], core.tiny[:, 8:40], ACT.Exp))
            own.tell(sems["grown"])

        @block.tensor
        def _(pe):
            lora = small[:, SMALL1["lora_up"]:SMALL1["lora_up"] + 512]
            g_up = small[:, SMALL1["g_up"]:SMALL1["g_up"] + 512]
            head = con[:, CONST1["headsum"]:CONST1["headsum"] + P]

            def product(bank, lhsT, rhs, name):
                pe.matmul(bank[:, :], lhsT, rhs, start=True, stop=True).then_inc(sems[name], 1)

            pe.wait_ge(sems["hidden"], 1)
            for m in range(4):
                product(banks[m], lora[0:64, m * P:(m + 1) * P], p[0:64, 12, 1:], "decay_mm")
            for m in range(4):
                product(banks[4 + m], lora[64:128, m * P:(m + 1) * P], p[64:128, 12, 1:], "rate_mm")
            pe.wait_ge(sems["decay_rate_out"], 1)
            for m in range(4):
                product(banks[m], g_up[:, m * P:(m + 1) * P], p[:, 13, 1:], "gate_mm")
            pe.wait_ge(sems["keys_squared"], 1)
            for m in range(4):
                product(banks[4 + m], head, grow[:, m, :], "norm_mm")
            pe.wait_ge(sems["gate_out"], 1)
            pe.wait_ge(sems["rkk"], 1)
            for m in range(4):
                product(banks[m], head, tmp[:, m, :], "bonus_mm")


def rwkv_scan(nc, core, b, y):
    con, banks, ident = core.con, core.banks, core.ident
    A, B, V, Kt, R = b["A"], b["C"], b["p_rw"][:, 8:12, 1:], b["p_rw"][:, 4:8, 1:], b["p_rw"][:, 0:4, 1:]
    S = b["state"]

    def heads(name, n=P):
        return con[:, CONST1[name]:CONST1[name] + n].rearrange("p (o t) -> p o t", o=1).to_broadcast([P, 4, P])

    def level(l):
        at = CONST1["level"] + l * P
        return con[:, at:at + P].rearrange("p (o t) -> p o t", o=1).to_broadcast([P, 4, P])

    def token_major(h, m):
        return slice(m * P + h * 64, m * P + h * 64 + 64)

    with phase(nc, "tok_mm", "tok_out", "pair_mm", "pair_out", "level_ready", "x_mm", "x_out", "inv_mm", "inv_out",
               "mix_mm", "mix_out", "u_mm", "u_out", "y_mm", "y_out", "state_mm", "scaled", "own",
               "own_act") as (block, sems):
        @block.vector
        def _(dve):
            own = Own(dve, sems["own"])
            own(dve.memset(S[:, :, :], 0.0))
            own.settle()
            for c in range(NCH):
                for m in range(4):
                    own(dve.tensor_scalar(S[:, m, :], S[:, m, :], core.tiny[:, 8 + 4 * m + c:9 + 4 * m + c], None, ALU.mult))
                own.tell(sems["scaled"])
                for h in range(2):
                    n = 2 * c + h
                    w = b["work"][h]
                    dve.wait_ge(sems["pair_mm"], 5 * n + 1)
                    own(dve.tensor_tensor(w["negNT"][:, :, :], wide(banks[0][:, :], 4), heads("neg_strict_su"), ALU.mult))
                    own.settle()
                    own(dve.tensor_tensor(w["invT"][:, :, :], w["negNT"][:, :, :], level(0), ALU.mult))
                    own.tell(sems["pair_out"])
                    dve.wait_ge(sems["pair_mm"], 5 * n + 2)
                    own(dve.tensor_tensor(w["inv"][:, :, :], wide(banks[1][:, :], 4), heads("level0"), ALU.mult))
                    own.tell(sems["pair_out"])
                    own(dve.tensor_tensor(w["invT"][:, :, :], w["invT"][:, :, :], heads("ident"), ALU.add))
                    own(dve.tensor_tensor(w["inv"][:, :, :], w["inv"][:, :, :], heads("ident"), ALU.add))
                    for q, name in enumerate(("PmT", "QbT", "QkT")):
                        dve.wait_ge(sems["pair_mm"], 5 * n + 3 + q)
                        own(dve.tensor_tensor(w[name][:, :, :], wide(banks[(2 + q) % 2][:, :], 4),
                                              heads("strict_su") if q == 0 else heads("incl_su"), ALU.mult))
                        own.tell(sems["pair_out"])
                for l in range(1, 7):
                    for h in range(2):
                        n = (c * 6 + l - 1) * 2 + h
                        w = b["work"][h]
                        dve.wait_ge(sems["inv_mm"], n + 1)
                        if l < 6:
                            own(dve.tensor_tensor(w["inv"][:, :, :], w["inv"][:, :, :], wide(banks[4 + h][:, :], 4), ALU.add))
                        own(dve.tensor_tensor(w["invT"][:, :, :], w["invT"][:, :, :], wide(banks[6 + h][:, :], 4), ALU.add))
                        own.tell(sems["inv_out"])
                dve.wait_ge(sems["state_mm"], c + 1)
                own(dve.tensor_tensor(S[:, :, :], S[:, :, :], wide(banks[2][:, 0:256], 4), ALU.add))
                own.settle()
                for m in range(4):
                    own(dve.tensor_scalar(S[:, m, :], S[:, m, :], core.tiny[:, 24 + 4 * m + c:25 + 4 * m + c], None, ALU.mult))
                own.settle()

        @block.gpsimd
        def _(pool):
            for c in range(NCH):
                for l in range(1, 7):
                    for h in range(2):
                        n = (c * 6 + l - 1) * 2 + h
                        w = b["work"][h]
                        if l == 1:
                            pool.wait_ge(sems["pair_out"], (2 * c + h) * 5 + 1)
                        if n >= 2:
                            pool.wait_ge(sems["x_mm"], n - 1)
                        pool.tensor_tensor(w["levelT"][:, :, :], w["negNT"][:, :, :], level(l), ALU.mult)\
                            .then_inc(sems["level_ready"], 1)

        @block.scalar
        def _(act):
            own = Own(act, sems["own_act"])
            for c in range(NCH):
                for i, name in enumerate(("Vt", "Kt", "Bt")):
                    act.wait_ge(sems["tok_mm"], 3 * c + i + 1)
                    act.copy(b[name][:, :], banks[5 + i][:, :]).then_inc(sems["tok_out"], 1)
                for l in range(1, 7):
                    for h in range(2):
                        n = (c * 6 + l - 1) * 2 + h
                        act.wait_ge(sems["x_mm"], n + 1)
                        act.copy(b["work"][h]["X"][:, :, :], wide(banks[2 + h][:, :], 4)).then_inc(sems["x_out"], 1)
                for name, ready, out, at, by in (("mix", "mix_mm", "mix_out", 0, -1.0), ("U", "u_mm", "u_out", 256, 1.0)):
                    for h in range(2):
                        act.wait_ge(sems[ready], 2 * c + h + 1)
                        act.mul(wide(b[name][:, :], 4)[:, :, 64 * h:64 * h + 64], wide(banks[h][:, at:at + 256], 4), by)\
                            .then_inc(sems[out], 1)
                act.wait_ge(sems["y_mm"], c + 1)
                act.copy(y[:, :, c * CH:(c + 1) * CH], wide(banks[3][:, :], 4)).then_inc(sems["y_out"], 1)

        @block.tensor
        def _(pe):
            for c in range(NCH):
                t = slice(c * CH, (c + 1) * CH)
                for i, src in enumerate((V, Kt, B)):
                    if c:
                        pe.wait_ge(sems["inv_out"], 12 * c)
                    for m in range(4):
                        mm = pe.transpose(banks[5 + i][:, m * P:(m + 1) * P], src[:, m, t], ident)
                    mm.then_inc(sems["tok_mm"], 1)
                for h in range(2):
                    n = 2 * c + h

                    def pairs(index, left, right):
                        if index >= 2:
                            pe.wait_ge(sems["pair_out"], 5 * n + index - 1)
                        elif n and index == 0:
                            pe.wait_ge(sems["pair_out"], 5 * n)
                            if h == 0:
                                pe.wait_ge(sems["mix_out"], 2 * c)
                                pe.wait_ge(sems["u_out"], 2 * c)
                        for m in range(4):
                            lo = 64 * h
                            mm = pe.matmul(banks[index % 2][:, m * P:(m + 1) * P], left[lo:lo + 64, m, t],
                                           right[lo:lo + 64, m, t], start=True, stop=True)
                        mm.then_inc(sems["pair_mm"], 1)

                    pairs(0, B, A)
                    pairs(1, A, B)
                    pairs(2, Kt, A)
                    pairs(3, B, R)
                    pairs(4, Kt, R)
                pe.wait_ge(sems["tok_out"], 3 * c + 3)
                for l in range(1, 7):
                    for h in range(2):
                        n = (c * 6 + l - 1) * 2 + h
                        w = b["work"][h]
                        pe.wait_ge(sems["level_ready"], n + 1)
                        if l == 1:
                            pe.wait_ge(sems["pair_out"], 10 * c + 10)
                        else:
                            pe.wait_ge(sems["inv_out"], n - 1)
                        for q in range(4):
                            mm = pe.matmul(banks[2 + h][:, q * P:(q + 1) * P], w["levelT"][:, q, :], w["inv"][:, q, :],
                                           start=True, stop=True)
                        mm.then_inc(sems["x_mm"], 1)
                    for h in range(2):
                        n = (c * 6 + l - 1) * 2 + h
                        w = b["work"][h]
                        pe.wait_ge(sems["x_out"], n + 1)
                        for q in range(4):
                            if l < 6:
                                pe.matmul(banks[4 + h][:, q * P:(q + 1) * P], w["invT"][:, q, :], w["X"][:, q, :],
                                          start=True, stop=True)
                            mm = pe.matmul(banks[6 + h][:, q * P:(q + 1) * P], w["X"][:, q, :], w["invT"][:, q, :],
                                           start=True, stop=True)
                        mm.then_inc(sems["inv_mm"], 1)
                pe.wait_ge(sems["scaled"], c + 1)
                for h in range(2):
                    w, lo = b["work"][h], 64 * h
                    for m in range(4):
                        out = banks[h][:, m * 64:(m + 1) * 64]
                        pe.matmul(out, A[lo:lo + 64, m, t], S[lo:lo + 64, m, :], start=True, stop=False)
                        mm = pe.matmul(out, w["PmT"][:, m, :], b["Vt"][:, token_major(h, m)], start=False, stop=True)
                    mm.then_inc(sems["mix_mm"], 1)
                pe.wait_ge(sems["inv_out"], 12 * c + 12)
                for h in range(2):
                    pe.wait_ge(sems["mix_out"], 2 * c + h + 1)
                    for m in range(4):
                        mm = pe.matmul(banks[h][:, 256 + m * 64:256 + (m + 1) * 64], b["work"][h]["invT"][:, m, :],
                                       b["mix"][:, token_major(h, m)], start=True, stop=True)
                    mm.then_inc(sems["u_mm"], 1)
                for h in range(2):
                    pe.wait_ge(sems["u_out"], 2 * c + h + 1)
                    w, lo = b["work"][h], 64 * h
                    for m in range(4):
                        out, at = banks[3][lo:lo + 64, m * P:(m + 1) * P], token_major(h, m)
                        pe.matmul(out, S[lo:lo + 64, m, :], R[lo:lo + 64, m, t], start=True, stop=False)
                        pe.matmul(out, b["U"][:, at], w["QbT"][:, m, :], start=False, stop=False)
                        mm = pe.matmul(out, b["Vt"][:, at], w["QkT"][:, m, :], start=False, stop=True)
                mm.then_inc(sems["y_mm"], 1)
                for h in range(2):
                    for m in range(4):
                        out, at = banks[2][64 * h:64 * h + 64, m * 64:(m + 1) * 64], token_major(h, m)
                        pe.matmul(out, b["Kt"][:, at], b["Vt"][:, at], start=True, stop=False)
                        mm = pe.matmul(out, b["Bt"][:, at], b["U"][:, at], start=False, stop=True)
                mm.then_inc(sems["state_mm"], 1)


def rwkv_finish(nc, core, b, y):
    par, con, banks = core.par, core.con, core.banks
    centred, squares, root = b["E"], b["B"], b["G"]
    with phase(nc, "mean_mm", "centred", "var_mm", "rooted", "own", "own_act") as (block, sems):
        head = con[:, CONST1["headsum"]:CONST1["headsum"] + P]

        @block.tensor
        def _(pe):
            for m in range(4):
                pe.matmul(banks[m][:, :], head, y[:, m, :], start=True, stop=True).then_inc(sems["mean_mm"], 1)
            for m in range(4):
                pe.wait_ge(sems["centred"], m + 1)
                pe.matmul(banks[4 + m][:, :], head, squares[:, m, :], start=True, stop=True).then_inc(sems["var_mm"], 1)

        @block.scalar
        def _(act):
            for m in range(4):
                act.wait_ge(sems["var_mm"], m + 1)
                act.activation(root[:, m, :], banks[4 + m][:, :], ACT.Sqrt, bias=core.eps[:, 1:2], scale=1.0 / 64)\
                    .then_inc(sems["rooted"], 1)

        @block.vector
        def _(dve):
            own = Own(dve, sems["own"])
            for m in range(4):
                dve.wait_ge(sems["mean_mm"], m + 1)
                own(dve.scalar_tensor_tensor(out=centred[:, m, :], in0=banks[m][:, :], scalar=-1.0 / 64, in1=y[:, m, :],
                                             op0=ALU.mult, op1=ALU.add))
                own.settle()
                dve.tensor_tensor(squares[:, m, :], centred[:, m, :], centred[:, m, :], ALU.mult).then_inc(sems["centred"], 1)
            dve.wait_ge(sems["rooted"], 4)
            own(dve.reciprocal(root[:, :, :], root[:, :, :]))
            own.settle()
            own(dve.tensor_tensor(centred[:, :, :], centred[:, :, :], root[:, :, :], ALU.mult))
            own.settle()
            for m in range(4):
                g, beta = PAR1["lnx_g"] + m, PAR1["lnx_b"] + m
                own(dve.tensor_scalar(centred[:, m, :], centred[:, m, :], par[:, g:g + 1], par[:, beta:beta + 1], ALU.mult, ALU.add))
            own.settle()
            own(dve.tensor_tensor(centred[:, :, :], centred[:, :, :], b["F"][:, :, :], ALU.add))
            own.settle()
            own(dve.tensor_tensor(y[:, :, :], centred[:, :, :], b["D"][:, :, :], ALU.mult))
            own.settle()


def retention(nc, core, b, y):
    con, banks, ident = core.con, core.banks, core.ident
    q, k, v, g = (b["p_rs"][:, lo:hi, :] for lo, hi in ((0, 2), (2, 4), (4, 8), (8, 12)))

    def table(name, n):
        return con[:, CONST1[name]:CONST1[name] + n]

    def block_of(name, c):
        return b[name][:, c, :]

    with phase(nc, "rot_mm", "rotated", "k_mm", "k_out", "v_mm", "v_out", "score_mm", "score_out", "kv_mm", "state_ready",
               "y_mm", "y_out", "squared", "summed", "rooted", "gated", "own", "own_act") as (block, sems):
        @block.tensor
        def _(pe):
            rot = table("rot", P)
            for i in range(4):
                src = q if i < 2 else k
                pe.matmul(banks[i][:, :], rot, src[:, i % 2, :], start=True, stop=True).then_inc(sems["rot_mm"], 1)
            for c in range(NCH):
                if c >= 2:
                    pe.wait_ge(sems["v_out"], c - 1)
                for m in range(4):
                    mm = pe.transpose(banks[4 + c % 2][:, m * P:(m + 1) * P], v[:, m, c * CH:(c + 1) * CH], ident)
                mm.then_inc(sems["v_mm"], 1)
            pe.wait_ge(sems["rotated"], 4)
            for c in range(NCH):
                t = slice(c * CH, (c + 1) * CH)
                if c >= 2:
                    pe.wait_ge(sems["k_out"], c - 1)
                for m in range(2):
                    mm = pe.transpose(banks[6 + c % 2][:, m * P:(m + 1) * P], k[:, m, t], ident)
                mm.then_inc(sems["k_mm"], 1)
                if c >= 2:
                    pe.wait_ge(sems["score_out"], 2 * (c - 1))
                if c == 1:
                    pe.wait_ge(sems["v_out"], NCH)
                for h in range(2):
                    for m in range(2):
                        mm = pe.matmul(banks[4 * (c % 2) + h][:, m * P:(m + 1) * P], k[64 * h:64 * h + 64, m, t],
                                       q[64 * h:64 * h + 64, m, t], start=True, stop=True)
                    mm.then_inc(sems["score_mm"], 1)
            for c in range(NCH):
                t = slice(c * CH, (c + 1) * CH)
                pe.wait_ge(sems["k_out"], c + 1)
                pe.wait_ge(sems["v_out"], c + 1)
                if c:
                    pe.wait_ge(sems["state_ready"], c + 1)
                if c < NCH - 1:
                    for h in range(4):
                        m, lo = h // 2, 64 * (h % 2)
                        mm = pe.matmul(banks[2][lo:lo + 64, m * P:(m + 1) * P], b["kt"][:, c, h * 64:(h + 1) * 64],
                                       b["vt"][:, c, h * P:(h + 1) * P], start=True, stop=True)
                    mm.then_inc(sems["kv_mm"], 1)
                pe.wait_ge(sems["score_out"], 2 * (c + 1))
                if c:
                    pe.wait_ge(sems["y_out"], 2 * c)
                else:
                    pe.wait_ge(sems["k_out"], NCH)
                for half in range(2):
                    for m in range(2):
                        h, lo = 2 * m + half, 64 * half
                        out = banks[3 + 4 * half][:, m * P:(m + 1) * P]
                        mm = pe.matmul(out, b["vt"][:, c, h * P:(h + 1) * P], b["scores"][:, c, h * P:(h + 1) * P],
                                       start=True, stop=(c == 0))
                        if c:
                            mm = pe.matmul(out, b["states"][lo:lo + 64, c, m * P:(m + 1) * P],
                                           b["qdec"][lo:lo + 64, m, t], start=False, stop=True)
                    mm.then_inc(sems["y_mm"], 1)
            pe.wait_ge(sems["y_out"], 2 * NCH)
            for h in range(4):
                pe.wait_ge(sems["squared"], h + 1)
                pe.matmul(banks[4 + h][:, :], core.ones[:, :], b["tmp"][:, h, :], start=True, stop=True)\
                    .then_inc(sems["summed"], 1)

        @block.scalar
        def _(act):
            for c in range(NCH):
                act.wait_ge(sems["v_mm"], c + 1)
                act.copy(b["vt"][:, c, :], banks[4 + c % 2][:, :]).then_inc(sems["v_out"], 1)
            for c in range(NCH):
                for half in range(2):
                    act.wait_ge(sems["y_mm"], 2 * c + half + 1)
                    act.copy(y[:, half::2, c * CH:(c + 1) * CH], wide(banks[3 + 4 * half][:, 0:256], 2))\
                        .then_inc(sems["y_out"], 1)
            act.activation(g, g, ACT.Silu).then_inc(sems["gated"], 1)
            for h in range(4):
                act.wait_ge(sems["summed"], h + 1)
                act.activation(b["root"][:, h, :], banks[4 + h][:, :], ACT.Sqrt, bias=core.eps[:, 0:1], scale=1.0 / P)\
                    .then_inc(sems["rooted"], 1)

        @block.vector
        def _(dve):
            own = Own(dve, sems["own"])
            scale = 64 ** -0.5
            for i in range(4):
                src = (q if i < 2 else k)[:, i % 2, :]
                by = 1.0 if i < 2 else scale
                dve.wait_ge(sems["rot_mm"], i + 1)
                own(dve.scalar_tensor_tensor(out=b["tmp"][:, i, :], in0=banks[i][:, :], scalar=by, in1=table("ret_sin", T),
                                             op0=ALU.mult, op1=ALU.mult))
                own(dve.scalar_tensor_tensor(out=src, in0=src, scalar=by, in1=table("ret_cos", T), op0=ALU.mult, op1=ALU.mult))
                own.settle()
                own(dve.tensor_tensor(src, src, b["tmp"][:, i, :], ALU.add))
                own.tell(sems["rotated"])
            own(dve.tensor_tensor(b["qdec"][:, :, :], q, wide(table("ret_qdec", 1024), 2), ALU.mult))
            kdec = table("ret_kdec", 4).rearrange("p (h o) -> p h o", o=1).to_broadcast([P, 4, 64])
            for c in range(NCH):
                dve.wait_ge(sems["k_mm"], c + 1)
                dve.tensor_tensor(wide(block_of("kt", c), 4), wide(banks[6 + c % 2][:, 0:256], 4), kdec, ALU.mult)\
                    .then_inc(sems["k_out"], 1)
                for h in range(2):
                    dve.wait_ge(sems["score_mm"], 2 * c + h + 1)
                    dve.tensor_tensor(wide(block_of("scores", c), 4)[:, h::2, :], wide(banks[4 * (c % 2) + h][:, 0:256], 2),
                                      wide(table("ret_decay", 512), 4)[:, h::2, :], ALU.mult).then_inc(sems["score_out"], 1)
            own(dve.memset(b["states"][:, 0, :], 0.0))
            own.tell(sems["state_ready"])
            for c in range(NCH - 1):
                dve.wait_ge(sems["kv_mm"], c + 1)
                for m in range(2):
                    cd = CONST1["ret_chunk"] + m
                    own(dve.scalar_tensor_tensor(out=b["states"][:, c + 1, m * P:(m + 1) * P],
                                                 in0=b["states"][:, c, m * P:(m + 1) * P], scalar=con[:, cd:cd + 1],
                                                 in1=banks[2][:, m * P:(m + 1) * P], op0=ALU.mult, op1=ALU.add))
                own.tell(sems["state_ready"])
            dve.wait_ge(sems["y_out"], 2 * NCH)
            for h in range(4):
                dve.tensor_tensor(b["tmp"][:, h, :], y[:, h, :], y[:, h, :], ALU.mult).then_inc(sems["squared"], 1)
            dve.wait_ge(sems["rooted"], 4)
            own(dve.reciprocal(b["root"][:, :, :], b["root"][:, :, :]))
            own.settle()
            own(dve.tensor_tensor(y[:, :, :], y[:, :, :], b["root"][:, :, :], ALU.mult))
            own.settle()
            dve.wait_ge(sems["gated"], 1)
            own(dve.tensor_tensor(y[:, :, :], y[:, :, :], g, ALU.mult))
            own.settle()


def spatial_gate(nc, core, b, y):
    con, par, small, banks, ident = core.con, core.par, core.small, core.banks, core.ident
    u, v = b["p_rs"][:, 12:16, :], b["p_rs"][:, 16:20, :]
    squares, root, ws, vt = b["tmp"], b["root"], b["ws"], b["vt"]
    with phase(nc, "activated", "mean_mm", "squared", "var_mm", "rooted", "normed", "t_mm", "t_out", "masked", "mix_mm",
               "own", "own_act") as (block, sems):
        @block.scalar
        def _(act):
            act.activation(v, v, ACT.Gelu).then_inc(sems["activated"], 1)
            act.activation(u, u, ACT.Gelu).then_inc(sems["activated"], 1)
            act.wait_ge(sems["var_mm"], 1)
            act.activation(root[:, 0, :], banks[1][:, :], ACT.Sqrt, bias=core.eps[:, 0:1], scale=1.0 / 512)\
                .then_inc(sems["rooted"], 1)
            for c in range(NCH):
                act.wait_ge(sems["t_mm"], c + 1)
                act.copy(vt[:, c, :], banks[2 + c % 2][:, :]).then_inc(sems["t_out"], 1)

        @block.vector
        def _(dve):
            own = Own(dve, sems["own"])
            w = small[:, SMALL1["w_sT"]:SMALL1["w_sT"] + 512]
            causal = con[:, CONST1["incl_su"]:CONST1["incl_su"] + P].rearrange("p (o t) -> p o t", o=1).to_broadcast([P, 4, P])
            own(dve.tensor_tensor(wide(ws[:, :], 4), wide(w, 4), causal, ALU.mult))
            own.tell(sems["masked"])
            dve.wait_ge(sems["mean_mm"], 1)
            for m in range(4):
                own(dve.scalar_tensor_tensor(out=v[:, m, :], in0=banks[0][:, :], scalar=-1.0 / 512, in1=v[:, m, :],
                                             op0=ALU.mult, op1=ALU.add))
            own.settle()
            for m in range(4):
                dve.tensor_tensor(squares[:, m, :], v[:, m, :], v[:, m, :], ALU.mult).then_inc(sems["squared"], 1)
            dve.wait_ge(sems["rooted"], 1)
            own(dve.reciprocal(root[:, 0, :], root[:, 0, :]))
            own.settle()
            for m in range(4):
                g = PAR1["ln_g"] + m
                own(dve.scalar_tensor_tensor(out=v[:, m, :], in0=v[:, m, :], scalar=par[:, g:g + 1], in1=root[:, 0, :],
                                             op0=ALU.mult, op1=ALU.mult))
            own.settle()
            for m in range(4):
                beta = PAR1["ln_b"] + m
                own(dve.tensor_scalar(v[:, m, :], v[:, m, :], par[:, beta:beta + 1], None, ALU.add))
            own.tell(sems["normed"])
            dve.wait_ge(sems["activated"], 2)
            for g in range(4):
                dve.wait_ge(sems["mix_mm"], g + 1)
                own(dve.tensor_tensor(y[:, g, :], u[:, g, :], banks[4 + g][:, :], ALU.mult))
            own.settle()

        @block.tensor
        def _(pe):
            pe.wait_ge(sems["activated"], 1)
            for m in range(4):
                mm = pe.matmul(banks[0][:, :], core.ones[:, :], v[:, m, :], start=(m == 0), stop=(m == 3))
            mm.then_inc(sems["mean_mm"], 1)
            for m in range(4):
                pe.wait_ge(sems["squared"], m + 1)
                mm = pe.matmul(banks[1][:, :], core.ones[:, :], squares[:, m, :], start=(m == 0), stop=(m == 3))
            mm.then_inc(sems["var_mm"], 1)
            pe.wait_ge(sems["normed"], 1)
            for c in range(NCH):
                if c >= 2:
                    pe.wait_ge(sems["t_out"], c - 1)
                for m in range(4):
                    mm = pe.transpose(banks[2 + c % 2][:, m * P:(m + 1) * P], v[:, m, c * CH:(c + 1) * CH], ident)
                mm.then_inc(sems["t_mm"], 1)
            pe.wait_ge(sems["t_out"], NCH)
            pe.wait_ge(sems["masked"], 1)
            for g in range(4):
                at = SMALL1["sg_b"] + g * P
                bias = small[0:1, at:at + P].rearrange("p (o i) -> p o i", o=1).to_broadcast([1, NCH, P])
                pe.matmul(wide(banks[4 + g][:, :], 4), core.ones[0:1, :], bias, start=True, stop=False)
                for c in range(NCH):
                    mm = pe.matmul(banks[4 + g][:, c * CH:(c + 1) * CH], vt[:, c, g * P:(g + 1) * P],
                                   ws[:, g * P:(g + 1) * P], start=False, stop=(c == NCH - 1))
                mm.then_inc(sems["mix_mm"], 1)


def merge(nc, core, layer, units, ys, highs, lows, blocks, merged, gate, part):
    n_br = len(ys)
    banks = core.banks
    width = (KD + blocks) * P
    pair = 2 * n_br
    with phase(nc, *LANDED, "landed4", "projected", "rounded", "split", "gated", "taken", "added", "y_rounded",
               "y_split") as (block, sems):
        names = LANDED + ["landed4"]

        @block.sync
        def _(sp):
            def load(n, s):
                sp.dma_start(slot(core, s, width), units[layer * (KD * n_br) + n]).then_inc(sems[names[s]], 16)

            for s in range(n_br):
                load(s, s)
            with sp.Fori(1, KD) as d:
                for s in range(n_br):
                    sp.wait_ge(sems["split"], (d - 1) * n_br + (s + 1))
                    load(d * n_br + s, s)

        @block.tensor
        def _(pe):
            def unit(u, base):
                pe.wait_ge(sems["split"], base + (u + 1))
                before = u - 1
                if not isinstance(base, int) or base + before > 0:
                    pe.wait_ge(sems["taken"], base + before)
                three_passes(pe, banks[u % 2][:, :], core, u % 2)
                s = u % n_br
                if isinstance(base, int) and u < n_br:
                    pe.wait_ge(sems["y_split"], (s + 1) * blocks)
                for k in range(blocks):
                    mm = block_passes(pe, banks[4 + u % 2][:, :], core, u % 2, KD + k, highs[s][:, k, :],
                                      lows[s][:, k, :], k == 0, k == blocks - 1)
                mm.then_inc(sems["projected"], 1)

            for u in range(pair):
                unit(u, 0)
            with pe.Fori(1, KD // 2) as dd:
                for u in range(pair):
                    unit(u, dd * pair)

        @block.scalar
        def _(act):
            def unit(u, base, landed, ahead=True):
                act.wait_ge(sems["projected"], base + (u + 1))
                if ahead:
                    a = u + 2
                    act.wait_ge(sems[names[a % n_br]], landed + 16 * (1 + a // n_br))
                    high_part(act, sems, core, (a % n_br, width), a % 2)
                if not isinstance(base, int) or base + u >= 2:
                    act.wait_ge(sems["taken"], base + (u - 1))
                else:
                    act.wait_ge(sems["y_split"], n_br * blocks)
                act.activation(gate[:, u % 2, :], banks[u % 2][:, :], ACT.Sigmoid).then_inc(sems["gated"], 1)

            for n in range(2):
                act.wait_ge(sems[names[n]], 16)
                high_part(act, sems, core, (n, width), n)
            for y, high in zip(ys, highs):
                for k in range(blocks):
                    source_high(act, y[:, k, :], high[:, k, :], sems["y_rounded"])
            for u in range(pair):
                unit(u, 0, 0)
            with act.Fori(1, KD // 2 - 1) as dd:
                for u in range(pair):
                    unit(u, dd * pair, dd * 32)
            for u in range(pair):
                unit(u, (KD // 2 - 1) * pair, (KD // 2 - 1) * 32, ahead=(u + 2 < pair))

        @block.vector
        def _(dve):
            def low(u, base):
                dve.wait_ge(sems["rounded"], base + (u + 1))
                low_part(dve, sems, core, (u % n_br, width), u % 2)

            def unit(u, base, d, added, ahead=True):
                if ahead:
                    low(u + 2, base)
                dve.wait_ge(sems["gated"], base + (u + 1))
                s = u % n_br
                to = merged[:, d, :] if s == 0 else part[:, u % 2, :]
                before = added + (u // n_br) * (n_br - 1) + max(s - 1, 0)
                if s and (not isinstance(before, int) or before > 0):
                    dve.wait_ge(sems["added"], before)
                dve.tensor_tensor(to, gate[:, u % 2, :], banks[4 + u % 2][:, :], ALU.mult).then_inc(sems["taken"], 1)
                if s:
                    dve.wait_ge(sems["taken"], base + (u + 1))
                    dve.tensor_tensor(merged[:, d, :], merged[:, d, :], part[:, u % 2, :], ALU.add).then_inc(sems["added"], 1)

            low(0, 0)
            low(1, 0)
            for u, (y, high, low_y) in enumerate(zip(ys, highs, lows)):
                for k in range(blocks):
                    dve.wait_ge(sems["y_rounded"], u * blocks + k + 1)
                    source_low(dve, y[:, k, :], high[:, k, :], low_y[:, k, :], sems["y_split"])
            dve.wait_ge(sems["y_split"], n_br * blocks)
            for u in range(pair):
                unit(u, 0, u // n_br, 0)
            with dve.Fori(1, KD // 2 - 1) as dd:
                for u in range(pair):
                    unit(u, dd * pair, dd * 2 + u // n_br, dd * (2 * (n_br - 1)))
            for u in range(pair):
                unit(u, (KD // 2 - 1) * pair, KD - 2 + u // n_br, (KD // 2 - 1) * 2 * (n_br - 1), ahead=(u + 2 < pair))
            dve.wait_ge(sems["added"], KD * (n_br - 1))


def add_projection(nc, core, layer, units, src, high, low, blocks, parts):
    x, banks = core.x, core.banks
    count = KD * parts
    core.count += 1
    with nc.sbuf_tensor(f"squares{core.count}", [P, 3, T], F32) as core.squares, \
            phase(nc, *LANDED, "projected", "rounded", "split", "src_rounded", "src_split", "added", *ROOT) as (block, sems):
        @block.sync
        def _(sp):
            stream(sp, sems, core, lambda n: units[layer * count + n], count, blocks)

        @block.tensor
        def _(pe):
            for n in range(count):
                d, half = n // parts, n % parts
                pe.wait_ge(sems["split"], n + 1)
                if d >= 4:
                    pe.wait_ge(sems["added"], d - 3)
                for k in range(blocks):
                    t = half * blocks + k
                    if d == 0 and src is not None:
                        pe.wait_ge(sems["src_split"], t + 1)
                    mm = block_passes(pe, banks[d % 4][:, :], core, n % 2, k, high[:, t, :], low[:, t, :], t == 0,
                                      t == parts * blocks - 1)
                mm.then_inc(sems["projected"], 1)
            sum_channels(pe, sems, core)

        @block.scalar
        def _(act):
            for n in range(count):
                act.wait_ge(sems[LANDED[n % RING]], 16 * (n // RING + 1))
                if n >= 2:
                    act.wait_ge(sems["projected"], n - 1)
                high_part(act, sems, core, (n % RING, blocks * P), n % 2)
                if n < parts and src is not None:
                    for k in range(n * blocks, (n + 1) * blocks):
                        source_high(act, src[:, k, :], high[:, k, :], sems["src_rounded"])
                d = n // parts - 2
                if n % parts == parts - 1 and d >= 0:
                    act.wait_ge(sems["added"], d + 1)
                    square_tile(act, sems, core, d)
            for d in (KD - 2, KD - 1):
                act.wait_ge(sems["added"], d + 1)
                square_tile(act, sems, core, d)
            take_root(act, sems, core)

        @block.vector
        def _(dve):
            for n in range(count + parts):
                if n < count:
                    dve.wait_ge(sems["rounded"], n + 1)
                    low_part(dve, sems, core, (n % RING, blocks * P), n % 2)
                if n < parts and src is not None:
                    for k in range(n * blocks, (n + 1) * blocks):
                        dve.wait_ge(sems["src_rounded"], k + 1)
                        source_low(dve, src[:, k, :], high[:, k, :], low[:, k, :], sems["src_split"])
                d = n // parts - 1
                if n % parts == parts - 1 and d >= 0:
                    dve.wait_ge(sems["projected"], parts * (d + 1))
                    dve.tensor_tensor(x[:, d, :], x[:, d, :], banks[d % 4][:, :], ALU.add).then_inc(sems["added"], 1)
                    if d >= 3:
                        sum_tile(dve, sems, core, d - 2)
            sum_tile(dve, sems, core, KD - 2)
            invert_root(dve, sems, core)


def ffn_up(nc, core, layer, units, conv, high, low, tmp):
    par, banks = core.par, core.banks
    count = 2 * FFN_TILES
    with phase(nc, *LANDED, "projected", "evacuated", "rounded", "split", *NORM, "tapped", "silu", "own",
               "product", "f_rounded", "f_split") as (block, sems):
        @block.sync
        def _(sp):
            stream(sp, sems, core, lambda n: units[layer * count + n], count)

        @block.tensor
        def _(pe):
            project(pe, sems, core, count, sems["normed"])

        def tap(j, n):
            at = PAR1["conv"] + j * count + n
            return par[:, at:at + 1]

        @block.scalar
        def _(act):
            norm_round(act, sems, core, tmp)

            def silu(j):
                act.wait_ge(sems["evacuated"], 2 * j + 1)
                act.activation(conv[:, 2 * j % 4, :], conv[:, 2 * j % 4, :], ACT.Silu).then_inc(sems["silu"], 1)

            def high_product(j):
                act.wait_ge(sems["product"], j + 1)
                source_high(act, conv[:, 2 * j % 4, :], high[:, j, :], sems["f_rounded"])

            for n in range(count):
                j = n // 2
                act.wait_ge(sems["projected"], n + 1)
                if n + 2 < count:
                    act.wait_ge(sems[LANDED[(n + 2) % RING]], 16 * (1 + (n + 2) // RING))
                    high_part(act, sems, core, ((n + 2) % RING, KD * P), n % 2)
                if n >= 4:
                    act.wait_ge(sems["f_split"], j - 1)
                elif n == 0:
                    act.wait_ge(sems["normed"], KD)
                at = PAR1["conv_b"] + n
                act.activation(conv[:, n % 4, :], banks[n % 4][:, :], ACT.Identity, bias=par[:, at:at + 1], scale=tap(2, n))\
                    .then_inc(sems["tapped"], 1)
                if n % 2 and j:
                    silu(j - 1)
                    high_product(j - 1)
            silu(FFN_TILES - 1)
            high_product(FFN_TILES - 1)

        @block.vector
        def _(dve):
            own = Own(dve, sems["own"])

            def low_weights(n):
                dve.wait_ge(sems["rounded"], n + 1)
                low_part(dve, sems, core, (n % RING, KD * P), n % 2)

            norm_split(dve, sems, core, par[:, PAR1["norm2"]:PAR1["norm2"] + 8], tmp)

            def product(j):
                dve.wait_ge(sems["silu"], j + 1)
                c = conv[:, 2 * j % 4, :]
                dve.tensor_tensor(c, c, conv[:, (2 * j + 1) % 4, :], ALU.mult).then_inc(sems["product"], 1)

            def low_product(j):
                dve.wait_ge(sems["f_rounded"], j + 1)
                source_low(dve, conv[:, 2 * j % 4, :], high[:, j, :], low[:, j, :], sems["f_split"])

            for n in range(count):
                bank, c = banks[n % 4], conv[:, n % 4, :]
                if n + 2 < count:
                    low_weights(n + 2)
                dve.wait_ge(sems["tapped"], n + 1)
                own(dve.scalar_tensor_tensor(out=c[:, 1:], in0=bank[:, 0:T - 1], scalar=tap(1, n), in1=c[:, 1:],
                                             op0=ALU.mult, op1=ALU.add))
                own.settle()
                dve.scalar_tensor_tensor(out=c[:, 2:], in0=bank[:, 0:T - 2], scalar=tap(0, n), in1=c[:, 2:],
                                         op0=ALU.mult, op1=ALU.add).then_inc(sems["evacuated"], 1)
                if n % 2 and n > 1:
                    product(n // 2 - 1)
                    low_product(n // 2 - 1)
            dve.wait_ge(sems["evacuated"], count)
            product(FFN_TILES - 1)
            low_product(FFN_TILES - 1)
            dve.wait_ge(sems["f_split"], FFN_TILES)


def final_norm(nc, core, gain, again):
    core.count += 1
    with nc.sbuf_tensor(f"squares{core.count}", [P, 3, T], F32) as core.squares, phase(nc, "normed", *ROOT) as (block, sems):
        @block.vector
        def _(dve):
            for k in range(KD):
                dve.scalar_tensor_tensor(out=core.x[:, k, :], in0=core.x[:, k, :], scalar=gain[:, k:k + 1],
                                         in1=core.root[:, :], op0=ALU.mult, op1=ALU.mult).then_inc(sems["normed"], 1)
                if again and k >= 2:
                    sum_tile(dve, sems, core, k - 1)
            if again:
                dve.wait_ge(sems["normed"], KD)
                invert_root(dve, sems, core)
            else:
                dve.wait_ge(sems["normed"], KD)

        if again:
            root_of_x(block, sems, core, sems["normed"])


def root_of_x(block, sems, core, ready=None):
    @block.scalar
    def _(act):
        for d in range(KD):
            if ready is not None:
                act.wait_ge(ready, d + 1)
            square_tile(act, sems, core, d)
        take_root(act, sems, core)

    @block.tensor
    def _(pe):
        sum_channels(pe, sems, core)


@contextmanager
def split_weights(nc, core, blocks=KD):
    core.count = core.count + 1
    with nc.sbuf_tensor(f"weights_high{core.count}", [P, 2, blocks * P], F32R) as core.wh, \
            nc.sbuf_tensor(f"weights_low{core.count}", [P, 2, blocks * P], F32R) as core.wl:
        yield


def block1_layer(nc, core, layer, w):
    with ExitStack() as outer:
        def buf(stack, name, shape, dt=F32):
            return stack.enter_context(nc.sbuf_tensor(name, [P] + shape, dt))

        core.small, core.con = buf(outer, "small1_sb", [NSMALL1]), buf(outer, "con1_sb", [NCONST1])
        core.ident = core.con[:, CONST1["ident"]:CONST1["ident"] + P]
        core.hh, core.hl = buf(outer, "h_high1", [KD, T], F32R), buf(outer, "h_low1", [KD, T], F32R)
        y_rw = buf(outer, "y_rw", [4, T])
        with ExitStack() as stack:
            b = {"p_rw": buf(stack, "p_rw", [RW_TILES, T + 1])}
            with split_weights(nc, core), nc.sbuf_tensor("norm_tmp1", [P, 4, T], F32) as tmp:
                project_h(nc, core, lambda n: w["in1"][layer * IN1_TILES + n], RW_TILES, ((RW_TILES, lambda n: b["p_rw"][:, n, 1:]),),
                          core.par[:, PAR1["norm1"]:PAR1["norm1"] + 8], tmp,
                          ((core.par[:, 0:NPAR1], w["par1"][layer]), (core.small[:, :], w["small1"][layer]),
                           (core.con[:, :], w["con1"])))
            for name in "ACDF":
                b[name] = buf(stack, f"rw_{name}", [4, T])
            with ExitStack() as scratch:
                for name in "BEGH":
                    b[name] = buf(scratch, f"rw_{name}", [4, T])
                rwkv_prepare(nc, core, b)
            with ExitStack() as scratch:
                b["state"] = buf(scratch, "rw_state", [4, 64])
                for name in ("Vt", "Kt", "Bt", "mix", "U"):
                    b[name] = buf(scratch, f"rw_{name}_", [T])
                b["work"] = [{name: buf(scratch, f"{name}{h}", [4, P])
                              for name in ("negNT", "inv", "invT", "levelT", "X")} for h in range(2)]
                for h in range(2):
                    for i, name in enumerate(("PmT", "QbT", "QkT")):
                        at = (3 * h + i) * T
                        b["work"][h][name] = wide(core.ring[:, at:at + T], 4)
                rwkv_scan(nc, core, b, y_rw)
            with ExitStack() as scratch:
                for name in "BEG":
                    b[name] = buf(scratch, f"rwf_{name}", [4, T])
                rwkv_finish(nc, core, b, y_rw)
        y_rs = buf(outer, "y_rs", [8, T])
        with ExitStack() as stack:
            b = {"p_rs": buf(stack, "p_rs", [RET_TILES + SG_TILES, T])}
            with split_weights(nc, core):
                project_h(nc, core, lambda n: w["in1"][layer * IN1_TILES + RW_TILES + n], RET_TILES + SG_TILES,
                          ((RET_TILES + SG_TILES, lambda n: b["p_rs"][:, n, :]),))
            b["tmp"] = buf(stack, "rs_tmp", [4, T])
            b["root"] = buf(stack, "rs_root", [4, T])
            b["vt"] = core.ring[:, 0:4 * T].rearrange("p (c n) -> p c n", c=NCH)
            b["scores"] = core.ring[:, 4 * T:8 * T].rearrange("p (c n) -> p c n", c=NCH)
            b["ws"] = buf(stack, "rs_ws", [T])
            with ExitStack() as scratch:
                b["kt"] = buf(scratch, "ret_kt", [NCH, 256])
                b["states"] = buf(scratch, "ret_states", [NCH, 256])
                b["qdec"] = buf(scratch, "ret_q", [2, T])
                retention(nc, core, b, y_rs[:, 0:4, :])
            spatial_gate(nc, core, b, y_rs[:, 4:8, :])
        merged, gate, part = y_rs, y_rw[:, 0:2, :], y_rw[:, 2:4, :]
        with split_weights(nc, core, KD + 4), nc.sbuf_tensor("y_high1", [P, 12, T], F32R) as y_high, \
                nc.sbuf_tensor("y_low1", [P, 12, T], F32R) as y_low:
            merge(nc, core, layer, w["merge1"], [y_rw, y_rs[:, 0:4, :], y_rs[:, 4:8, :]],
                  [y_high[:, 4 * n:4 * n + 4, :] for n in range(3)], [y_low[:, 4 * n:4 * n + 4, :] for n in range(3)],
                  4, merged, gate, part)
        with split_weights(nc, core), nc.sbuf_tensor("merged_high1", [P, KD, T], F32R) as high, \
                nc.sbuf_tensor("merged_low1", [P, KD, T], F32R) as low:
            add_projection(nc, core, layer, w["out1"], merged, high, low, KD, 1)
    with nc.sbuf_tensor("ffn_high", [P, FFN_TILES, T], F32R) as f_high, nc.sbuf_tensor("ffn_low", [P, FFN_TILES, T], F32R) as f_low:
        with nc.sbuf_tensor("h_high2", [P, KD, T], F32R) as core.hh, nc.sbuf_tensor("h_low2", [P, KD, T], F32R) as core.hl, \
                nc.sbuf_tensor("conv", [P, 4, T], F32) as conv, split_weights(nc, core):
            ffn_up(nc, core, layer, w["up1"], conv, f_high, f_low, conv)
        with split_weights(nc, core, 11):
            add_projection(nc, core, layer, w["down1"], None, f_high, f_low, 11, 2)


def by_tiles(w, rows):
    L, _, n = w.shape
    return w.reshape(L, rows, P, n // P, P).transpose(0, 3, 2, 1, 4)


def vectors(v):
    return v.reshape(v.shape[0], -1, P).transpose(0, 2, 1)


def layout1(i):
    w_in = i["w_in"]
    n_in = IN1_TILES * P
    a = {}
    a["in1"] = by_tiles(w_in[:, :, :n_in], KD).reshape(-1, P, KD * P)
    gates = by_tiles(w_in[:, :, n_in:], KD).reshape(DEPTH, 3, KD, P, KD, P)
    wb = i["w_branch"]
    branch = np.stack([by_tiles(wb[:, n], 4) for n in range(3)], 1)
    a["merge1"] = np.concatenate([gates, branch], 4).transpose(0, 2, 1, 3, 4, 5).reshape(-1, P, 12 * P)
    a["out1"] = by_tiles(i["w_out"], KD).reshape(-1, P, KD * P)
    up = by_tiles(i["ffn_w_up"], KD).reshape(DEPTH, 2, FFN_TILES, P, KD * P).transpose(0, 2, 1, 3, 4)
    a["up1"] = up.reshape(-1, P, KD * P)
    down = by_tiles(i["ffn_w_down"], FFN_TILES).reshape(DEPTH, KD, P, 2, 11 * P).transpose(0, 1, 3, 2, 4)
    a["down1"] = down.reshape(-1, P, 11 * P)

    def interleave(v):
        return v.reshape(DEPTH, P, 2, FFN_TILES).transpose(0, 1, 3, 2).reshape(DEPTH, P, 2 * FFN_TILES)

    cols = [vectors(i["norm1_g"]), vectors(i["rw_mu"])]
    cols += [vectors(i[n]) for n in ("rw_w0", "rw_a0", "rw_k_k", "rw_k_a")]
    cols += [vectors(i[n].reshape(DEPTH, -1)) for n in ("rw_r_k", "rw_lnx_g", "rw_lnx_b")]
    cols += [vectors(i["sg_ln_g"]), vectors(i["sg_ln_b"]), vectors(i["norm2_g"])]
    cols += [interleave(vectors(i["ffn_conv_w"][:, j])) for j in range(3)] + [interleave(vectors(i["ffn_conv_b"]))]
    a["par1"] = np.concatenate(cols, 2)
    lora = np.concatenate([i["rw_w_up"], i["rw_a_up"]], 1)
    w_sT = i["sg_w_s"].transpose(0, 3, 1, 2).reshape(DEPTH, P, 512)
    sg_b = np.broadcast_to(i["sg_b"].reshape(DEPTH, 1, 512), (DEPTH, P, 512))
    a["small1"] = np.concatenate([lora, i["rw_g_up"], w_sT, sg_b], 2)
    return a


TILES2 = {name: i for i, name in enumerate((
    "dsa_q", "dsa_q1", "fox_q", "fox_q1", "sb_q", "sb_q1", "nsa_q", "nsa_q1", "mem_q", "mem_q1", "ckv", "idx_q", "idx_k",
    "dsa_z", "dsa_z1", "fox_k", "fox_k1", "fox_z", "fox_z1", "sb_k", "sb_k1", "sb_z", "sb_z1", "kc_vc", "ks", "kw",
    "nsa_z", "nsa_z1", "mem_z", "mem_z1", "fox_v", "fox_v1", "sb_v", "sb_v1", "vs_vw", "scalars"))}
Q_TILES = 12
IN2_TILES = len(TILES2)
N_BR2 = 5
NH = 4
IDX_W, NSA_G, FOX_F = 0, 4, 16
N_SCALARS = 20
N_MEM = 256
CMP_LEN, CMP_STRIDE = 32, 16
N_CMP = (T - CMP_LEN) // CMP_STRIDE + 1
SELECTED = min(256, T // 4)
IDX_SCALE = (32 ** -0.5) * (4 ** -0.5)
TAKEN = -3e38
SCALE = 64 ** -0.5

PAR2, NPAR2 = offsets([("norm", 8), ("kv_norm", 1), ("fox_b", 4), ("mem_norm", 8)])
SMALL2, NSMALL2 = offsets([("w_uk", 256), ("w_uv", 256), ("pe", 32), ("w2_k", 128), ("w2_v", 64)])
CONST2, NCONST2 = offsets([("ident", 128), ("rot64", 128), ("rot32", 128), ("causal", 896), ("after", 896), ("cmp", 128),
                           ("suffix", 128), ("strict01", 128), ("strict_neg", 128), ("sel", 512), ("inv", 2)])


def constants2():
    c = np.zeros((P, NCONST2), np.float32)

    def put(name, a):
        a = np.asarray(a, np.float32).reshape(P, -1)
        c[:, CONST2[name]:CONST2[name] + a.shape[1]] = a

    i, j = np.arange(P)[:, None], np.arange(P)[None, :]
    at = np.arange(896)[None, :] - 384
    put("ident", i == j)
    put("rot64", rotation(64))
    put("rot32", rotation(32))
    put("causal", np.where(at <= i, 0.0, NEG))
    put("after", at >= i)
    ends = np.arange(32) * CMP_STRIDE + CMP_LEN - 1
    tok = np.arange(4)[None, :, None] * P + i[:, :, None]
    put("cmp", np.where(ends[None, None, :] <= tok, 0.0, NEG))
    put("suffix", i >= j)
    put("strict01", i < j)
    put("strict_neg", np.where(i < j, 0.0, NEG))
    sel = np.zeros((P, 4, P), np.float32)
    for h in range(4):
        sel[h, h] = 1.0
    put("sel", sel)
    inv = np.stack([10000.0 ** (-np.float32(2.0) * (np.arange(P) % (w // 2)).astype(np.float32) / np.float32(w))
                    for w in (64, 32)], 1)
    put("inv", inv)
    return c


def rope_tables(nc, core, con, tables, positions):
    turn = 2 * np.pi
    high = 6.28125
    middle = float(np.float32(int((turn - high) * 2 ** 22) / 2 ** 22))
    low = turn - high - middle
    with phase(nc, "loaded", "reduced", "own") as (block, sems), \
            nc.sbuf_tensor("pos_i", [P, T], I32) as whole, nc.sbuf_tensor("angles", [P, 4, T], F32) as angle, \
            nc.sbuf_tensor("turns", [P, T], F32) as turns:
        @block.sync
        def _(sp):
            sp.dma_start(whole[:, :], positions.to_broadcast([P, T])).then_inc(sems["loaded"], 16)

        @block.vector
        def _(dve):
            own = Own(dve, sems["own"])
            dve.wait_ge(sems["loaded"], 16)
            own(dve.tensor_copy(turns[:, :], whole[:, :]))
            own.settle()
            for n in range(4):
                inv = con[:, CONST2["inv"] + n // 2:CONST2["inv"] + n // 2 + 1]
                own(dve.tensor_scalar(angle[:, n, :], turns[:, :], inv, None, ALU.mult))
            own.settle()
            for n in range(4):
                a = angle[:, n, :]
                quarter = 0.25 if n % 2 == 0 else 0.0
                own(dve.tensor_scalar(turns[:, :], a, float(1 / turn), quarter, ALU.mult, ALU.add))
                own.settle()
                own(dve.tensor_copy(whole[:, :], turns[:, :]))
                own.settle()
                own(dve.tensor_copy(turns[:, :], whole[:, :]))
                own.settle()
                for part in (high, middle, low):
                    own(dve.scalar_tensor_tensor(out=a, in0=turns[:, :], scalar=-part, in1=a, op0=ALU.mult, op1=ALU.add))
                    own.settle()
                if quarter:
                    own(dve.tensor_scalar(a, a, float(np.pi / 2), None, ALU.add))
                    own.settle()
                for test, by in ((ALU.is_gt, -1.0), (ALU.is_lt, 1.0)):
                    own(dve.tensor_scalar(turns[:, :], a, -by * float(np.pi), by * turn, test, ALU.mult))
                    own.settle()
                    own(dve.tensor_tensor(a, a, turns[:, :], ALU.add))
                    own.settle()
                own(dve.tensor_scalar(a, a, 3.1415925, -3.1415925, ALU.min, ALU.max))
                own.settle()
            own.tell(sems["reduced"])

        @block.scalar
        def _(act):
            act.wait_ge(sems["reduced"], 1)
            act.activation(tables[:, :, :], angle[:, :, :], ACT.Sin)


def prepare2(nc, core, b, p):
    con, small, par, banks, tables = b["con"], core.small, core.par, core.banks, b["tables"]
    tl = TILES2

    def table(name, n):
        return con[:, CONST2[name]:CONST2[name] + n]

    rot64, rot32 = table("rot64", P), table("rot32", P)
    ckv, ka = p[:, tl["ckv"], :], b["dsa_k"]
    turning = [(p[:, tl[n], :], rot64, 0, P) for n in ("dsa_q", "dsa_q1", "nsa_q", "nsa_q1", "ks", "kw")]
    turning += [(p[:, tl[n], :], rot32, 2, P) for n in ("idx_q", "idx_k")]
    turning += [(p[:, tl["kc_vc"], :], rot64, 0, 64)]
    turning += [(ka[:, m, :], rot64, 0, P) for m in range(2)]
    n_turn = len(turning)
    f, fa, lf = b["tm_s"][:, :, FOX_F:FOX_F + 4], b["f_abs"], b["f_log"]
    wm = w1 = core.ring
    half_w = 2 * KD * P
    mem, mem_tmp = b["mem"], wide(core.ring[:, 2 * half_w:2 * half_w + 4 * N_MEM], 4)
    squares = core.ring[:, 2 * half_w + 4 * N_MEM:2 * half_w + 4 * N_MEM + T]
    mem_root = core.ring[:, 2 * half_w + 4 * N_MEM + T:2 * half_w + 5 * N_MEM + T]
    placed = b["turn"][:, :, :].rearrange("p a t -> p (a t)")
    with phase(nc, "mem_landed", "wm_landed0", "wm_landed1", "turn_mm", "turn_out", "squared", "sum_steps", "rooted", "normed", "mk_mm",
               "mk_out", "mv_mm", "mv_out", "w1_landed0", "w1_landed1", "ckv_squared", "ckv_sum", "ckv_rooted", "ckv_normed", "ka_mm", "ka_out", "va_mm", "va_out",
               "rot_mm", "turned", "placed", "hid_mm", "hid_silu", "hid_turned", "hid_out", "cmp_mm", "f_biased", "f_exped", "f_logged", "cum_mm",
               "own", "own_act") as (block, sems):
        @block.sync
        def _(sp):
            sp.dma_start(mem[:, :, :], b["mem_dram"]).then_inc(sems["mem_landed"], 16)
            for m in range(2):
                part = slice(m * half_w, (m + 1) * half_w)
                sp.dma_start(wm[:, part], b["wm_dram"][:, part]).then_inc(sems[f"wm_landed{m}"], 16)
            for m, used in enumerate(("mk_mm", "mv_mm")):
                part = slice(m * half_w, (m + 1) * half_w)
                sp.wait_ge(sems[used], 1)
                sp.dma_start(w1[:, part], b["w1_dram"][:, part]).then_inc(sems[f"w1_landed{m}"], 16)

        @block.tensor
        def _(pe):
            for i in range(4):
                mm = pe.transpose(banks[1][:, i * P:(i + 1) * P], p[:, tl["scalars"], i * P:(i + 1) * P], core.ident2)
            mm.then_inc(sems["turn_mm"], 1)
            pe.wait_ge(sems["ckv_squared"], 1)
            pe.matmul(banks[7][:, :], core.ones[:, :], squares, start=True, stop=True).then_inc(sems["ckv_sum"], 1)
            pe.matmul(banks[0][:, :], turning[0][1], turning[0][0], start=True, stop=True).then_inc(sems["rot_mm"], 1)
            for i in range(4):
                for m in range(4):
                    pe.transpose(banks[2 + i][:, m * P:(m + 1) * P], p[:, tl["fox_v"] + m, i * P:(i + 1) * P], core.ident2)
                mm = pe.transpose(banks[6][:, i * P:(i + 1) * P], p[:, tl["vs_vw"], i * P:(i + 1) * P], core.ident2)
            mm.then_inc(sems["turn_mm"], 1)
            pe.wait_ge(sems["turn_out"], 1)

            def memory_keys(m):
                for k in range(KD):
                    mm = pe.matmul(banks[6][:, m * 256:(m + 1) * 256], wm[:, (m * KD + k) * P:(m * KD + k + 1) * P],
                                   mem[:, k, :], start=(k == 0), stop=(k == KD - 1))
                return mm

            for n, (x, rot, _, _) in enumerate(turning):
                if n == 3:
                    pe.wait_ge(sems["ckv_rooted"], 1)
                    for k in range(KD):
                        pe.wait_ge(sems["squared"], k + 1)
                        pe.matmul(banks[7][:, 0:N_MEM], core.ones[:, :], mem_tmp[:, k % 4, :], start=(k == 0),
                                  stop=(k == KD - 1)).then_inc(sems["sum_steps"], 1)
                if n == 8:
                    pe.wait_ge(sems["normed"], KD)
                    pe.wait_ge(sems["wm_landed0"], 16)
                    pe.wait_ge(sems["turn_out"], 2)
                    memory_keys(0)
                if n == n_turn - 2:
                    memory_keys(1).then_inc(sems["mk_mm"], 1)
                    pe.wait_ge(sems["ckv_normed"], 1)
                    for m in range(2):
                        at = SMALL2["w_uk"] + m * P
                        pe.matmul(banks[3 + m][:, :], small[:, at:at + P], ckv, start=True, stop=True)\
                            .then_inc(sems["ka_mm"], 1)
                    for i in range(4):
                        at = SMALL2["w_uv"]
                        mm = pe.matmul(banks[(2, 5)[i // 2]][:, (i % 2) * 256:(i % 2) * 256 + 256], ckv[:, i * P:(i + 1) * P],
                                       small[:, at:at + 256], start=True, stop=True)
                    mm.then_inc(sems["va_mm"], 1)
                    pe.wait_ge(sems["ka_out"], 2)
                if n >= 2:
                    pe.wait_ge(sems["turned"], n - 1)
                if n:
                    pe.matmul(banks[n % 2][:, :], rot, x, start=True, stop=True).then_inc(sems["rot_mm"], 1)
            pe.wait_ge(sems["wm_landed1"], 16)
            pe.wait_ge(sems["rooted"], 1)
            for m in range(2):
                for k in range(KD):
                    at = half_w + k * 256
                    mm = pe.matmul(banks[7][:, m * 256:(m + 1) * 256], mem[:, k, m * P:(m + 1) * P], wm[:, at:at + 256],
                                   start=(k == 0), stop=(k == KD - 1))
            mm.then_inc(sems["mv_mm"], 1)
            pe.wait_ge(sems["placed"], 1)
            pe.wait_ge(sems["va_out"], 1)
            for j in range(CMP_LEN):
                if j % (CMP_LEN // 2) == 0:
                    pe.wait_ge(sems[f"w1_landed{j // (CMP_LEN // 2)}"], 16)
                for half in range(2):
                    lo = 64 * half
                    mm = pe.matmul(banks[2 + half][0:N_CMP, 0:P], placed[lo:lo + 64, j * N_CMP:(j + 1) * N_CMP],
                                   w1[lo:lo + 64, j * P:(j + 1) * P], start=(j == 0), stop=(j == CMP_LEN - 1))
                    if j == CMP_LEN - 1:
                        mm.then_inc(sems["hid_mm"], 1)
            pe.wait_ge(sems["mk_out"], 1)
            for half in range(2):
                pe.wait_ge(sems["hid_silu"], half + 1)
                pe.transpose(banks[5 + half][:, 0:N_CMP], b["hidden_t"][0:N_CMP, half, :], core.ident2[0:N_CMP, 0:N_CMP])\
                    .then_inc(sems["hid_turned"], 1)
            pe.wait_ge(sems["hid_out"], 2)
            pe.matmul(banks[4][:, 0:N_CMP], small[:, SMALL2["w2_k"]:SMALL2["w2_k"] + P], b["hidden"][:, 0, 0:N_CMP],
                      start=True, stop=True)
            pe.matmul(banks[4][0:N_CMP, 64:128], b["hidden"][:, 1, 0:N_CMP], small[:, SMALL2["w2_v"]:SMALL2["w2_v"] + 64],
                      start=True, stop=True).then_inc(sems["cmp_mm"], 1)
            pe.wait_ge(sems["f_logged"], 1)
            pe.wait_ge(sems["mv_out"], 1)
            for j in range(4):
                at = CONST2["after"] + 384 - j * P
                mm = pe.matmul(banks[7][0:4, :], lf[:, j, :], con[:, at:at + T], start=(j == 0), stop=(j == 3))
            mm.then_inc(sems["cum_mm"], 1)

        @block.scalar
        def _(act):
            own = Own(act, sems["own_act"])
            act.activation(squares, ckv, ACT.Square).then_inc(sems["ckv_squared"], 1)
            act.wait_ge(sems["turn_mm"], 1)
            act.copy(p[:, tl["scalars"], :], banks[1][:, :]).then_inc(sems["turn_out"], 1)
            act.wait_ge(sems["ckv_sum"], 1)
            act.activation(core.root[:, :], banks[7][:, :], ACT.Sqrt, bias=core.eps[:, 0:1], scale=1.0 / P)\
                .then_inc(sems["ckv_rooted"], 1)
            act.wait_ge(sems["turn_mm"], 2)
            for i in range(4):
                own(act.copy(p[:, tl["fox_v"] + i, :], banks[2 + i][:, :]))
            own(act.copy(p[:, tl["vs_vw"], :], banks[6][:, :]))
            own.tell(sems["turn_out"])
            act.wait_ge(sems["mem_landed"], 16)
            for k in range(KD):
                if k >= 4:
                    act.wait_ge(sems["sum_steps"], k - 3)
                act.activation(mem_tmp[:, k % 4, :], mem[:, k, :], ACT.Square).then_inc(sems["squared"], 1)
            act.wait_ge(sems["sum_steps"], KD)
            act.activation(mem_root, banks[7][:, 0:N_MEM], ACT.Sqrt, bias=core.eps[:, 0:1], scale=1.0 / D)\
                .then_inc(sems["rooted"], 1)
            act.wait_ge(sems["f_biased"], 1)
            own(act.activation(fa[:, :, :], lf[:, :, :], ACT.Abs))
            own.settle()
            own(act.activation(fa[:, :, :], fa[:, :, :], ACT.Exp, scale=-1.0))
            own.settle()
            own(act.activation(fa[:, :, :], fa[:, :, :], ACT.Ln, bias=core.ones[:, 0:1]))
            own.tell(sems["f_exped"])
            own(act.activation(b["tm_s"][:, :, NSA_G:NSA_G + 12], b["tm_s"][:, :, NSA_G:NSA_G + 12], ACT.Sigmoid))
            for name in ("dsa_z", "fox_z", "sb_z", "nsa_z", "mem_z"):
                z = p[:, tl[name]:tl[name] + 2, :]
                own(act.activation(z, z, ACT.Silu))
            act.wait_ge(sems["mk_mm"], 1)
            act.copy(b["mem_k"][:, :, :], wide(banks[6][:, :], 2)).then_inc(sems["mk_out"], 1)
            for m in range(2):
                act.wait_ge(sems["ka_mm"], m + 1)
                act.copy(ka[:, m, :], banks[3 + m][:, :]).then_inc(sems["ka_out"], 1)
            act.wait_ge(sems["va_mm"], 1)
            for i in range(2):
                own(act.copy(b["dsa_v"][:, 2 * i:2 * i + 2, :], wide(banks[(2, 5)[i]][:, :], 2)))
            own.tell(sems["va_out"])
            act.wait_ge(sems["mv_mm"], 1)
            act.copy(b["mem_v"][:, :, :], wide(banks[7][:, :], 2)).then_inc(sems["mv_out"], 1)
            for half in range(2):
                act.wait_ge(sems["hid_mm"], half + 1)
                act.activation(b["hidden_t"][0:N_CMP, half, :], banks[2 + half][0:N_CMP, 0:P], ACT.Silu)\
                    .then_inc(sems["hid_silu"], 1)
            act.wait_ge(sems["cmp_mm"], 1)
            own(act.copy(b["cmp_k"][:, :], banks[4][:, 0:N_CMP]))
            own(act.copy(b["cmp_v"][:, :], banks[4][0:N_CMP, 64:128]))
            own.settle()

        @block.vector
        def _(dve):
            own = Own(dve, sems["own"])
            dve.wait_ge(sems["turn_out"], 1)
            fb = par[:, PAR2["fox_b"]:PAR2["fox_b"] + 4].rearrange("p (o h) -> p o h", o=1).to_broadcast([P, 4, 4])
            own(dve.tensor_tensor(lf[:, :, :], f, fb, ALU.add))
            own.tell(sems["f_biased"])
            dve.wait_ge(sems["ckv_rooted"], 1)
            own(dve.reciprocal(core.root[:, :], core.root[:, :]))
            own.settle()
            own(dve.scalar_tensor_tensor(out=ckv, in0=ckv, scalar=par[:, PAR2["kv_norm"]:PAR2["kv_norm"] + 1],
                                         in1=core.root[:, :], op0=ALU.mult, op1=ALU.mult))
            own.tell(sems["ckv_normed"])
            for n, (x, _, at, rows) in enumerate(turning):
                if n == 4:
                    norm_scale(dve, sems, own, mem, mem_root, par[:, PAR2["mem_norm"]:PAR2["mem_norm"] + 8], mem)
                if n == n_turn - 2:
                    dve.wait_ge(sems["ka_out"], 2)
                dve.wait_ge(sems["rot_mm"], n + 1)
                s = b["turn"][:, n % 2, :]
                own(dve.tensor_tensor(s[0:rows, :], banks[n % 2][0:rows, :], tables[0:rows, at + 1, :], ALU.mult))
                own(dve.tensor_tensor(x[0:rows, :], x[0:rows, :], tables[0:rows, at, :], ALU.mult))
                own.settle()
                own(dve.tensor_tensor(x[0:rows, :], x[0:rows, :], s[0:rows, :], ALU.add))
                own.tell(sems["turned"])
            x = p[:, tl["kc_vc"], :]
            windows = bass.AP(tensor=x.tensor, offset=x.offset, ap=[list(x.ap[0]), [1, CMP_LEN], [CMP_STRIDE, N_CMP]])
            pos = small[:, SMALL2["pe"]:SMALL2["pe"] + CMP_LEN].rearrange("p (j o) -> p j o", o=1)
            own(dve.tensor_tensor(placed[:, 0:CMP_LEN * N_CMP].rearrange("p (j n) -> p j n", j=CMP_LEN), windows,
                                  pos.to_broadcast([P, CMP_LEN, N_CMP]), ALU.add))
            own.tell(sems["placed"])
            dve.wait_ge(sems["f_exped"], 1)
            own(dve.scalar_tensor_tensor(out=lf[:, :, :], in0=lf[:, :, :], scalar=0.0, in1=fa[:, :, :], op0=ALU.min,
                                         op1=ALU.subtract))
            own.tell(sems["f_logged"])
            for half in range(2):
                dve.wait_ge(sems["hid_turned"], half + 1)
                dve.tensor_copy(b["hidden"][:, half, 0:N_CMP], banks[5 + half][:, 0:N_CMP]).then_inc(sems["hid_out"], 1)
            dve.wait_ge(sems["cum_mm"], 1)
            own(dve.tensor_scalar(b["cum"][0:4, 0, :], banks[7][0:4, :], 1.0 / SCALE, None, ALU.mult))
            own(dve.tensor_scalar(b["cum"][0:4, 1, :], banks[7][0:4, :], -1.0 / SCALE, None, ALU.mult))
            own.settle()


def attention(nc, core, b, parts):
    banks, ident = core.banks, core.ident2
    stats, probs, turned, score = b["stats"], b["probs"], b["probsT"], b["score"]
    n_parts = len(parts)
    ev = {0: [], 1: []}
    for n, part in enumerate(parts):
        for j in range(len(part["blocks"])):
            ev[j % 2].append((n, j))
    count = {nj: (side, c + 1) for side, l in ev.items() for c, nj in enumerate(l)}
    outs = [n for n in range(n_parts) if parts[n]["last"]]
    steps = range(-1, n_parts + 1)

    def has(n):
        return 0 <= n < n_parts

    def has_block(n, j):
        return has(n) and j < len(parts[n]["blocks"])

    with phase(nc, "logit_mm", "masked", "exped", "ready", "t_mm0", "t_mm1", "t_out0", "t_out1", "pv_mm", "y_out", "own",
               "ranked", "replaced", "inverted", "scaled") as (block, sems):
        @block.tensor
        def _(pe):
            def logits(n, i):
                if not has(n):
                    return
                part = parts[n]
                if n:
                    pe.wait_ge(sems["masked"], 4 * (n - 1) + i + 1)
                width = part["keys"](i)
                extra = part["extra"]
                mm = pe.matmul(banks[i][:, 0:width], part["q"][:, i * P:(i + 1) * P], part["k"][:, 0:width],
                               start=True, stop=extra is None)
                if extra is not None:
                    mm = extra(pe, banks[i], i)
                mm.then_inc(sems["logit_mm"], 1)

            def transposes(n, j):
                if not has_block(n, j):
                    return
                rows, first = parts[n]["blocks"][j]
                if j == 0:
                    pe.wait_ge(sems["ready"], n + 1)
                    pe.wait_ge(sems["scaled"], n + 1)
                side, c = count[n, j]
                if c > 1:
                    pe.wait_ge(sems[f"t_out{side}"], c - 1)
                for i in range(first, 4):
                    mm = pe.transpose(banks[4 + side][0:rows, i * P:(i + 1) * P], probs[n % 3][:, i, j * P:j * P + rows], ident)
                mm.then_inc(sems[f"t_mm{side}"], 1)

            def values(n):
                if not has(n):
                    return
                part = parts[n]
                done = sum(m < n for m in outs)
                if part["first"] and done >= 2:
                    pe.wait_ge(sems["y_out"], done - 1)
                lo = part["lo"]
                out = banks[6 + done % 2][lo:lo + 64, :]
                last = len(part["blocks"]) - 1
                for j, (rows, first) in enumerate(part["blocks"]):
                    side, c = count[n, j]
                    pe.wait_ge(sems[f"t_out{side}"], c)
                    mm = pe.matmul(out[:, first * P:], part["values"](j), turned[0:rows, n % 2, j, first * P:],
                                   start=(part["first"] and j == 0), stop=(part["last"] and j == last))
                mm.then_inc(sems["pv_mm"], 1)

            for n in steps:
                transposes(n - 1, 0)
                transposes(n - 1, 1)
                logits(n + 1, 0)
                logits(n + 1, 1)
                transposes(n - 1, 2)
                transposes(n - 1, 3)
                logits(n + 1, 2)
                logits(n + 1, 3)
                values(n - 1)

        @block.scalar
        def _(act):
            def exps(n, i):
                if has(n):
                    act.wait_ge(sems["masked"], 4 * n + i + 1)
                    l = probs[n % 3][:, i, 0:parts[n]["keys"](i)]
                    act.activation(l, l, ACT.Exp, scale=SCALE, bias=stats[:, n % 2, 4 + i:5 + i],
                                   accum_out=stats[:, n % 2, 8 + i:9 + i]).then_inc(sems["exped"], 1)

            def evacuate(n, j):
                if has_block(n, j):
                    rows, first = parts[n]["blocks"][j]
                    act.wait_ge(sems["t_mm0"], count[n, j][1])
                    act.copy(turned[0:rows, n % 2, j, first * P:], banks[4][0:rows, first * P:]).then_inc(sems["t_out0"], 1)

            def scale_last(n):
                if has(n):
                    act.wait_ge(sems["inverted"], n + 1)
                    l = probs[n % 3][:, 3, 0:parts[n]["keys"](3)]
                    act.mul(l, l, stats[:, n % 2, 11:12]).then_inc(sems["scaled"], 1)

            for n in steps:
                evacuate(n - 1, 0)
                exps(n + 1, 0)
                exps(n + 1, 1)
                scale_last(n)
                evacuate(n - 1, 2)
                exps(n + 1, 2)
                exps(n + 1, 3)

        @block.vector
        def _(dve):
            own = Own(dve, sems["own"])

            def mask(n, i):
                if not has(n):
                    return
                part = parts[n]
                if n >= 3 and i == 0:
                    dve.wait_ge(sems["pv_mm"], n - 2)
                dve.wait_ge(sems["logit_mm"], 4 * n + i + 1)
                width = part["keys"](i)
                own(dve.tensor_tensor_reduce(out=probs[n % 3][:, i, 0:width], in0=banks[i][:, 0:width],
                                             in1=part["mask"](i), scale=1.0, scalar=NEG * 1e-5, op0=ALU.add, op1=ALU.max,
                                             accum_out=stats[:, n % 2, i:i + 1]))
                own.settle()
                dve.tensor_scalar(stats[:, n % 2, 4 + i:5 + i], stats[:, n % 2, i:i + 1], -SCALE, None, ALU.mult)\
                    .then_inc(sems["masked"], 1)

            def normalise(n):
                if not has(n):
                    return
                part = parts[n]
                dve.wait_ge(sems["exped"], 4 * n + 4)
                s = stats[:, n % 2, 8:12]
                own(dve.tensor_scalar(s, s, 1e-30, None, ALU.max))
                own.settle()
                own(dve.reciprocal(s, s))
                own.settle()
                if part["row"] is not None:
                    own(dve.tensor_tensor(s, s, part["row"], ALU.mult))
                own.tell(sems["inverted"])
                for i in range(3):
                    l = probs[n % 3][:, i, 0:part["keys"](i)]
                    own(dve.tensor_scalar(l, l, stats[:, n % 2, 8 + i:9 + i], None, ALU.mult))
                own.tell(sems["ready"])

            def evacuate(n, j):
                if has_block(n, j):
                    rows, first = parts[n]["blocks"][j]
                    dve.wait_ge(sems["t_mm1"], count[n, j][1])
                    dve.tensor_copy(turned[0:rows, n % 2, j, first * P:], banks[5][0:rows, first * P:]).then_inc(sems["t_out1"], 1)

            def output(n):
                if has(n) and parts[n]["last"]:
                    part = parts[n]
                    dve.wait_ge(sems["pv_mm"], n + 1)
                    lo, done = part["lo"], sum(m < n for m in outs)
                    dve.tensor_tensor(part["out"], banks[6 + done % 2][lo:lo + 64, :], part["z"], ALU.mult).then_inc(sems["y_out"], 1)

            rounds = SELECTED // 8

            def rank(r):
                if 0 <= r < rounds:
                    if r:
                        dve.wait_ge(sems["replaced"], 3 * r)
                    for i in range(1, 4):
                        dve.max(b["top"][:, i, :], score(i)).then_inc(sems["ranked"], 1)

            def replace(r):
                if 0 <= r < rounds:
                    for i in range(1, 4):
                        dve.wait_ge(sems["ranked"], 3 * r + i)
                        s = score(i)
                        dve.match_replace(s, b["top"][:, i, :], s, TAKEN).then_inc(sems["replaced"], 1)
                if r == rounds - 1:
                    dve.wait_ge(sems["replaced"], 3 * rounds)
                    for i in range(1, 4):
                        s = score(i)
                        own(dve.tensor_scalar(s, s, TAKEN / 2, NEG, ALU.is_gt, ALU.mult))
                    own.settle()

            for n in steps:
                evacuate(n - 1, 1)
                mask(n + 1, 0)
                mask(n + 1, 1)
                rank(n)
                normalise(n)
                evacuate(n - 1, 3)
                mask(n + 1, 2)
                mask(n + 1, 3)
                output(n - 2)
                replace(n)
            output(n_parts - 1)
            dve.wait_ge(sems["y_out"], len(outs))


def stick_breaking(nc, core, b, p):
    con, banks = b["con"], core.banks
    tl = TILES2
    width = [T - j * P for j in range(4)]
    at = [sum(width[:j]) for j in range(5)]
    zs, soft = b["z"], b["soft"]
    suffix, strict01, strict_neg = (con[:, CONST2[n]:CONST2[n] + P] for n in ("suffix", "strict01", "strict_neg"))

    def span(buf, h, j):
        return buf[:, h % 2, at[j]:at[j + 1]]

    cum = [(4, 0), (5, 0), (6, 0), (6, 256)]
    rel, score = b["rel"], b["score"]
    qi, ki = p[:, tl["idx_q"], :], p[:, tl["idx_k"], :]

    def causal(i):
        start = CONST2["causal"] + 384 - i * P
        return con[:, start:start + (i + 1) * P]

    with phase(nc, "rel_mm", "rel_out", "weighted", "z_mm", "z_out", "logged", "soft", "cum_mm", "less", "weights", "pv_mm", "y_out", "own", "own_act") as (block, sems):
        @block.tensor
        def _(pe):
            def index_products(i):
                for h in range(4):
                    pe.wait_ge(sems["z_out"], 4 * (i - 1) + h + 1)
                    pe.matmul(banks[h][:, 0:(i + 1) * P], qi[32 * h:32 * h + 32, i * P:(i + 1) * P],
                              ki[32 * h:32 * h + 32, 0:(i + 1) * P], start=True, stop=True).then_inc(sems["rel_mm"], 1)

            def logits(h):
                m, lo = h // 2, 64 * (h % 2)
                q, k = p[lo:lo + 64, tl["sb_q"] + m, :], p[lo:lo + 64, tl["sb_k"] + m, :]
                for j in range(4):
                    if h:
                        pe.wait_ge(sems["rel_out"], 4 * (h - 1) + j + 1)
                    pe.matmul(banks[j][:, 0:width[j]], k[:, j * P:(j + 1) * P], q[:, j * P:], start=True, stop=True)\
                        .then_inc(sems["z_mm"], 1)

            logits(0)
            for h in range(4):
                m, lo = h // 2, 64 * (h % 2)
                if h < 3:
                    index_products(h + 1)
                    logits(h + 1)
                pe.wait_ge(sems["soft"], h + 1)
                if h:
                    pe.wait_ge(sems["less"], h)
                for j in range(4):
                    bank, c = cum[j]
                    mm = pe.matmul(banks[bank][:, c:c + width[j]], suffix, span(soft, h, j), start=True, stop=(j == 3))
                    for later in range(j + 1, 4):
                        off = c + (later - j) * P
                        mm = pe.matmul(banks[bank][:, off:off + width[later]], core.ones[:, :], span(soft, h, later),
                                       start=False, stop=(later == 3))
                mm.then_inc(sems["cum_mm"], 1)
                if h:
                    pe.wait_ge(sems["y_out"], h)
                pe.wait_ge(sems["weights"], h + 1)
                for j in range(4):
                    mm = pe.matmul(banks[7][lo:lo + 64, j * P:], b["tm_v"][:, j, 256 + h * 64:256 + (h + 1) * 64],
                                   span(zs, h, j), start=(j == 0), stop=(j == 3))
                mm.then_inc(sems["pv_mm"], 1)

        @block.scalar
        def _(act):
            own = Own(act, sems["own_act"])

            def whole(buf, h):
                return buf[:, h % 2, 0:at[4]]

            def logarithm(h):
                if h >= 2:
                    act.wait_ge(sems["pv_mm"], h - 1)
                for j in range(4):
                    act.wait_ge(sems["z_mm"], 4 * h + j + 1)
                    own(act.mul(span(zs, h, j), banks[j][:, 0:width[j]], SCALE))
                    own(act.activation(span(soft, h, j), banks[j][:, 0:width[j]], ACT.Abs, scale=SCALE))
                    own.tell(sems["z_out"])
                own(act.activation(whole(soft, h), whole(soft, h), ACT.Exp, scale=-1.0))
                own.settle()
                act.activation(whole(soft, h), whole(soft, h), ACT.Ln, bias=core.ones[:, 0:1]).then_inc(sems["logged"], 1)

            def relu(i):
                for h in range(4):
                    n = 4 * (i - 1) + h
                    act.wait_ge(sems["rel_mm"], n + 1)
                    if i > 1:
                        act.wait_ge(sems["weighted"], n - 3)
                    act.activation(rel[:, h, 0:(i + 1) * P], banks[h][:, 0:(i + 1) * P], ACT.Relu).then_inc(sems["rel_out"], 1)

            logarithm(0)
            for h in range(4):
                if h < 3:
                    relu(h + 1)
                    logarithm(h + 1)
                act.wait_ge(sems["less"], h + 1)
                act.activation(whole(zs, h), whole(zs, h), ACT.Exp).then_inc(sems["weights"], 1)

        @block.vector
        def _(dve):
            own = Own(dve, sems["own"])

            def softplus(h):
                dve.wait_ge(sems["logged"], h + 1)
                a = slice(0, at[4])
                own(dve.scalar_tensor_tensor(out=soft[:, h % 2, a], in0=zs[:, h % 2, a], scalar=0.0, in1=soft[:, h % 2, a],
                                             op0=ALU.max, op1=ALU.add))
                own.settle()
                for j in range(4):
                    d = span(soft, h, j)[:, 0:P]
                    own(dve.tensor_tensor(d, d, strict01, ALU.mult))
                own.tell(sems["soft"])
                for j in range(4):
                    d = span(zs, h, j)[:, 0:P]
                    own(dve.tensor_tensor(d, d, strict_neg, ALU.add))
                own.settle()

            def weigh(i):
                for h in range(4):
                    n = 4 * (i - 1) + h
                    dve.wait_ge(sems["rel_out"], n + 1)
                    wi = b["tm_s"][:, i, IDX_W + h:IDX_W + h + 1]
                    r = rel[:, h, 0:(i + 1) * P]
                    if h == 0:
                        dve.tensor_scalar(score(i), r, wi, None, ALU.mult).then_inc(sems["weighted"], 1)
                    else:
                        dve.wait_ge(sems["weighted"], n)
                        dve.scalar_tensor_tensor(out=score(i), in0=r, scalar=wi, in1=score(i), op0=ALU.mult, op1=ALU.add)\
                            .then_inc(sems["weighted"], 1)
                dve.wait_ge(sems["weighted"], 4 * i)
                own(dve.scalar_tensor_tensor(out=score(i), in0=score(i), scalar=IDX_SCALE, in1=causal(i), op0=ALU.mult, op1=ALU.add))

            own(dve.tensor_copy(score(0), causal(0)))
            softplus(0)
            for h in range(4):
                if h < 3:
                    weigh(h + 1)
                dve.wait_ge(sems["cum_mm"], h + 1)
                for j in range(4):
                    bank, c = cum[j]
                    own(dve.scalar_tensor_tensor(out=span(zs, h, j), in0=banks[bank][:, c:c + width[j]], scalar=-1.0,
                                                 in1=span(zs, h, j), op0=ALU.mult, op1=ALU.add))
                own.tell(sems["less"])
                if h < 3:
                    softplus(h + 1)
                dve.wait_ge(sems["pv_mm"], h + 1)
                m, lo = h // 2, 64 * (h % 2)
                dve.tensor_tensor(p[lo:lo + 64, tl["sb_q"] + m, :], banks[7][lo:lo + 64, :], p[lo:lo + 64, tl["sb_z"] + m, :],
                                  ALU.mult).then_inc(sems["y_out"], 1)
            dve.wait_ge(sems["y_out"], 4)


class TwoBuffers:

    def __init__(self, queries, others):
        self.queries, self.others = queries, others

    def __getitem__(self, at):
        rows, tiles, tokens = at
        if isinstance(tiles, slice):
            if tiles.start < Q_TILES:
                return self.queries[rows, tiles, tokens]
            return self.others[rows, tiles.start - Q_TILES:tiles.stop - Q_TILES, tokens]
        return self.queries[rows, tiles, tokens] if tiles < Q_TILES else self.others[rows, tiles - Q_TILES, tokens]


def block2_layer(nc, core, layer, w, con, tables):
    with ExitStack() as outer:
        def buf(stack, name, shape, dt=F32, rows=P):
            return stack.enter_context(nc.sbuf_tensor(name, [rows] + shape, dt))

        tl = TILES2
        queries = buf(outer, "queries", [Q_TILES, T])
        core.hh, core.hl = buf(outer, "h_high3", [KD, T], F32R), buf(outer, "h_low3", [KD, T], F32R)
        inner = outer.enter_context(ExitStack())
        others = buf(inner, "others", [IN2_TILES - Q_TILES, T])
        p = TwoBuffers(queries, others)
        with split_weights(nc, core), nc.sbuf_tensor("norm_tmp3", [P, 4, T], F32) as tmp:
            project_h(nc, core, lambda n: w["in2"][layer * IN2_TILES + n], IN2_TILES,
                      ((Q_TILES, lambda n: queries[:, n, :]), (IN2_TILES, lambda n: others[:, n - Q_TILES, :])),
                      core.par[:, PAR2["norm"]:PAR2["norm"] + 8], tmp,
                      ((core.par[:, 0:NPAR2], w["par2"][layer]), (core.small[:, 0:NSMALL2], w["small2"][layer])))
        with ExitStack() as stack:
            b = {"con": con, "tables": tables, "w1_dram": w["w1_2"][layer],
                 "wm_dram": w["wm2"][layer], "mem_dram": w["mem"]}
            b["tm_v"] = p[:, tl["fox_v"]:tl["fox_v"] + 4, :]
            b["tm_kv"], b["tm_s"] = (wide(p[:, tl[n], :], 4) for n in ("vs_vw", "scalars"))
            b["mem_k"], b["mem_v"] = buf(stack, "mem_k", [2, N_MEM]), buf(stack, "mem_v", [2, 256])
            b["dsa_k"], b["dsa_v"] = buf(stack, "dsa_k", [2, T]), buf(stack, "dsa_v", [4, 256])
            b["cmp_k"], b["cmp_v"] = buf(stack, "cmp_k", [N_CMP]), buf(stack, "cmp_v", [64], rows=N_CMP)
            b["f_abs"], b["f_log"], b["cum"] = buf(stack, "f_abs", [4, 4]), buf(stack, "f_log", [4, 4]), buf(stack, "cum", [2, T], rows=4)
            b["stats"] = buf(stack, "stats", [2, 12])
            with ExitStack() as scratch:
                b["turn"], b["mem"], b["hidden"] = buf(scratch, "turn", [2, T]), buf(scratch, "mem_x", [KD, N_MEM]), buf(scratch, "hidden", [2, 32])
                b["hidden_t"] = buf(scratch, "hidden_t", [2, P])
                prepare2(nc, core, b, p)
            with ExitStack() as scratch:
                b["z"] = core.ring[:, 0:2560].rearrange("p (h n) -> p h n", h=2)
                b["soft"] = core.ring[:, 2560:5120].rearrange("p (h n) -> p h n", h=2)

                def score(i):
                    start = 5120 + i * (i + 1) // 2 * P
                    return core.ring[:, start:start + (i + 1) * P]

                b["score"] = score
                with nc.sbuf_tensor("rel", [P, 4, T], F32) as b["rel"]:
                    stick_breaking(nc, core, b, p)
                b["top"] = buf(scratch, "top", [4, 8])
                b["probs"] = [buf(scratch, f"probs{n}", [4, T]) for n in range(2)] + [p[:, tl["sb_k"]:tl["sb_k"] + 4, :]]
                b["probsT"] = core.ring[:, 0:8 * T].rearrange("p (a j t) -> p a j t", a=2, j=4)

                def causal(i):
                    at = CONST2["causal"] + 384 - i * P
                    return con[:, at:at + (i + 1) * P]

                triangle = [(P, j) for j in range(4)]

                def grow(i):
                    return (i + 1) * P

                def part(name, h, k, values, mask, keys=grow, blocks=triangle, extra=None, row=None, first=True, last=True):
                    m, lo = h // 2, 64 * (h % 2)
                    return {"q": p[lo:lo + 64, tl[name + "_q"] + m, :], "k": k[lo:lo + 64], "values": values, "mask": mask,
                            "keys": keys, "blocks": blocks, "extra": extra, "row": row, "first": first, "last": last,
                            "lo": lo, "out": p[lo:lo + 64, tl[name + "_q"] + m, :], "z": p[lo:lo + 64, tl[name + "_z"] + m, :]}

                def forget(h):
                    sel = con[0:4, CONST2["sel"] + h * P:CONST2["sel"] + (h + 1) * P]

                    def extra(pe, bank, i):
                        width = (i + 1) * P
                        pe.matmul(wide(bank[:, 0:width], i + 1), b["cum"][0:4, 0, i * P:(i + 1) * P],
                                  sel.rearrange("p (o t) -> p o t", o=1).to_broadcast([4, i + 1, P]), start=False, stop=False)
                        return pe.matmul(bank[:, 0:width], sel, b["cum"][0:4, 1, 0:width], start=False, stop=True)
                    return extra

                parts = []
                for h in range(NH):
                    m = h // 2
                    parts.append(part("fox", h, p[:, tl["fox_k"] + m, :], lambda j, h=h: b["tm_v"][:, j, h * 64:(h + 1) * 64],
                                      causal, extra=forget(h)))
                for h in range(NH):
                    def gate(n, h=h):
                        return b["tm_s"][:, :, NSA_G + 4 * n + h]

                    parts.append(part("nsa", h, b["cmp_k"], lambda j: b["cmp_v"][:, :],
                                      lambda i: con[:, CONST2["cmp"] + i * 32:CONST2["cmp"] + i * 32 + N_CMP],
                                      keys=lambda i: N_CMP, blocks=[(N_CMP, 0)], row=gate(0), last=False))
                    parts.append(part("nsa", h, p[:, tl["ks"], :], lambda j: b["tm_kv"][:, j, 0:64], causal, row=gate(1),
                                      first=False, last=False))
                    parts.append(part("nsa", h, p[:, tl["kw"], :], lambda j: b["tm_kv"][:, j, 64:128], causal, row=gate(2),
                                      first=False))
                for h in range(NH):
                    m = h // 2
                    parts.append(part("mem", h, b["mem_k"][:, m, :], lambda j, h=h: b["mem_v"][:, j, h * 64:(h + 1) * 64],
                                      lambda i: core.zeros[:, 0:N_MEM], keys=lambda i: N_MEM, blocks=[(P, 0), (P, 0)]))
                for h in range(NH):
                    m = h // 2
                    parts.append(part("dsa", h, b["dsa_k"][:, m, :], lambda j, h=h: b["dsa_v"][:, j, h * 64:(h + 1) * 64],
                                      b["score"]))
                attention(nc, core, b, parts)
        inner.close()
        merged, gate, part = queries[:, 0:KD, :], queries[:, KD:KD + 2, :], queries[:, KD + 2:KD + 4, :]
        with split_weights(nc, core, KD + 2), nc.sbuf_tensor("y_high2", [P, 10, T], F32R) as y_high, \
                nc.sbuf_tensor("y_low2", [P, 10, T], F32R) as y_low:
            ys, highs, lows = ([a[:, 2 * n:2 * n + 2, :] for n in range(N_BR2)] for a in (queries, y_high, y_low))
            merge(nc, core, layer, w["merge2"], ys, highs, lows, 2, merged, gate, part)
        with split_weights(nc, core), nc.sbuf_tensor("merged_high2", [P, KD, T], F32R) as high, \
                nc.sbuf_tensor("merged_low2", [P, KD, T], F32R) as low:
            add_projection(nc, core, layer, w["out2"], merged, high, low, KD, 1)


def layout2(i):
    w = i["w_in_2"]
    at, c = 0, {}
    for name, n in (("dsa_q", 256), ("ckv", 128), ("idx_q", 128), ("idx_k", 32), ("idx_w", 4), ("dsa_z", 256), ("fox_q", 256),
                    ("fox_k", 256), ("fox_v", 256), ("fox_f", 4), ("fox_z", 256), ("sb_q", 256), ("sb_k", 256), ("sb_v", 256),
                    ("sb_z", 256), ("nsa_q", 256), ("kc", 64), ("vc", 64), ("ks", 64), ("vs", 64), ("kw", 64), ("vw", 64),
                    ("nsa_g", 12), ("nsa_z", 256), ("mem_q", 256), ("mem_z", 256), ("merge", N_BR2 * D)):
        c[name] = w[:, :, at:at + n]
        at += n
    assert at == w.shape[2]
    tiles = [c["dsa_q"], c["fox_q"], c["sb_q"], c["nsa_q"], c["mem_q"], c["ckv"], c["idx_q"]] + [c["idx_k"]] * 4
    tiles += [c["dsa_z"], c["fox_k"], c["fox_z"], c["sb_k"], c["sb_z"], c["kc"], c["vc"], c["ks"], c["ks"], c["kw"], c["kw"],
              c["nsa_z"], c["mem_z"], c["fox_v"], c["sb_v"], c["vs"], c["vw"]]
    scalars = np.concatenate([c["idx_w"], c["nsa_g"], c["fox_f"]], 2)
    tiles += [scalars] * 6 + [scalars[:, :, 0:P - 6 * N_SCALARS]]
    a = {"in2": by_tiles(np.concatenate(tiles, 2), KD).reshape(-1, P, KD * P)}

    def rows(v, k):
        return v.reshape(DEPTH, k, P, -1).transpose(0, 2, 1, 3).reshape(DEPTH, P, -1)

    wm = i["w_mem_kv_2"]
    a["wm2"] = np.concatenate([by_tiles(wm[:, :, 0:256], KD).reshape(DEPTH, 2, P, KD * P).transpose(0, 2, 1, 3)
                               .reshape(DEPTH, P, -1), rows(wm[:, :, 256:], KD)], 2)
    gates = by_tiles(c["merge"], KD).reshape(DEPTH, N_BR2, KD, P, KD, P)
    branch = np.stack([by_tiles(i["w_branch_2"][:, n], 2) for n in range(N_BR2)], 1)
    a["merge2"] = np.concatenate([gates, branch], 4).transpose(0, 2, 1, 3, 4, 5).reshape(-1, P, 10 * P)
    a["out2"] = by_tiles(i["w_out_2"], KD).reshape(-1, P, KD * P)
    a["par2"] = np.concatenate([vectors(i["norm_g_2"]), vectors(i["kv_norm_2"]),
                                np.broadcast_to(i["fox_bias_2"][:, None, :], (DEPTH, P, 4)), vectors(i["mem_norm_2"])], 2)
    pe = np.concatenate([i["nsa_pe_k_2"], i["nsa_pe_v_2"]], 2).transpose(0, 2, 1)
    a["small2"] = np.concatenate([i["w_uk_2"], i["w_uv_2"], pe, i["nsa_wc2_k_2"], i["nsa_wc2_k_2"], i["nsa_wc2_v_2"]], 2)
    w1 = [i[n].reshape(DEPTH, CMP_LEN, 64, P).transpose(0, 2, 1, 3) for n in ("nsa_wc1_k_2", "nsa_wc1_v_2")]
    a["w1_2"] = np.concatenate(w1, 1).reshape(DEPTH, P, CMP_LEN * P)
    a["mem"] = i["mem_2"][0].T.reshape(KD, P, N_MEM).transpose(1, 0, 2)
    return a


def program(nc, w, positions, out, blocks=(1, 2)):
    core = Core()
    with ExitStack() as stack:
        def buf(ctx, name, shape):
            return ctx.enter_context(nc.sbuf_tensor(name, [P] + shape, F32))

        core.x, core.ring = buf(stack, "x", [KD, T]), buf(stack, "ring", [RING_COLUMNS])
        core.count = 0
        core.root, core.ones, core.eps, core.tiny = (buf(stack, "root", [T]), buf(stack, "ones", [P]), buf(stack, "eps", [2]),
                                                     buf(stack, "tiny", [64]))
        core.banks = [stack.enter_context(nc.psum_tensor(f"bank{n}", [P, T], F32)) for n in range(8)]
        gains = buf(stack, "gains", [2 * KD])
        with ExitStack() as ctx:
            core.par = buf(ctx, "par1_sb", [NPAR1])
            with phase(nc, "loaded") as (block, sems):
                @block.sync
                def _(sp):
                    for dst, src in ((core.x[:, :, :], w["x"]), (gains[:, :], w["gains"])):
                        sp.dma_start(dst, src).then_inc(sems["loaded"], 16)
                    sp.wait_ge(sems["loaded"], 32)

                @block.vector
                def _(dve):
                    dve.memset(core.ones[:, :], 1.0)
                    dve.memset(core.eps[:, 0:1], EPS)
                    dve.memset(core.eps[:, 1:2], GN_EPS)

            with nc.sbuf_tensor("squares0", [P, 3, T], F32) as core.squares, phase(nc, *ROOT) as (block, sems):
                @block.vector
                def _(dve):
                    for d in range(1, KD - 1):
                        sum_tile(dve, sems, core, d)
                    invert_root(dve, sems, core)

                root_of_x(block, sems, core)

            if 1 in blocks:
                with nc.Fori(0, DEPTH) as layer:
                    block1_layer(nc, core, layer, w)
                final_norm(nc, core, gains[:, 0:KD], True)
        if 2 in blocks:
            with ExitStack() as ctx:
                con, tables, core.zeros = buf(ctx, "con2_sb", [NCONST2]), buf(ctx, "rope", [4, T]), buf(ctx, "zeros", [N_MEM])
                core.par, core.small = buf(ctx, "par2_sb", [NPAR2]), buf(ctx, "small2_sb", [NSMALL2])
                core.ident2 = con[:, CONST2["ident"]:CONST2["ident"] + P]
                with phase(nc, "loaded") as (block, sems):
                    @block.sync
                    def _(sp):
                        sp.dma_start(con[:, :], w["con2"]).then_inc(sems["loaded"], 16)
                        sp.wait_ge(sems["loaded"], 16)

                    @block.vector
                    def _(dve):
                        dve.memset(core.zeros[:, :], 0.0)

                rope_tables(nc, core, con, tables, positions)
                with nc.Fori(0, DEPTH) as layer:
                    block2_layer(nc, core, layer, w, con, tables)
                final_norm(nc, core, gains[:, KD:2 * KD], False)
        with phase(nc, "stored") as (block, sems):
            @block.sync
            def _(sp):
                sp.dma_start(out, core.x[:, :, :]).then_inc(sems["stored"], 16)
                sp.wait_ge(sems["stored"], 16)


def kernel(**inputs):
    import concourse.bacc as _bacc
    from concourse import mybir as _mybir
    from concourse.bass_utils import run_bass_kernel_spmd as _run

    i = {name: np.asarray(a) for name, a in inputs.items()}
    arrays = {**layout1(i), **layout2(i), "con1": constants1(), "con2": constants2()}
    arrays["x"] = i["x"][0].T.reshape(KD, P, T).transpose(1, 0, 2)
    arrays["gains"] = np.concatenate([i["final_g"].reshape(KD, P).T, i["final_norm_2"].reshape(KD, P).T], 1)
    arrays["positions"] = i["positions_2"].reshape(1, T)
    arrays = {name: np.ascontiguousarray(a) for name, a in arrays.items()}
    nc = _bacc.Bacc("TRN2", target_bir_lowering=False, num_devices=1)
    w = {name: nc.dram_tensor(f"in_{name}", a.shape, _mybir.dt.from_np(a.dtype), kind="ExternalInput").ap()
         for name, a in arrays.items()}
    out = nc.dram_tensor("out", (P, KD, T), F32, kind="ExternalOutput").ap()
    program(nc, w, w["positions"], out)
    r = _run(nc, [{f"in_{name}": a for name, a in arrays.items()}], core_ids=[0])
    return r.results[0]["out"].transpose(1, 0, 2).reshape(1, D, T).transpose(0, 2, 1)
```
